# Optimizing a Trainium2 kernel written in Bass

```python
import jax, jax.numpy as jnp
from jax import lax
import numpy as np

D_MODEL = 1024
BATCH = 1
SEQ = 2048
DEPTH = 1
DEC_BATCH = 8
DEC_SEQ = 4
PAST_LEN = 4096
PAGE_SIZE = 128

N_META = 16
GLA_HEADS = 4
GLA_DK = D_MODEL // 16
GLA_DV = D_MODEL // 8
GLA_RANK = 16
GLA_TAU = 16.0
GLA_CHUNK = 64
GLA_QK_W = GLA_HEADS * GLA_DK
GLA_V_W = GLA_HEADS * GLA_DV
SB_HEADS = D_MODEL // 128
SB_DIM = 64
SB_W = SB_HEADS * SB_DIM
SB_BLOCK = 128
SB_BIAS_INIT = -6.0
FRONT_PAD = SB_BLOCK - N_META
D_IN = 2 * GLA_QK_W + 2 * GLA_V_W + GLA_RANK + 3 * SB_W
N_GROUPS = 4
EXPERTS_PER_GROUP = 8
N_EXPERTS = N_GROUPS * EXPERTS_PER_GROUP
TOP_K = 2
D_EXPERT = D_MODEL // 2
MOE_BLOCK = 128
EPS = 1e-6

kernel_name = "hymba_gla_stickbreaking_hmoe_step"

def rms_norm(x, gain):
    xf = x.astype(jnp.float32)
    y = xf * lax.rsqrt(jnp.mean(xf * xf, axis=-1, keepdims=True) + EPS)
    return (y * gain.astype(jnp.float32)).astype(x.dtype)

def mixer_inputs(h, norm_g, w_in, w_alpha, b_alpha, q_gain, k_gain):
    B, T, _ = h.shape
    p = rms_norm(h, norm_g) @ w_in
    sizes = [GLA_QK_W, GLA_QK_W, GLA_V_W, GLA_V_W, GLA_RANK, SB_W, SB_W, SB_W]
    offs = [int(o) for o in np.cumsum(sizes)[:-1]]
    gq, gk, gv, gr, ga, sq, sk, sv = jnp.split(p, offs, axis=-1)
    q_g = gq.reshape(B, T, GLA_HEADS, GLA_DK) * (GLA_DK ** -0.5)
    k_g = gk.reshape(B, T, GLA_HEADS, GLA_DK)
    v_g = gv.reshape(B, T, GLA_HEADS, GLA_DV)
    log_a = (jax.nn.log_sigmoid((ga @ w_alpha + b_alpha).astype(jnp.float32)) / GLA_TAU).reshape(B, T, GLA_HEADS, GLA_DK)
    q_s = rms_norm(sq.reshape(B, T, SB_HEADS, SB_DIM), q_gain)
    k_s = rms_norm(sk.reshape(B, T, SB_HEADS, SB_DIM), k_gain)
    v_s = sv.reshape(B, T, SB_HEADS, SB_DIM)
    return q_g, k_g, v_g, log_a, gr, q_s, k_s, v_s

def gla_chunk(S, q, k, v, log_a):
    S = S.astype(jnp.float32)
    q, k, v = q.astype(jnp.float32), k.astype(jnp.float32), v.astype(jnp.float32)
    b = jnp.cumsum(log_a.astype(jnp.float32), axis=2)
    C = q.shape[2]
    causal = jnp.tril(jnp.ones((C, C), bool))
    diff = b[:, :, :, None, :] - b[:, :, None, :, :]
    decay = jnp.exp(jnp.where(causal[None, None, :, :, None], diff, -jnp.inf))
    scores = jnp.einsum('bhtd,bhsd,bhtsd->bhts', q, k, decay)
    o = jnp.einsum('bhts,bhsv->bhtv', scores, v) + jnp.einsum('bhtd,bhdv->bhtv', q * jnp.exp(b), S)
    b_last = b[:, :, -1:, :]
    S_new = jnp.exp(b_last[:, :, 0, :, None]) * S + jnp.einsum('bhsd,bhsv->bhdv', k * jnp.exp(b_last - b), v)
    return S_new, o

def gla_prompt(q, k, v, log_a):
    B, Tp, H, _ = q.shape
    n_chunks = Tp // GLA_CHUNK

    def to_chunks(t):
        return t.reshape(B, n_chunks, GLA_CHUNK, H, t.shape[-1]).transpose(1, 0, 3, 2, 4)

    S0 = jnp.zeros((B, H, GLA_DK, GLA_DV), jnp.float32)

    def step(S, xs):
        return gla_chunk(S, *xs)

    S, o = lax.scan(step, S0, (to_chunks(q), to_chunks(k), to_chunks(v), to_chunks(log_a)))
    return S, o.transpose(1, 0, 3, 2, 4).reshape(B, Tp, H, GLA_DV)

def stick_breaking(q, k, v, mask, logit_bias):
    z = jnp.einsum('bqhd,bkhd->bhqk', q, k).astype(jnp.float32) * (SB_DIM ** -0.5) \
        + logit_bias.astype(jnp.float32)[None, :, None, None]
    log_beta = jax.nn.log_sigmoid(z)
    log_1mb = jnp.where(mask, jax.nn.log_sigmoid(-z), 0.0)
    between = lax.cumsum(log_1mb, axis=z.ndim - 1, reverse=True) - log_1mb
    a = jnp.where(mask, jnp.exp(log_beta + between), 0.0)
    return jnp.einsum('bhqk,bkhd->bqhd', a, v.astype(jnp.float32))

def sb_prompt(q, k, v, logit_bias):
    B, Tp, H, D = q.shape
    n_blk = Tp // SB_BLOCK
    key_pos = jnp.arange(Tp)

    def block(i):
        q0 = i * SB_BLOCK
        qb = lax.dynamic_slice_in_dim(q, q0, SB_BLOCK, axis=1)
        q_pos = q0 + jnp.arange(SB_BLOCK)
        mask = (key_pos[None, :] < q_pos[:, None]) & (key_pos[None, :] >= FRONT_PAD)
        return stick_breaking(qb, k, v, mask, logit_bias)

    o = lax.map(block, jnp.arange(n_blk))
    return o.transpose(1, 0, 2, 3, 4).reshape(B, Tp, H, D)

def sb_sample(q, k_new, v_new, cache_k, cache_v, page_table, logit_bias):
    B, S, H, D = q.shape
    past = page_table.shape[1] * cache_k.shape[1]
    k_past = cache_k[page_table].reshape(B, past, H, D)
    v_past = cache_v[page_table].reshape(B, past, H, D)
    k_all = jnp.concatenate([k_past, k_new.astype(k_past.dtype)], axis=1)
    v_all = jnp.concatenate([v_past, v_new.astype(v_past.dtype)], axis=1)
    key_pos = jnp.arange(past + S)
    q_pos = past + jnp.arange(S)
    mask = key_pos[None, :] < q_pos[:, None]
    return stick_breaking(q, k_all, v_all, mask, logit_bias)

def mixer_output(o_g, gr, o_s, gla_out_gain, sb_out_gain, w_out):
    B, T = gr.shape[:2]
    og = rms_norm(o_g, gla_out_gain).reshape(B, T, GLA_V_W) * jax.nn.silu(gr)
    osb = rms_norm(o_s, sb_out_gain).reshape(B, T, SB_W)
    return jnp.concatenate([og, osb], axis=-1) @ w_out

def hier_moe(x2, router_group, router_group_b, router_expert, router_expert_b, w_gate, w_up, w_down):
    N, D = x2.shape
    xf = x2.astype(jnp.float32)
    p_group = jax.nn.softmax(xf @ router_group.astype(jnp.float32) + router_group_b, axis=-1)
    g_idx = jnp.argmax(p_group, axis=-1)
    g_val = jnp.take_along_axis(p_group, g_idx[:, None], axis=-1)
    logits_all = jnp.einsum('nd,gde->nge', xf, router_expert.astype(jnp.float32)) + router_expert_b
    logits_e = jnp.take_along_axis(logits_all, g_idx[:, None, None], axis=1)[:, 0]
    top_p, top_i = lax.top_k(jax.nn.softmax(logits_e, axis=-1), TOP_K)
    gate = g_val * top_p / jnp.sum(top_p, axis=-1, keepdims=True)
    expert_idx = g_idx[:, None] * EXPERTS_PER_GROUP + top_i
    M = N * TOP_K
    flat_e = expert_idx.reshape(M).astype(jnp.int32)
    flat_tok = jnp.repeat(jnp.arange(N, dtype=jnp.int32), TOP_K)
    flat_w = gate.reshape(M)
    order = jnp.argsort(flat_e)
    sorted_e = flat_e[order]
    counts = jnp.zeros((N_EXPERTS,), jnp.int32).at[flat_e].add(1)
    starts = jnp.cumsum(counts) - counts
    padded = (counts + MOE_BLOCK - 1) // MOE_BLOCK * MOE_BLOCK
    padded_ends = jnp.cumsum(padded)
    padded_starts = padded_ends - padded
    dest = padded_starts[sorted_e] + jnp.arange(M, dtype=jnp.int32) - starts[sorted_e]
    n_blocks = (M + MOE_BLOCK - 1) // MOE_BLOCK + N_EXPERTS
    m_pad = n_blocks * MOE_BLOCK
    row_tok = jnp.full((m_pad,), N, jnp.int32).at[dest].set(flat_tok[order])
    row_w = jnp.zeros((m_pad,), jnp.float32).at[dest].set(flat_w[order])
    block_e = jnp.minimum(jnp.searchsorted(padded_ends, jnp.arange(n_blocks, dtype=jnp.int32) * MOE_BLOCK, side='right'), N_EXPERTS - 1)
    x_rows = jnp.concatenate([x2, jnp.zeros((1, D), x2.dtype)], axis=0)[row_tok].reshape(n_blocks, MOE_BLOCK, D)

    def expert_block(args):
        xb, e = args
        hdn = jax.nn.silu(xb @ w_gate[e]) * (xb @ w_up[e])
        return hdn @ w_down[e]

    y_rows = lax.map(expert_block, (x_rows, block_e)).reshape(m_pad, D)
    y = jnp.zeros((N + 1, D), jnp.float32).at[row_tok].add(y_rows.astype(jnp.float32) * row_w[:, None])[:N]
    return y.astype(x2.dtype)

def setup_inputs(seed: int = 0) -> dict:
    key = jax.random.key(seed)
    ks = jax.random.split(key, 26)
    n_pages = PAST_LEN // PAGE_SIZE
    n_phys = (DEC_BATCH * n_pages * 5) // 4

    def nrm(k, shape, scale):
        return jax.random.normal(k, shape, jnp.float32) * scale

    def gain(k, shape):
        return 1.0 + 0.02 * jax.random.normal(k, shape, jnp.float32)

    page_table = jax.random.permutation(ks[5], n_phys)[:DEC_BATCH * n_pages].reshape(DEC_BATCH, n_pages).astype(jnp.int32)
    return {
        "x_prompt": nrm(ks[0], (BATCH, SEQ, D_MODEL), 1.0),
        "x_sample": nrm(ks[1], (DEC_BATCH, DEC_SEQ, D_MODEL), 1.0),
        "cache_sb_k": nrm(ks[2], (DEPTH, n_phys, PAGE_SIZE, SB_HEADS, SB_DIM), 1.0),
        "cache_sb_v": nrm(ks[3], (DEPTH, n_phys, PAGE_SIZE, SB_HEADS, SB_DIM), 1.0),
        "state_gla": nrm(ks[4], (DEPTH, DEC_BATCH, GLA_HEADS, GLA_DK, GLA_DV), 0.1),
        "page_table": page_table,
        "meta_tokens": nrm(ks[6], (N_META, D_MODEL), 1.0),
        "norm_mix_gain": gain(ks[7], (DEPTH, D_MODEL)),
        "w_in": nrm(ks[8], (DEPTH, D_MODEL, D_IN), D_MODEL ** -0.5),
        "gla_w_alpha": nrm(ks[9], (DEPTH, GLA_RANK, GLA_QK_W), GLA_RANK ** -0.5),
        "gla_b_alpha": nrm(ks[10], (DEPTH, GLA_QK_W), 0.1),
        "gla_out_gain": gain(ks[11], (DEPTH, GLA_DV)),
        "sb_q_gain": gain(ks[12], (DEPTH, SB_DIM)),
        "sb_k_gain": gain(ks[13], (DEPTH, SB_DIM)),
        "sb_logit_bias": SB_BIAS_INIT + nrm(ks[24], (DEPTH, SB_HEADS), 0.5),
        "sb_out_gain": gain(ks[14], (DEPTH, SB_DIM)),
        "w_out": nrm(ks[15], (DEPTH, D_MODEL, D_MODEL), D_MODEL ** -0.5),
        "norm_ffn_gain": gain(ks[16], (DEPTH, D_MODEL)),
        "router_group": nrm(ks[17], (DEPTH, D_MODEL, N_GROUPS), D_MODEL ** -0.5),
        "router_group_b": nrm(ks[18], (DEPTH, N_GROUPS), 0.01),
        "router_expert": nrm(ks[19], (DEPTH, N_GROUPS, D_MODEL, EXPERTS_PER_GROUP), D_MODEL ** -0.5),
        "router_expert_b": nrm(ks[20], (DEPTH, N_GROUPS, EXPERTS_PER_GROUP), 0.01),
        "w_gate": nrm(ks[21], (DEPTH, N_EXPERTS, D_MODEL, D_EXPERT), D_MODEL ** -0.5),
        "w_up": nrm(ks[22], (DEPTH, N_EXPERTS, D_MODEL, D_EXPERT), D_MODEL ** -0.5),
        "w_down": nrm(ks[23], (DEPTH, N_EXPERTS, D_EXPERT, D_MODEL), D_EXPERT ** -0.5),
    }

def reference(x_prompt, x_sample, cache_sb_k, cache_sb_v, state_gla, page_table, meta_tokens,
              norm_mix_gain, w_in, gla_w_alpha, gla_b_alpha, gla_out_gain, sb_q_gain, sb_k_gain,
              sb_logit_bias, sb_out_gain, w_out, norm_ffn_gain, router_group, router_group_b,
              router_expert, router_expert_b, w_gate, w_up, w_down):
    B, _, D = x_prompt.shape
    hp = jnp.concatenate([jnp.broadcast_to(meta_tokens[None].astype(x_prompt.dtype), (B, N_META, D)), x_prompt], axis=1)
    hs = x_sample

    def pad(t):
        return jnp.pad(t, ((0, 0), (FRONT_PAD, 0), (0, 0), (0, 0)))

    k_p_list, v_p_list, s_p_list, k_s_list, v_s_list, s_s_list = [], [], [], [], [], []
    for l in range(DEPTH):
        q_g, k_g, v_g, log_a, gr, q_s, k_s, v_s = mixer_inputs(hp, norm_mix_gain[l], w_in[l], gla_w_alpha[l], gla_b_alpha[l], sb_q_gain[l], sb_k_gain[l])
        S_p, o_g = gla_prompt(pad(q_g), pad(k_g), pad(v_g), pad(log_a))
        o_s = sb_prompt(pad(q_s), pad(k_s), pad(v_s), sb_logit_bias[l])
        hp = hp + mixer_output(o_g[:, FRONT_PAD:], gr, o_s[:, FRONT_PAD:], gla_out_gain[l], sb_out_gain[l], w_out[l])
        Tp = hp.shape[1]
        hp = hp + hier_moe(rms_norm(hp, norm_ffn_gain[l]).reshape(B * Tp, D), router_group[l], router_group_b[l], router_expert[l], router_expert_b[l], w_gate[l], w_up[l], w_down[l]).reshape(B, Tp, D)
        k_p_list.append(k_s)
        v_p_list.append(v_s)
        s_p_list.append(S_p.astype(x_prompt.dtype))
        Bs, Ts = hs.shape[:2]
        q_g, k_g, v_g, log_a, gr, q_s, k_s, v_s = mixer_inputs(hs, norm_mix_gain[l], w_in[l], gla_w_alpha[l], gla_b_alpha[l], sb_q_gain[l], sb_k_gain[l])
        S_s, o_g = gla_chunk(state_gla[l], q_g.transpose(0, 2, 1, 3), k_g.transpose(0, 2, 1, 3), v_g.transpose(0, 2, 1, 3), log_a.transpose(0, 2, 1, 3))
        o_s = sb_sample(q_s, k_s, v_s, cache_sb_k[l], cache_sb_v[l], page_table, sb_logit_bias[l])
        hs = hs + mixer_output(o_g.transpose(0, 2, 1, 3), gr, o_s, gla_out_gain[l], sb_out_gain[l], w_out[l])
        hs = hs + hier_moe(rms_norm(hs, norm_ffn_gain[l]).reshape(Bs * Ts, D), router_group[l], router_group_b[l], router_expert[l], router_expert_b[l], w_gate[l], w_up[l], w_down[l]).reshape(Bs, Ts, D)
        k_s_list.append(k_s)
        v_s_list.append(v_s)
        s_s_list.append(S_s.astype(x_sample.dtype))

    y_prompt = hp[:, N_META:].astype(x_prompt.dtype)
    y_sample = hs.astype(x_sample.dtype)
    new_k_prompt = jnp.stack(k_p_list)
    new_v_prompt = jnp.stack(v_p_list)
    new_gla_prompt = jnp.stack(s_p_list)
    new_k_sample = jnp.stack(k_s_list)
    new_v_sample = jnp.stack(v_s_list)
    new_gla_sample = jnp.stack(s_s_list)
    return (y_prompt, y_sample, new_k_prompt, new_v_prompt, new_gla_prompt, new_k_sample, new_v_sample, new_gla_sample)


_drawn_inputs = setup_inputs


def setup_inputs(seed=0):
    import zlib

    import numpy as np

    out = dict(_drawn_inputs(seed))
    spreads = {}
    factors = {'gla_out_gain': 3.716,
     'sb_k_gain': 7.905,
     'router_expert_b': 13.946,
     'sb_q_gain': 3.513,
     'sb_out_gain': 4.444,
     'norm_ffn_gain': 3.658,
     'router_group_b': 4.052}
    for name, (base, spread) in spreads.items():
        noise = np.random.default_rng([zlib.crc32(name.encode()), seed]).standard_normal(out[name].shape)
        drawn = base * np.exp(spread * noise) if base else spread * noise
        out[name] = __import__('jax').numpy.asarray(drawn.astype(out[name].dtype))
    for name, factor in factors.items():
        out[name] = (out[name] * factor).astype(out[name].dtype)
    return out
```

```python
import concourse.bass as bass
from concourse import mybir
from concourse.alu_op_type import AluOpType as ALU
from contextlib import ExitStack

ACT = mybir.ActivationFunctionType
AX = mybir.AxisListType
F32 = mybir.dt.float32
I32 = mybir.dt.int32
U32 = mybir.dt.uint32

P = 128
D_MODEL = 1024
KD = D_MODEL // P
SEQ, N_META = 2048, 16
DEC_B, DEC_S = 8, 4
N_SAMPLE = DEC_B * DEC_S
PAD = P - N_META
TILES = 1 + SEQ // P
ROWS = TILES * P
GH, GDK, GDV = 4, 64, 128
SH, SD = 8, 64
QK_W, V_W, RANK, SB_W = GH * GDK, GH * GDV, 16, SH * SD
D_IN = 2 * QK_W + 2 * V_W + RANK + 3 * SB_W
OFF_GQK, OFF_GV, OFF_GR = 0, 2 * QK_W, 2 * QK_W + V_W
OFF_GA = OFF_GR + V_W
OFF_SQ, OFF_SK, OFF_SV = OFF_GA + RANK, OFF_GA + RANK + SB_W, OFF_GA + RANK + 2 * SB_W
CHUNK = 64
GLA_TAU = 16.0
EPS = 1e-6
CLAMP = 30.0
NEVER = -30000.0
PAST, PAGE = 4096, 128
PAGES = PAST // PAGE
N_GROUPS, PER_GROUP = 4, 8
N_EXP = N_GROUPS * PER_GROUP
D_EXP = 512
N_TOK = SEQ + N_META + N_SAMPLE
BLOCKS = (2 * N_TOK + N_EXP * (P - 1)) // P


class Chain:

    def __init__(self, eng, sem, per_round=0, i=0):
        self.eng, self.sem, self.per, self.i, self.n = eng, sem, per_round, i, 0

    def value(self):
        return self.i * self.per + self.n

    def __call__(self, ins, wait=True):
        self.n += 1
        ins.then_inc(self.sem, 1)
        if wait:
            self.eng.wait_ge(self.sem, self.value())

    def sync(self):
        self.eng.wait_ge(self.sem, self.value())

    def done(self):
        assert self.n == self.per, self.n


class Scope:

    def __init__(self, nc, tag):
        self.nc, self.tag, self.ctx, self.sems = nc, tag, ExitStack(), []

    def __enter__(self):
        self.ctx.__enter__()
        return self

    def __exit__(self, *a):
        self.running.__exit__(*a)
        self.nc.clear_and_free_semaphores(self.sems)
        self.nc.all_engine_barrier()
        return self.ctx.__exit__(*a)

    def sb(self, name, shape, dt=F32):
        return self.ctx.enter_context(self.nc.sbuf_tensor(f"{self.tag}_{name}", shape, dt))

    def ps(self, name, shape):
        return self.ctx.enter_context(self.nc.psum_tensor(f"{self.tag}_{name}", shape, F32))

    def sem(self, name):
        self.sems.append(self.nc.alloc_semaphore(f"{self.tag}_{name}"))
        return self.sems[-1]

    def block(self):
        self.running = self.nc.Block()
        return self.running.__enter__()


def make_identity(nc, pool, ident, done):
    nc.gpsimd.memset(ident[:], 0.0).then_inc(done, 1)
    pool.wait_ge(done, 1)
    nc.gpsimd.affine_select(out=ident[:], in_=ident[:], compare_op=ALU.not_equal, fill=1.0, base=0,
                            pattern=[[-1, P]], channel_multiplier=1).then_inc(done, 1)


def phase_project(nc, d):
    with Scope(nc, "pr") as s:
        w = s.sb("w_in", [P, KD, D_IN])
        w_alpha = s.sb("w_alpha", [RANK, QK_W])
        gain = s.sb("gain", [P, KD])
        q_gain = s.sb("q_gain", [P, SD])
        k_gain = s.sb("k_gain", [P, SD])
        b_alpha = s.sb("b_alpha", [P, QK_W])
        ident = s.sb("ident", [P, P])
        x = s.sb("x", [P, D_MODEL])
        xn = s.sb("xn", [P, D_MODEL])
        sq = s.sb("sq", [P, D_MODEL])
        ssum = s.sb("ssum", [P, 4])
        eps = s.sb("eps", [P, 1])
        xT = s.sb("xT", [P, KD, P])
        gaT = s.sb("gaT", [RANK, P])
        headsq = s.sb("headsq", [P, 2, SB_W])
        headss = s.sb("headss", [P, 2, SH])
        headln = s.sb("headln", [P, 2, SH])
        headrs = s.sb("headrs", [P, 2, SH])
        qk = s.sb("qk", [P, 2, SB_W])
        qkT = s.sb("qkT", [P, 2, 4 * P])
        gqk = s.sb("gqk", [P, 2 * QK_W])
        gv = s.sb("gv", [P, V_W])
        gr = s.sb("gr", [P, V_W])
        sv = s.sb("sv", [P, SB_W])
        t_a = s.sb("t_a", [P, QK_W])
        m_a = s.sb("m_a", [P, QK_W])
        e_a = s.sb("e_a", [P, QK_W])
        l_a = s.sb("l_a", [P, QK_W])
        l2_a = s.sb("l2_a", [P, QK_W])
        la = s.sb("la", [P, QK_W])

        extra = s.sb("extra", [SH, 4, ROWS])
        logit_bias = s.sb("logit_bias", [SH, 1])
        extra_step, bias_loaded, st_extra = s.sem("extra_step"), s.sem("bias_loaded"), s.sem("st_extra")

        ps_x = [s.ps("xT0", [P, 512]), s.ps("xT1", [P, 512])]
        ps_qkT = [s.ps("qT", [P, 512]), s.ps("kT", [P, 512])]
        bank = [s.ps(f"c{n}", [P, 512]) for n in range(4)]

        w_loaded, small_loaded, x_loaded, x0_loaded, x0_zero = (
            s.sem("w_loaded"), s.sem("small_loaded"), s.sem("x_loaded"), s.sem("x0_loaded"), s.sem("x0_zero"))
        ident_ready, eps_ready = s.sem("ident_ready"), s.sem("eps_ready")
        ss_ready, rstd_ready, xn_ready = s.sem("ss_ready"), s.sem("rstd_ready"), s.sem("xn_ready")
        act_step, dve_step = s.sem("act_step"), s.sem("dve_step")
        xT_done, xT_act, xT_dve = s.sem("xT_done"), s.sem("xT_act"), s.sem("xT_dve")
        proj_done = s.sem("proj_done")
        q_used, k_used, gqk_out, gv_out, gr_out, sv_out = (
            s.sem("q_used"), s.sem("k_used"), s.sem("gqk_out"), s.sem("gv_out"), s.sem("gr_out"), s.sem("sv_out"))
        ga_out, hl_step, ea_step = s.sem("ga_out"), s.sem("hl_step"), s.sem("ea_step")
        hs_ready, hsum_ready, hr_ready = s.sem("hs_ready"), s.sem("hsum_ready"), s.sem("hr_ready")
        qk_ready, qkT_done, qT_out, kT_out = s.sem("qk_ready"), s.sem("qkT_done"), s.sem("qT_out"), s.sem("kT_out")
        m_ready, l_ready, la_ready = s.sem("m_ready"), s.sem("l_ready"), s.sem("la_ready")
        st_qkT, st_k, st_gqk, st_gv, st_gr, st_sv, st_la = (s.sem(f"st_{n}") for n in
                                                            ("qkT", "k", "gqk", "gv", "gr", "sv", "la"))
        block = s.block()
        LAST = TILES - 1

        @block.sync
        def _(sp):
            sp.wait_ge(x0_zero, 1)
            sp.dma_start(x[0:N_SAMPLE, :], d["x_sample"].rearrange("b t m -> (b t) m")).then_inc(x0_loaded, 16)
            sp.dma_start(x[PAD:P, :], d["meta_tokens"]).then_inc(x0_loaded, 16)
            w_rows = d["w_in"][0].rearrange("(k p) n -> p k n", p=P)
            for k in range(KD):
                sp.dma_start(w[:, k, :], w_rows[:, k, :]).then_inc(w_loaded, 16)

            def store(i, rows):
                sp.wait_ge(gqk_out, i + 1)
                sp.dma_start(d["s_gqk"][rows, :], gqk[:]).then_inc(st_gqk, 16)
                sp.wait_ge(gv_out, i + 1)
                sp.dma_start(d["s_gv"][rows, :], gv[:]).then_inc(st_gv, 16)
                sp.wait_ge(gr_out, i + 1)
                sp.dma_start(d["s_gr"][rows, :], gr[:]).then_inc(st_gr, 16)
                sp.wait_ge(sv_out, i + 1)
                sp.dma_start(d["s_v"].rearrange("h t e -> t h e")[rows], sv[:].rearrange("p (h e) -> p h e", h=SH)
                             ).then_inc(st_sv, 16)
                sp.wait_ge(qk_ready, 2 * i + 2)
                sp.dma_start(d["s_k"][rows, :], qk[:, 1, :]).then_inc(st_k, 16)
                sp.wait_ge(la_ready, i + 1)
                sp.dma_start(d["s_la"][rows, :], la[:]).then_inc(st_la, 16)

            with sp.Fori(0, LAST) as i:
                rows = bass.ds(sp.snap(i * P), P)
                sp.wait_ge(xn_ready, i + 1)
                sp.dma_start(x[:], d["x_prompt"][0, rows, :]).then_inc(x_loaded, 16)
                store(i, rows)
            store(LAST, slice(LAST * P, ROWS))
            for st, n in ((st_gqk, 1), (st_gv, 1), (st_gr, 1), (st_sv, 1), (st_k, 1), (st_la, 1)):
                sp.wait_ge(st, 16 * n * TILES)

        @block.gpsimd
        def _(pool):
            make_identity(nc, pool, ident, ident_ready)
            nc.gpsimd.memset(extra[:, 0, :], 0.0)
            nc.gpsimd.memset(extra[:, 1:3, :], 1.0)
            nc.gpsimd.memset(extra[:, 3, 0:PAD], NEVER)
            nc.gpsimd.memset(extra[:, 3, PAD:], 0.0).then_inc(extra_step, 1)
            pool.dma_start(logit_bias[:], d["sb_logit_bias"][0].rearrange("(h o) -> h o", o=1)).then_inc(bias_loaded, 16)
            pool.wait_ge(bias_loaded, 16)
            pool.wait_ge(extra_step, 1)
            nc.gpsimd.tensor_scalar(extra[:, 0, :], extra[:, 0, :], logit_bias[:], None, ALU.add).then_inc(extra_step, 1)
            pool.wait_ge(extra_step, 2)
            for n, name in enumerate(("s_qT", "s_kT")):
                pool.dma_start(d[name][:, SD:, :], extra[:, 2 * n:2 * n + 2, :]).then_inc(st_extra, 16)
            pool.wait_ge(st_extra, 32)

        @block.scalar
        def _(act):
            nc.scalar.preload_act_table_set("natural_log_exp_and_others")
            act.dma_start(gain[:], d["norm_mix_gain"][0].rearrange("(k p) -> p k", p=P),
                          allow_slow_non_contiguous=True).then_inc(small_loaded, 16)
            act.dma_start(w_alpha[:], d["gla_w_alpha"][0]).then_inc(small_loaded, 16)
            act.dma_start(b_alpha[:], d["gla_b_alpha"][0].partition_broadcast(P)).then_inc(small_loaded, 16)
            act.dma_start(q_gain[:], d["sb_q_gain"][0].partition_broadcast(P)).then_inc(small_loaded, 16)
            act.dma_start(k_gain[:], d["sb_k_gain"][0].partition_broadcast(P)).then_inc(small_loaded, 16)
            act.wait_ge(eps_ready, 1)

            def norm(t, c):
                c(nc.scalar.activation(sq[:], x[:], ACT.Square, accum_out=ssum[:, 0:1]))
                c(nc.scalar.activation(ssum[:, 1:2], ssum[:, 0:1], ACT.Ln, bias=eps[:], scale=1.0 / D_MODEL))
                nc.scalar.activation(ssum[:, 2:3], ssum[:, 1:2], ACT.Exp, scale=-0.5).then_inc(rstd_ready, 1)

            def transposed(t):
                act.wait_ge(xT_done, t + 1)
                for k in range(0, KD // 2):
                    nc.scalar.activation(xT[:, k, :], ps_x[0][:, k * P:(k + 1) * P], ACT.Copy,
                                         scale=gain[:, k:k + 1]).then_inc(xT_act, 1)

            PER = 2
            act.wait_ge(x0_loaded, 32)
            norm(0, Chain(act, act_step))
            act.wait_ge(small_loaded, 80)
            transposed(0)

            def work(i, last, rows):
                if not last:
                    act.wait_ge(x_loaded, 16 * i + 16)
                    act.wait_ge(xn_ready, i + 1)
                    c = Chain(act, act_step, PER, i)
                    c.n = PER
                    norm(i + 1, c)
                for n in range(2):
                    act.wait_ge(proj_done, 8 * i + n + 1)
                    act.wait_ge(hsum_ready, 2 * i + n)
                    nc.scalar.activation(headsq[:, n, :], bank[n][:], ACT.Square).then_inc(hs_ready, 1)
                for n in range(2):
                    act.wait_ge(hsum_ready, 2 * i + n + 1)
                    nc.scalar.activation(headln[:, n, :], headss[:, n, :], ACT.Ln, bias=eps[:],
                                         scale=1.0 / SD).then_inc(hl_step, 1)
                    act.wait_ge(hl_step, 2 * i + n + 1)
                    nc.scalar.activation(headrs[:, n, :], headln[:, n, :], ACT.Exp, scale=-0.5).then_inc(hr_ready, 1)
                act.wait_ge(proj_done, 8 * i + 4)
                act.wait_ge(st_gv, 16 * i)
                nc.scalar.copy(gv[:], bank[3][:]).then_inc(gv_out, 1)
                act.wait_ge(proj_done, 8 * i + 5)
                nc.scalar.copy(gaT[:], ps_x[0][0:RANK, 0:P]).then_inc(ga_out, 1)
                act.wait_ge(m_ready, i + 1)
                nc.scalar.activation(e_a[:], m_a[:], ACT.Exp).then_inc(ea_step, 1)
                act.wait_ge(ea_step, i + 1)
                nc.scalar.activation(l_a[:], e_a[:], ACT.Ln, bias=1.0).then_inc(l_ready, 1)
                act.wait_ge(proj_done, 8 * i + 6)
                act.wait_ge(st_gr, 16 * i)
                nc.scalar.copy(gr[:], bank[0][:]).then_inc(gr_out, 1)
                act.wait_ge(qkT_done, 2 * i + 1)
                act.wait_ge(st_qkT, 64 * i)
                nc.scalar.copy(qkT[:, 0, :], ps_qkT[0][:]).then_inc(qT_out, 1)
                if not last:
                    transposed(i + 1)
                act.wait_ge(qT_out, i + 1)
                act.wait_ge(kT_out, i + 1)
                for n, name in enumerate(("s_qT", "s_kT")):
                    for a in range(2):
                        act.dma_start(d[name].rearrange("(g a) r t -> a r g t", a=2)[a, 0:SD, :, rows],
                                      qkT[a * SD:(a + 1) * SD, n, :].rearrange("p (g t) -> p g t", g=4)
                                      ).then_inc(st_qkT, 16)

            with act.Fori(0, LAST) as i:
                work(i, False, bass.ds(i * P, P))
            work(LAST, True, slice(LAST * P, ROWS))
            act.wait_ge(st_qkT, 64 * TILES)

        @block.vector
        def _(dve):
            nc.vector.memset(eps[:], EPS).then_inc(eps_ready, 1)
            nc.vector.memset(x[:], 0.0).then_inc(x0_zero, 1)

            def norm(t):
                dve.wait_ge(rstd_ready, t + 1)
                dve.wait_ge(xT_done, t)
                nc.vector.tensor_scalar(xn[:], x[:], ssum[:, 2:3], None, ALU.mult).then_inc(xn_ready, 1)

            def transposed(t):
                dve.wait_ge(xT_done, t + 1)
                for k in range(KD // 2, KD):
                    nc.vector.tensor_scalar(xT[:, k, :], ps_x[1][:, (k - 4) * P:(k - 3) * P],
                                            gain[:, k:k + 1], None, ALU.mult).then_inc(xT_dve, 1)

            dve.wait_ge(x0_loaded, 32)
            norm(0)
            dve.wait_ge(small_loaded, 80)
            transposed(0)
            nc.vector.tensor_scalar(q_gain[:], q_gain[:], float(SD) ** -0.5, None, ALU.mult).then_inc(eps_ready, 1)
            dve.wait_ge(eps_ready, 2)
            PER = 2

            def work(i, last):
                if not last:
                    norm(i + 1)
                c = Chain(dve, dve_step, PER, i)
                for n in range(2):
                    dve.wait_ge(hs_ready, 2 * i + n + 1)
                    dve.wait_ge(hr_ready, 2 * i + n)
                    nc.vector.tensor_reduce(headss[:, n, :], headsq[:, n, :].rearrange("p (h e) -> p h e", h=SH),
                                            AX.X, ALU.add).then_inc(hsum_ready, 1)
                for n, (g, used) in enumerate(((q_gain, q_used), (k_gain, k_used))):
                    dve.wait_ge(hr_ready, 2 * i + n + 1)
                    dve.wait_ge(qkT_done, 2 * i)
                    if n == 1:
                        dve.wait_ge(st_k, 16 * i)
                    out = qk[:, n, :].rearrange("p (h e) -> p h e", h=SH)
                    nc.vector.tensor_tensor(out, bank[n][:].rearrange("p (h e) -> p h e", h=SH),
                                            headrs[:, n, :].unsqueeze(2).to_broadcast([P, SH, SD]),
                                            ALU.mult).then_inc(used, 1)
                    dve.wait_ge(used, i + 1)
                    nc.vector.tensor_tensor(out, out, g[:].unsqueeze(1).to_broadcast([P, SH, SD]),
                                            ALU.mult).then_inc(qk_ready, 1)
                dve.wait_ge(proj_done, 8 * i + 3)
                dve.wait_ge(st_gqk, 16 * i)
                nc.vector.tensor_copy(gqk[:], bank[2][:]).then_inc(gqk_out, 1)
                dve.wait_ge(proj_done, 8 * i + 7)
                dve.wait_ge(la_ready, i)
                c(nc.vector.tensor_tensor(t_a[:], bank[1][:, 0:QK_W], b_alpha[:], ALU.add))
                dve.wait_ge(l_ready, i)
                nc.vector.tensor_scalar(m_a[:], t_a[:], -1.0, CLAMP, ALU.mult, ALU.min).then_inc(m_ready, 1)
                dve.wait_ge(l_ready, i + 1)
                c(nc.vector.scalar_tensor_tensor(l2_a[:], t_a[:], -1.0, l_a[:], ALU.mult, ALU.max))
                dve.wait_ge(st_la, 16 * i)
                nc.vector.tensor_scalar(la[:], l2_a[:], -1.0 / GLA_TAU, None, ALU.mult).then_inc(la_ready, 1)
                dve.wait_ge(proj_done, 8 * i + 8)
                dve.wait_ge(st_sv, 16 * i)
                nc.vector.tensor_copy(sv[:], bank[2][:]).then_inc(sv_out, 1)
                dve.wait_ge(qkT_done, 2 * i + 2)
                dve.wait_ge(st_qkT, 64 * i)
                nc.vector.tensor_copy(qkT[:, 1, :], ps_qkT[1][:]).then_inc(kT_out, 1)
                if not last:
                    transposed(i + 1)
                c.done()

            with dve.Fori(0, LAST) as i:
                work(i, False)
            work(LAST, True)

        @block.tensor
        def _(pe):
            def transpose_x(t):
                pe.wait_ge(xn_ready, t + 1)
                for k in range(KD):
                    last = nc.tensor.transpose(ps_x[k // 4][:, (k % 4) * P:(k % 4 + 1) * P],
                                               xn[:, k * P:(k + 1) * P], ident[:])
                last.then_inc(xT_done, 1)

            def project(out, off, n):
                for k in range(KD):
                    last = nc.tensor.matmul(out, xT[:, k, :], w[:, k, off:off + n], start=k == 0, stop=k == KD - 1)
                last.then_inc(proj_done, 1)

            pe.wait_ge(ident_ready, 2)
            transpose_x(0)
            pe.wait_ge(w_loaded, 16 * KD)
            pe.wait_ge(small_loaded, 80)

            def work(i, last_tile):
                pe.wait_ge(xT_act, 4 * i + 4)
                pe.wait_ge(xT_dve, 4 * i + 4)
                pe.wait_ge(gr_out, i)
                project(bank[0][:], OFF_SQ, SB_W)
                pe.wait_ge(m_ready, i)
                project(bank[1][:], OFF_SK, SB_W)
                pe.wait_ge(sv_out, i)
                project(bank[2][:], OFF_GQK, 2 * QK_W)
                pe.wait_ge(gv_out, i)
                project(bank[3][:], OFF_GV, V_W)
                for k in range(KD):
                    last = nc.tensor.matmul(ps_x[0][0:RANK, 0:P], w[:, k, OFF_GA:OFF_GA + RANK], xT[:, k, :],
                                            start=k == 0, stop=k == KD - 1)
                last.then_inc(proj_done, 1)
                pe.wait_ge(q_used, i + 1)
                project(bank[0][:], OFF_GR, V_W)
                pe.wait_ge(k_used, i + 1)
                pe.wait_ge(ga_out, i + 1)
                nc.tensor.matmul(bank[1][:, 0:QK_W], gaT[:], w_alpha[:], start=True, stop=True).then_inc(proj_done, 1)
                pe.wait_ge(gqk_out, i + 1)
                project(bank[2][:], OFF_SV, SB_W)
                for n, out in enumerate((qT_out, kT_out)):
                    pe.wait_ge(qk_ready, 2 * i + n + 1)
                    pe.wait_ge(out, i)
                    for g in range(4):
                        last = nc.tensor.transpose(ps_qkT[n][:, g * P:(g + 1) * P],
                                                   qk[:, n, g * P:(g + 1) * P], ident[:])
                    last.then_inc(qkT_done, 1)
                if not last_tile:
                    transpose_x(i + 1)

            with pe.Fori(0, LAST) as i:
                work(i, False)
            work(LAST, True)


def phase_gla_prompt(nc, d):
    H2 = P // 2
    with Scope(nc, "gp") as s:
        ident = s.sb("ident", [P, P])
        sums = s.sb("sums", [P, 4, P])
        causal = s.sb("causal", [P, P])
        ones = s.sb("ones", [P, 1])
        la, gqk, gv = s.sb("la", [P, QK_W]), s.sb("gqk", [P, 2 * QK_W]), s.sb("gv", [P, V_W])
        ex = s.sb("ex", [P, 4, QK_W])
        exn = s.sb("exn", [P, QK_W])
        scaled = s.sb("scaled", [P, 4, QK_W])
        ke = s.sb("ke", [P, QK_W])
        tT = s.sb("tT", [P, 4, 2, P])
        sc = s.sb("sc", [P, 2, 2, P])
        decay = s.sb("decay", [P, 2])
        state = s.sb("state", [P, 2, GDV])
        o = s.sb("o", [P, V_W])
        ps_b = [s.ps("b0", [P, 512]), s.ps("b1", [P, 512])]
        ps_t = [s.ps("t0", [P, 512]), s.ps("t1", [P, 512])]
        ps_s = [s.ps("s0", [P, 512]), s.ps("s1", [P, 512])]
        ps_kv = s.ps("kv", [P, 512])
        ps_d = s.ps("d", [P, 512])
        (consts, zeroed, la_loaded, qk_loaded, v_loaded, b_done, ex_ready, qk_ready, t_done, t_act, t_dve, s_done,
         sc_ready, o_done, kv_done, state_ready, o_ready, stored, state_stored) = (s.sem(n) for n in (
             "consts", "zeroed", "la_loaded", "qk_loaded", "v_loaded", "b_done", "ex_ready", "qk_ready", "t_done",
             "t_act", "t_dve", "s_done", "sc_ready", "o_done", "kv_done", "state_ready", "o_ready", "stored",
             "state_stored"))
        block = s.block()
        head = lambda h: (h % 2 * GDK, h % 2 * GDK + GDK, h // 2)

        @block.sync
        def _(sp):
            def load(c, to, rows):
                sp.wait_ge(b_done, c)
                sp.dma_start(la[to, :], d["s_la"][rows, :]).then_inc(la_loaded, 16)
                sp.wait_ge(qk_ready, c * 6)
                sp.dma_start(gqk[to, :], d["s_gqk"][rows, :]).then_inc(qk_loaded, 16)
                sp.wait_ge(kv_done, c)
                sp.dma_start(gv[to, :], d["s_gv"][rows, :]).then_inc(v_loaded, 16)

            sp.wait_ge(zeroed, 3)
            load(0, slice(PAD, P), slice(PAD, P))
            with sp.Fori(1, TILES) as c:
                rows = bass.ds(sp.snap(c * P), P)
                load(c, slice(0, P), rows)
            sp.wait_ge(state_ready, 1 + GH * TILES)
            sp.dma_start(d["new_gla_prompt"][0, 0].rearrange("(g a) k v -> a k g v", a=2)[0],
                         state[0:GDK]).then_inc(state_stored, 16)
            sp.dma_start(d["new_gla_prompt"][0, 0].rearrange("(g a) k v -> a k g v", a=2)[1],
                         state[GDK:]).then_inc(state_stored, 16)
            sp.wait_ge(state_stored, 32)

        def consts_on_pool(pool):
            n = 0

            def step(ins):
                nonlocal n
                n += 1
                ins.then_inc(consts, 1)
                pool.wait_ge(consts, n)

            def select(t, op, base, step_t, mult):
                step(nc.gpsimd.affine_select(out=t, in_=t, compare_op=op, fill=0.0, base=base,
                                             pattern=[[step_t, t.shape[1]]], channel_multiplier=mult))

            step(nc.gpsimd.memset(ident[:], 0.0))
            step(nc.gpsimd.affine_select(out=ident[:], in_=ident[:], compare_op=ALU.not_equal, fill=1.0, base=0,
                                         pattern=[[-1, P]], channel_multiplier=1))
            step(nc.gpsimd.memset(ones[:], 1.0))
            step(nc.gpsimd.memset(sums[:], 1.0))
            step(nc.gpsimd.memset(causal[:], 1.0))
            for t in (sums[:, 0, :], sums[:, 1, :], causal[:]):
                select(t, ALU.is_ge, 0, 1, -1)
            step(nc.gpsimd.tensor_scalar(sums[0:32, 1, :], sums[0:32, 1, :], 1.0, None, ALU.subtract))
            for lo in (32, 64):
                step(nc.gpsimd.tensor_scalar(sums[lo:lo + 32, 1, H2:], sums[lo:lo + 32, 1, H2:], 1.0, None,
                                             ALU.subtract))
            select(sums[:, 2, :], ALU.is_gt, 0, -1, 1)
            select(sums[:, 3, 0:H2], ALU.is_gt, 0, -1, 1)
            select(sums[:, 3, 0:H2], ALU.is_gt, H2, 0, -1)
            select(sums[:, 3, H2:], ALU.is_ge, H2, 1, -1)
            select(sums[:, 3, H2:], ALU.is_ge, -H2, 0, 1)
            return n

        CONSTS = 16

        @block.gpsimd
        def _(pool):
            for n, t in enumerate((la, gqk, gv)):
                nc.gpsimd.memset(t[:], 0.0).then_inc(zeroed, 1)
            assert consts_on_pool(pool) == CONSTS

        @block.scalar
        def _(act):
            nc.scalar.preload_act_table_set("natural_log_exp_and_others")
            def work(c, rows, of):
                act.wait_ge(b_done, c + 1)
                act.wait_ge(qk_ready, c * 6)
                for n in range(2):
                    nc.scalar.activation(ex[:, 2 * n:2 * n + 2, :], ps_b[n][:].rearrange("p (a n) -> p a n", a=2),
                                         ACT.Exp).then_inc(ex_ready, 1)
                nc.scalar.activation(exn[:], ps_b[0][:, QK_W:], ACT.Exp, scale=-1.0).then_inc(ex_ready, 1)
                act.wait_ge(state_ready, c * GH + 1)
                nc.scalar.activation(decay[:], ps_d[:, 0:2], ACT.Exp).then_inc(ex_ready, 1)
                act.wait_ge(t_done, 2 * c + 1)
                act.wait_ge(s_done, c)
                nc.scalar.copy(tT[:, 0:2], ps_t[0][:].rearrange("p (a g t) -> p a g t", a=2, g=2)
                               ).then_inc(t_act, 1)
                act.wait_ge(o_done, c + 1)
                act.wait_ge(stored, c * 16)
                for a in range(2):
                    nc.scalar.copy(o[:].rearrange("p (g a v) -> p a g v", g=2, a=2)[:, a],
                                   ps_s[a][:, 256:].rearrange("p (g v) -> p g v", g=2)).then_inc(o_ready, 1)
                act.wait_ge(o_ready, 2 * c + 2)
                act.dma_start(d["s_og"][rows, :], o[of, :]).then_inc(stored, 16)

            work(0, slice(PAD, P), slice(PAD, P))
            with act.Fori(1, TILES) as c:
                work(c, bass.ds(act.snap(c * P), P), slice(0, P))
            act.wait_ge(stored, 16 * TILES)

        @block.vector
        def _(dve):
            nc.vector.memset(state[:], 0.0).then_inc(state_ready, 1)
            dve.wait_ge(consts, CONSTS)

            def work(c):
                dve.wait_ge(qk_loaded, c * 16 + 16)
                dve.wait_ge(ex_ready, c * 4 + 3)
                dve.wait_ge(t_done, 2 * c)
                dve.wait_ge(kv_done, c)
                q, k = gqk[:, 0:QK_W], gqk[:, QK_W:]
                for out, src, by, rows in ((scaled[:, 0], q, ex[:, 1], slice(0, P)), (scaled[:, 1], k, exn, slice(0, P)),
                                           (scaled[:, 2], q, ex[:, 0], slice(0, P)),
                                           (scaled[:, 3], k, ex[:, 3], slice(0, H2)),
                                           (scaled[:, 3], q, ex[:, 3], slice(H2, P)),
                                           (ke, k, ex[:, 2], slice(0, P))):
                    nc.vector.scalar_tensor_tensor(out[rows, :], src[rows, :], GDK ** -0.5 if src is q else 1.0,
                                                   by[rows, :], ALU.mult, ALU.mult).then_inc(qk_ready, 1)
                dve.wait_ge(t_done, 2 * c + 2)
                dve.wait_ge(o_done, c)
                nc.vector.tensor_copy(tT[:, 2:4], ps_t[1][:].rearrange("p (a g t) -> p a g t", a=2, g=2)
                                      ).then_inc(t_dve, 1)
                dve.wait_ge(s_done, c + 1)
                for a in range(2):
                    nc.vector.scalar_tensor_tensor(sc[:, a], ps_s[a][:, 0:256].rearrange("p (g t) -> p g t", g=2),
                                                   1e37, causal[:].unsqueeze(1).to_broadcast([P, 2, P]), ALU.min,
                                                   ALU.mult).then_inc(sc_ready, 1)
                dve.wait_ge(kv_done, c + 1)
                dve.wait_ge(ex_ready, c * 4 + 4)
                dve.wait_ge(state_ready, c * GH + 1)
                for h in range(GH):
                    lo, hi, g = head(h)
                    nc.vector.scalar_tensor_tensor(state[lo:hi, g, :], state[lo:hi, g, :], decay[lo:hi, g:g + 1],
                                                   ps_kv[lo:hi, h * GDV:(h + 1) * GDV], ALU.mult,
                                                   ALU.add).then_inc(state_ready, 1)

            work(0)
            with dve.Fori(1, TILES) as c:
                work(c)

        @block.tensor
        def _(pe):
            pe.wait_ge(consts, CONSTS)

            def work(c):
                pe.wait_ge(la_loaded, c * 16 + 16)
                pe.wait_ge(ex_ready, c * 4)
                for n in range(4):
                    nc.tensor.matmul(ps_b[n // 2][:, n % 2 * QK_W:(n % 2 + 1) * QK_W], sums[:, n, :], la[:],
                                     start=True, stop=True)
                for g in range(2):
                    last = nc.tensor.matmul(ps_d[:, g:g + 1], la[:, g * P:(g + 1) * P], ones[:], start=True,
                                            stop=True)
                last.then_inc(b_done, 1)
                for n in range(4):
                    pe.wait_ge(qk_ready, c * 6 + (n + 1 if n < 3 else 5))
                    if n % 2 == 0:
                        pe.wait_ge(t_dve if n else t_act, c)
                    for g in range(2):
                        last = nc.tensor.transpose(ps_t[n // 2][:, (n % 2 * 2 + g) * P:(n % 2 * 2 + g + 1) * P],
                                                   scaled[:, n, g * P:(g + 1) * P], ident[:])
                    if n % 2:
                        last.then_inc(t_done, 1)
                pe.wait_ge(v_loaded, c * 16 + 16)
                pe.wait_ge(qk_ready, c * 6 + 6)
                pe.wait_ge(state_ready, c * GH + 1)
                for h in range(GH):
                    last_kv = nc.tensor.matmul(ps_kv[:, h * GDV:(h + 1) * GDV], ke[:, h // 2 * P:(h // 2 + 1) * P],
                                               gv[:, h * GDV:(h + 1) * GDV], start=True, stop=True)
                pe.wait_ge(t_act, c + 1)
                pe.wait_ge(t_dve, c + 1)
                pe.wait_ge(sc_ready, 2 * c)
                for h in range(GH):
                    lo, hi, g = head(h)
                    out = ps_s[h % 2]
                    nc.tensor.matmul(out[:, g * P:(g + 1) * P], tT[lo:hi, 1, g, :], tT[lo:hi, 0, g, :], start=True,
                                     stop=True)
                    last = nc.tensor.matmul(out[0:H2, g * P + H2:(g + 1) * P], tT[lo:hi, 3, g, 0:H2],
                                            tT[lo:hi, 3, g, H2:], start=True, stop=True)
                last.then_inc(s_done, 1)
                pe.wait_ge(sc_ready, 2 * c + 2)
                pe.wait_ge(o_ready, 2 * c)
                for h in range(GH):
                    lo, hi, g = head(h)
                    out = ps_s[h % 2][:, 256 + g * GDV:256 + (g + 1) * GDV]
                    nc.tensor.matmul(out, sc[:, h % 2, g, :], gv[:, h * GDV:(h + 1) * GDV], start=True, stop=False)
                    last = nc.tensor.matmul(out, tT[lo:hi, 2, g, :], state[lo:hi, g, :], start=False, stop=True)
                last.then_inc(o_done, 1)
                pe.wait_ge(o_done, c + 1)
                pe.sem_inc(kv_done, 1)

            work(0)
            with pe.Fori(1, TILES) as c:
                work(c)


def phase_gla_sample(nc, d):
    N, B, T = N_SAMPLE, DEC_B, DEC_S
    with Scope(nc, "gs") as s:
        ident = s.sb("ident", [P, P])
        upto = s.sb("upto", [N, N])
        after = s.sb("after", [N, N])
        member = s.sb("member", [N, B])
        la, gqk, gv = s.sb("la", [N, QK_W]), s.sb("gqk", [N, 2 * QK_W]), s.sb("gv", [N, V_W])
        state = s.sb("state", [GDK, B, GH, GDV])
        eb, en, ee = (s.sb(n, [N, QK_W]) for n in ("eb", "en", "ee"))
        qe, kd, ke = (s.sb(n, [N, QK_W]) for n in ("qe", "kd", "ke"))
        kem = s.sb("kem", [N, B, QK_W])
        tT = s.sb("tT", [GDK, 2, GH, N])
        qeTm = s.sb("qeTm", [GDK, B, GH, N])
        sc = s.sb("sc", [N, GH, N])
        decay = s.sb("decay", [GDK, GH, B])
        o = s.sb("o", [N, V_W])
        zero = s.sb("zero", [PAD - N, V_W])
        ps_b, ps_e, ps_d = s.ps("b", [N, 512]), s.ps("e", [N, 512]), s.ps("d", [GDK, 512])
        ps_t, ps_s, ps_o = s.ps("t", [GDK, 512]), s.ps("s", [N, 512]), s.ps("o_", [N, 512])
        ps_kv = [s.ps("kv0", [GDK, 512]), s.ps("kv1", [GDK, 512])]
        (consts, loaded, b_done, ex_ready, qk_ready, t_done, t_ready, s_done, sc_ready, o_done, kv_done,
         state_ready, o_ready, stored, dve_step, zeroed) = (s.sem(n) for n in (
             "consts", "loaded", "b_done", "ex_ready", "qk_ready", "t_done", "t_ready", "s_done", "sc_ready",
             "o_done", "kv_done", "state_ready", "o_ready", "stored", "dve_step", "zeroed"))
        block = s.block()
        rows = slice(0, N)

        @block.sync
        def _(sp):
            sp.dma_start(la[:], d["s_la"][rows, :]).then_inc(loaded, 16)
            sp.dma_start(gqk[:], d["s_gqk"][rows, :]).then_inc(loaded, 16)
            sp.dma_start(gv[:], d["s_gv"][rows, :]).then_inc(loaded, 16)
            sp.dma_start(state[:], d["state_gla"][0].rearrange("b h k v -> k b h v")).then_inc(loaded, 16)
            sp.wait_ge(zeroed, 1)
            sp.dma_start(d["s_og"][N:PAD, :], zero[:]).then_inc(stored, 16)
            sp.dma_start(d["s_os"].rearrange("h t e -> t h e")[N:PAD], zero[:].rearrange("p (h e) -> p h e", h=SH)).then_inc(stored, 16)
            sp.wait_ge(o_ready, 1)
            sp.dma_start(d["s_og"][rows, :], o[:]).then_inc(stored, 16)
            sp.wait_ge(state_ready, B * GH)
            sp.dma_start(d["new_gla_sample"][0].rearrange("b h k v -> k b h v"), state[:]).then_inc(stored, 16)
            sp.wait_ge(stored, 64)

        @block.gpsimd
        def _(pool):
            nc.gpsimd.memset(zero[:], 0.0).then_inc(zeroed, 1)
            make_identity(nc, pool, ident, consts)
            n = 2

            def step(ins):
                nonlocal n
                n += 1
                ins.then_inc(consts, 1)
                pool.wait_ge(consts, n)

            def select(t, op, base, pattern, mult):
                step(nc.gpsimd.affine_select(out=t, in_=t, compare_op=op, fill=0.0, base=base, pattern=pattern,
                                             channel_multiplier=mult))

            for t in (upto, after):
                step(nc.gpsimd.memset(t[:], 1.0))
                select(t[:], ALU.is_ge, 0, [[-T, B], [0, T]], 1)
                select(t[:], ALU.is_ge, T - 1, [[T, B], [0, T]], -1)
            select(upto[:], ALU.is_ge, 0, [[1, N]], -1)
            select(after[:], ALU.is_gt, 0, [[-1, N]], 1)
            step(nc.gpsimd.memset(member[:], 1.0))
            select(member[:], ALU.is_ge, 0, [[-T, B]], 1)
            select(member[:], ALU.is_ge, T - 1, [[T, B]], -1)

        CONSTS = 13

        @block.scalar
        def _(act):
            nc.scalar.preload_act_table_set("natural_log_exp_and_others")
            act.wait_ge(b_done, 1)
            nc.scalar.activation(eb[:], ps_b[:, 0:QK_W], ACT.Exp).then_inc(ex_ready, 1)
            nc.scalar.activation(en[:], ps_b[:, 0:QK_W], ACT.Exp, scale=-1.0).then_inc(ex_ready, 1)
            nc.scalar.activation(ee[:], ps_e[:, 0:QK_W], ACT.Exp).then_inc(ex_ready, 1)
            nc.scalar.activation(decay[:], ps_d[:, 0:GH * B].rearrange("p (h b) -> p h b", h=GH),
                                 ACT.Exp).then_inc(ex_ready, 1)
            act.wait_ge(o_done, 1)
            nc.scalar.copy(o[:], ps_o[:]).then_inc(o_ready, 1)

        @block.vector
        def _(dve):
            nc.vector.memset(qeTm[:], 0.0).then_inc(dve_step, 1)
            dve.wait_ge(loaded, 64)
            dve.wait_ge(ex_ready, 4)
            dve.wait_ge(consts, CONSTS)
            nc.vector.scalar_tensor_tensor(qe[:], gqk[:, 0:QK_W], GDK ** -0.5, eb[:], ALU.mult,
                                           ALU.mult).then_inc(qk_ready, 1)
            nc.vector.tensor_tensor(kd[:], gqk[:, QK_W:], en[:], ALU.mult).then_inc(qk_ready, 1)
            nc.vector.tensor_tensor(ke[:], gqk[:, QK_W:], ee[:], ALU.mult).then_inc(dve_step, 1)
            dve.wait_ge(dve_step, 2)
            for b in range(B):
                nc.vector.tensor_scalar(kem[:, b, :], ke[:], member[:, b:b + 1], None, ALU.mult).then_inc(qk_ready, 1)
            dve.wait_ge(t_done, 1)
            nc.vector.tensor_copy(tT[:], ps_t[:, 0:2 * GH * N].rearrange("p (a h t) -> p a h t", a=2, h=GH)
                                  ).then_inc(t_ready, 1)
            dve.wait_ge(t_ready, 1)
            for b in range(B):
                nc.vector.tensor_copy(qeTm[:, b, :, b * T:(b + 1) * T], tT[:, 0, :, b * T:(b + 1) * T]
                                      ).then_inc(t_ready, 1)
            dve.wait_ge(s_done, 1)
            nc.vector.tensor_tensor(sc[:], ps_s[:, 0:GH * N].rearrange("p (h t) -> p h t", h=GH),
                                    upto[:].unsqueeze(1).to_broadcast([N, GH, N]), ALU.mult).then_inc(sc_ready, 1)
            dve.wait_ge(o_done, 1)
            for b in range(B):
                dve.wait_ge(kv_done, b + 1)
                for h in range(GH):
                    nc.vector.scalar_tensor_tensor(state[:, b, h, :], state[:, b, h, :], decay[:, h, b:b + 1],
                                                   ps_kv[b % 2][:, h * GDV:(h + 1) * GDV], ALU.mult,
                                                   ALU.add).then_inc(state_ready, 1)

        @block.tensor
        def _(pe):
            pe.wait_ge(consts, CONSTS)
            pe.wait_ge(loaded, 64)
            nc.tensor.matmul(ps_b[:, 0:QK_W], upto[:], la[:], start=True, stop=True)
            nc.tensor.matmul(ps_e[:, 0:QK_W], after[:], la[:], start=True, stop=True)
            for h in range(GH):
                last = nc.tensor.matmul(ps_d[:, h * B:(h + 1) * B], la[:, h * GDK:(h + 1) * GDK], member[:],
                                        start=True, stop=True)
            last.then_inc(b_done, 1)
            pe.wait_ge(qk_ready, 2)
            for n, src in enumerate((qe, kd)):
                for h in range(GH):
                    at = (n * GH + h) * N
                    last = nc.tensor.transpose(ps_t[:, at:at + N], src[:, h * GDK:(h + 1) * GDK], ident[0:N, 0:N])
            last.then_inc(t_done, 1)
            pe.wait_ge(t_ready, 1)
            for h in range(GH):
                last = nc.tensor.matmul(ps_s[:, h * N:(h + 1) * N], tT[:, 1, h, :], tT[:, 0, h, :],
                                        start=True, stop=True)
            last.then_inc(s_done, 1)
            pe.wait_ge(sc_ready, 1)
            pe.wait_ge(t_ready, 1 + B)
            for h in range(GH):
                out = ps_o[:, h * GDV:(h + 1) * GDV]
                nc.tensor.matmul(out, sc[:, h, :], gv[:, h * GDV:(h + 1) * GDV], start=True, stop=False)
                for b in range(B):
                    last = nc.tensor.matmul(out, qeTm[:, b, h, :], state[:, b, h, :], start=False, stop=b == B - 1)
            last.then_inc(o_done, 1)
            pe.wait_ge(qk_ready, 2 + B)
            for b in range(B):
                if b >= 2:
                    pe.wait_ge(state_ready, (b - 1) * GH)
                for h in range(GH):
                    last = nc.tensor.matmul(ps_kv[b % 2][:, h * GDV:(h + 1) * GDV], kem[:, b, h * GDK:(h + 1) * GDK],
                                            gv[:, h * GDV:(h + 1) * GDV], start=True, stop=True)
                last.then_inc(kv_done, 1)


def attention_units():
    units = []
    for g in range((TILES - 1) // 4, -1, -1):
        q0, q1 = max(4 * g - 3, 0), 4 * g
        for j in range(q1, -1, -1):
            units.append((g, j, q0, q1, max(j - q0, 0) * P, j == q1))
    return units


def phase_attend(nc, d):
    units = attention_units()
    NU, NG = len(units), (TILES - 1) // 4 + 1
    R, RA = 5, 3
    assert NU % R == 0 and NU % RA == 0
    KA = SD + 2
    width = [(q1 - q0 + 1) * P for g, j, q0, q1, c0, first in units]
    with Scope(nc, "at") as s:
        neg_tri = s.sb("neg_tri", [P, P])
        neg_ones = s.sb("neg_ones", [P, P])
        ident = s.sb("ident", [P, P])
        never = s.sb("never", [P, P])
        zeros = s.sb("zeros", [P, P])
        kT = s.sb("kT", [KA, ROWS])
        qT = s.sb("qT", [KA, ROWS])
        v = s.sb("v", [P, TILES, SD])
        L = s.sb("L", [P, R, 512])
        acc = s.sb("acc", [P, 3, 512])
        a = s.sb("a", [P, RA, 512])
        o = s.sb("o", [P, 2, 4, SD])
        ps_d = [s.ps(f"d{n}", [P, 512]) for n in range(R)]
        ps_o = [s.ps(f"o{n}", [P, 512]) for n in range(2)]
        (consts, ones_ready, z_done, m_ready, e_step, l_ready, L_ready, acc_ready, d_done, a_ready,
         o_done, o_out, stored) = (s.sem(n) for n in (
             "consts", "ones_ready", "z_done", "m_ready", "e_step", "l_ready", "L_ready", "acc_ready",
             "d_done", "a_ready", "o_done", "o_out", "stored"))
        loaded = [s.sem(f"loaded{g}") for g in range(NG)]
        block = s.block()

        def done(h, n):
            return h * NU + (n + 1 + R)

        def summed(h, n):
            n_sums = NU - NG
            before = sum(units[m][1] > 0 for m in range(n % NU + 1))
            return (h + n // NU) * n_sums + (before + R) if n >= 0 else h * n_sums + (before - n_sums + R)

        ranges = [(max(4 * g - 3, 0), 4 * g) for g in range(NG - 1, -1, -1)]
        last_of = [max(n for n in range(NU) if units[n][0] == NG - 1 - k) for k in range(NG)]

        @block.sync
        def _(sp):
            def load(h, k, skip=0):
                q0, q1 = ranges[k]
                cols = slice(q0 * P, (q1 + 1) * P)
                for t, name, skipped in ((kT, "s_kT", skip), (qT, "s_qT", 0)):
                    use = slice(q0 * P + skipped, (q1 + 1) * P)
                    sp.dma_start(t[:, use], d[name][bass.ds(h, 1), :, use].rearrange("a r t -> (a r) t")
                                 ).then_inc(loaded[k], 16)
                sp.dma_start(v[:, q0:q1 + 1, :], d["s_v"][bass.ds(h, 1), cols].rearrange("a (t p) e -> p (a t) e", p=P)
                             ).then_inc(loaded[k], 16)

            def store(h, k):
                q0, q1 = ranges[k]
                sp.wait_ge(o_out, h * NG + (k + 1))
                if q0:
                    sp.dma_start(d["s_os"][bass.ds(h, 1), q0 * P:(q1 + 1) * P].rearrange("a (t p) e -> p (a t) e", p=P),
                                 o[:, k % 2]).then_inc(stored, 16)
                else:
                    sp.dma_start(d["s_os"][bass.ds(h, 1), PAD:P].rearrange("a p e -> (a p) e"),
                                 o[PAD:P, k % 2, 0, :]).then_inc(stored, 16)

            for k in range(NG):
                load(0, k)
            with sp.Fori(0, SH - 1) as h:
                for k in range(NG):
                    sp.wait_ge(o_done, done(h, last_of[k]))
                    load(h + 1, k, skip=0 if ranges[k][0] else 1)
                    store(h, k)
            for k in range(NG):
                store(SH - 1, k)
            sp.wait_ge(stored, SH * NG * 16)

        @block.gpsimd
        def _(pool):
            nc.gpsimd.memset(neg_ones[:], -1.0).then_inc(ones_ready, 1)
            nc.gpsimd.memset(neg_tri[:], -1.0).then_inc(consts, 1)
            pool.wait_ge(consts, 1)
            nc.gpsimd.affine_select(out=neg_tri[:], in_=neg_tri[:], compare_op=ALU.is_ge, fill=0.0, base=0,
                                    pattern=[[-1, P]], channel_multiplier=1).then_inc(ones_ready, 1)
            nc.gpsimd.memset(never[:], NEVER).then_inc(consts, 1)
            pool.wait_ge(consts, 2)
            nc.gpsimd.affine_select(out=never[:], in_=never[:], compare_op=ALU.is_ge, fill=0.0, base=0,
                                    pattern=[[-1, P]], channel_multiplier=1).then_inc(ones_ready, 1)
            nc.gpsimd.memset(zeros[:], 0.0).then_inc(consts, 1)
            nc.gpsimd.memset(ident[:], 0.0).then_inc(consts, 1)
            pool.wait_ge(consts, 4)
            nc.gpsimd.affine_select(out=ident[:], in_=ident[:], compare_op=ALU.not_equal, fill=1.0, base=0,
                                    pattern=[[-1, P]], channel_multiplier=1).then_inc(ones_ready, 1)
            pool.sem_inc(acc_ready, R)

            def sum_up(h, n):
                g, j, q0, q1, c0, first = units[n]
                W, l, new, old = width[n], L[:, n % R, :], acc[:, n % 3, :], acc[:, (n - 1) % 3, :]
                if j == 0:
                    return
                pool.wait_ge(d_done, done(h, n - 2))
                pool.wait_ge(acc_ready, summed(h, n - 1))
                pool.wait_ge(L_ready, done(h, n) - R)
                lo = c0
                if j >= q0:
                    lo = c0 + P
                    ins = nc.gpsimd.tensor_tensor(new[:, c0:lo], l[:, c0:lo], zeros[:], ALU.add)
                if lo < W:
                    ins = nc.gpsimd.tensor_tensor(new[:, lo:W], l[:, lo:W], old[:, lo:W], ALU.add)
                ins.then_inc(acc_ready, 1)

            with pool.Fori(0, SH) as h:
                for n in range(NU):
                    sum_up(h, n)

        @block.scalar
        def _(act):
            nc.scalar.preload_act_table_set("natural_log_exp_and_others")
            act.sem_inc(a_ready, R)
            act.sem_inc(e_step, R)

            def weight(h, n):
                g, j, q0, q1, c0, first = units[n]
                act.wait_ge(d_done, done(h, n))
                act.wait_ge(o_done, done(h, n - RA))
                nc.scalar.activation(a[:, n % RA, c0:width[n]], ps_d[n % R][:, c0:width[n]],
                                     ACT.Exp).then_inc(a_ready, 1)

            with act.Fori(0, SH) as h:
                for n in range(NU + 2):
                    if n < NU:
                        g, j, q0, q1, c0, first = units[n]
                        l = L[:, n % R, c0:width[n]]
                        act.wait_ge(m_ready, done(h, n) - R)
                        nc.scalar.activation(l, l, ACT.Exp).then_inc(e_step, 1)
                    if n >= 2:
                        weight(h, n - 2)
                    if n < NU:
                        act.wait_ge(e_step, done(h, n))
                        nc.scalar.activation(l, l, ACT.Ln, bias=1.0).then_inc(l_ready, 1)

        @block.vector
        def _(dve):
            def clamp(h, n):
                g, j, q0, q1, c0, first = units[n]
                dve.wait_ge(z_done, done(h, n) - R)
                dve.wait_ge(d_done, done(h, n - R))
                dve.wait_ge(acc_ready, summed(h, n - R))
                nc.vector.tensor_scalar(L[:, n % R, c0:width[n]], ps_d[n % R][:, c0:width[n]], CLAMP, None,
                                        ALU.min).then_inc(m_ready, 1)

            def softplus(h, n):
                g, j, q0, q1, c0, first = units[n]
                dve.wait_ge(l_ready, done(h, n) - R)
                l = L[:, n % R, c0:width[n]]
                nc.vector.tensor_tensor(l, ps_d[n % R][:, c0:width[n]], l, ALU.max).then_inc(L_ready, 1)

            def out(h, k):
                T = ranges[k][1] - ranges[k][0] + 1
                dve.wait_ge(o_done, done(h, last_of[k]))
                dve.wait_ge(stored, (h * NG + k) * 16)
                nc.vector.tensor_copy(o[:, k % 2, 0:T, :], ps_o[k % 2][:, 0:T * SD].rearrange(
                    "p (t e) -> p t e", t=T)).then_inc(o_out, 1)

            with dve.Fori(0, SH) as h:
                clamp(h, 0)
                for n in range(NU):
                    if n + 1 < NU:
                        clamp(h, n + 1)
                    softplus(h, n)
                    for k in range(NG):
                        if last_of[k] + 5 == n:
                            out(h, k)
                for k in range(NG):
                    if last_of[k] + 5 >= NU:
                        out(h, k)

        @block.tensor
        def _(pe):
            pe.sem_inc(d_done, R)
            pe.sem_inc(o_done, R)
            pe.wait_ge(ones_ready, 4)

            def logits(h, n):
                g, j, q0, q1, c0, first = units[n]
                if first:
                    pe.wait_ge(loaded[NG - 1 - g], h * 48 + 48)
                elif j < q0 and j % 4 == 0:
                    pe.wait_ge(loaded[NG - 1 - j // 4], h * 48 + 48)
                pe.wait_ge(a_ready, done(h, n - R))
                last = nc.tensor.matmul(ps_d[n % R][:, c0:width[n]], kT[:, j * P:(j + 1) * P],
                                        qT[:, q0 * P + c0:(q1 + 1) * P], start=True, stop=True)
                if j >= q0:
                    last = nc.tensor.matmul(ps_d[n % R][:, c0:c0 + P], ident[:], never[:], start=False, stop=True,
                                            skip_group_check=True)
                last.then_inc(z_done, 1)

            def exponent(h, n):
                g, j, q0, q1, c0, first = units[n]
                pe.wait_ge(L_ready, done(h, n) - R)
                last = nc.tensor.matmul(ps_d[n % R][:, c0:width[n]], neg_tri[:], L[:, n % R, c0:width[n]],
                                        start=False, stop=True, skip_group_check=True)
                if not first:
                    lo = c0 + P if j >= q0 else c0
                    pe.wait_ge(acc_ready, summed(h, n - 1))
                    last = nc.tensor.matmul(ps_d[n % R][:, lo:width[n]], neg_ones[:], acc[:, (n - 1) % 3, lo:width[n]],
                                            start=False, stop=True, skip_group_check=True)
                last.then_inc(d_done, 1)

            def values(h, n):
                g, j, q0, q1, c0, first = units[n]
                k = NG - 1 - g
                if first:
                    pe.wait_ge(o_out, h * NG + max(k - 1, 0))
                pe.wait_ge(a_ready, done(h, n))
                for t in range(c0 // P, q1 - q0 + 1):
                    last = nc.tensor.matmul(ps_o[k % 2][:, t * SD:(t + 1) * SD], a[:, n % RA, t * P:(t + 1) * P],
                                            v[:, j, :], start=first, stop=j == 0, skip_group_check=True)
                last.then_inc(o_done, 1)

            with pe.Fori(0, SH) as h:
                for n in range(NU + 4):
                    if n < NU:
                        logits(h, n)
                    if 2 <= n < NU + 2:
                        exponent(h, n - 2)
                    if n >= 4:
                        values(h, n - 4)


def phase_attend_sample(nc, d):
    B, T = DEC_B, DEC_S
    HQ = SH * T
    NS = PAGES + 1
    G = SH // 2
    HALF = PAGES // 2
    W3 = HQ * NS // 3
    with Scope(nc, "as") as s:
        ident = s.sb("ident", [P, P])
        neg_ones = s.sb("neg_ones", [P, P])
        below = s.sb("below", [P, P])
        never = s.sb("never", [P, B, SH, T])
        restart = s.sb("restart", [P, HQ, NS])
        bias = s.sb("bias", [P, SH])
        bias_hq = s.sb("bias_hq", [P, SH, T])
        qT = s.sb("qT", [P, G, N_SAMPLE])
        q2 = s.sb("q2", [P, B, G, 2, T])
        kT_new = s.sb("kT_new", [P, G, P])
        v_new = s.sb("v_new", [P, SB_W])
        table = s.sb("table", [1, B * PAGES], I32)
        kp = s.sb("kp", [P, PAGES, SB_W])
        vp = s.sb("vp", [P, PAGES, SB_W])
        kT = s.sb("kT", [P, 4, SB_W])
        zb = s.sb("zb", [P, HQ, NS])
        L = s.sb("L", [P, HQ, NS])
        run = s.sb("run", [P, HQ, NS])
        oT = s.sb("oT", [P, G, B, T])
        o = s.sb("o", [N_SAMPLE, SB_W])
        ps_kT = [s.ps("kT0", [P, 512]), s.ps("kT1", [P, 512])]
        ps_z = [s.ps(f"z{n}", [P, 512]) for n in range(3)]
        ps_o = s.ps("o_", [P, 512])
        (consts, loaded, table_loaded, q_step, ready, kT_done, kT_dve, kT_act, k_used, v_used, z_done, zb_ready,
         m_ready, e_step, l_ready, L_ready, run_ready, d_done, arg_ready, a_ready, o_done, o_ready, t_done, t_ready,
         stored) = (s.sem(n) for n in (
             "consts", "loaded", "table_loaded", "q_step", "ready", "kT_done", "kT_dve", "kT_act", "k_used", "v_used",
             "z_done", "zb_ready", "m_ready", "e_step", "l_ready", "L_ready", "run_ready", "d_done", "arg_ready",
             "a_ready", "o_done", "o_ready", "t_done", "t_ready", "stored"))
        k_loaded = [s.sem(f"k{p}") for p in range(PAGES)]
        v_loaded = [s.sem(f"v{p}") for p in range(PAGES)]
        block = s.block()
        N_LOADS = 7

        @block.sync
        def _(sp):
            sp.dma_start(table[:], d["page_table"].rearrange("(o b) n -> o (b n)", o=1)).then_inc(table_loaded, 16)
            sp.wait_ge(table_loaded, 16)
            pages = d["cache_sb_k"].shape[1]
            k_rows = d["cache_sb_k"][0].rearrange("n t h e -> n t (h e)")
            v_rows = d["cache_sb_v"][0].rearrange("n t h e -> n t (h e)")
            with sp.Fori(0, B) as b:
                for rows, buf, sems, used, order in (
                        (k_rows, kp, k_loaded, k_used, range(PAGES)),
                        (v_rows, vp, v_loaded, v_used, range(PAGES - 1, -1, -1))):
                    for n, p in enumerate(order):
                        if n % 8 == 0:
                            first = min(p, order[n + 7])
                            _, ids = nc.values_load_multi_w_load_instructions(
                                table[0:1, bass.ds(b * PAGES + first, 8)], engines=[mybir.EngineType.SP],
                                min_val=0, max_val=pages - 1)
                        page = ids[p - first]
                        if n % 8 == 0:
                            sp.wait_ge(used, b * PAGES + (n + 8))
                        sp.dma_start(buf[:, p, :], rows[bass.ds(page, 1)].rearrange("a t n -> (a t) n")
                                     ).then_inc(sems[p], 16)
            sp.wait_ge(t_ready, 1)
            sp.dma_start(d["s_os"].rearrange("h t e -> t h e")[0:N_SAMPLE], o[:].rearrange("p (h e) -> p h e", h=SH)
                         ).then_inc(stored, 16)
            sp.wait_ge(stored, 16)

        @block.gpsimd
        def _(pool):
            n = 0

            def step(ins):
                nonlocal n
                n += 1
                ins.then_inc(consts, 1)
                pool.wait_ge(consts, n)

            def select(t, op, fill, base, pattern, mult):
                step(nc.gpsimd.affine_select(out=t, in_=t, compare_op=op, fill=fill, base=base, pattern=pattern,
                                             channel_multiplier=mult))

            step(nc.gpsimd.memset(ident[:], 0.0))
            select(ident[:], ALU.not_equal, 1.0, 0, [[-1, P]], 1)
            step(nc.gpsimd.memset(neg_ones[:], -1.0))
            step(nc.gpsimd.memset(below[:], 1.0))
            select(below[:], ALU.is_gt, 0.0, 0, [[1, P]], -1)
            step(nc.gpsimd.memset(restart[:], 1.0))
            step(nc.gpsimd.memset(restart[:, :, 0:1], 0.0))
            step(nc.gpsimd.memset(never[:], 0.0))
            select(never[:], ALU.is_ge, NEVER, 0, [[-T, B], [0, SH], [0, T]], 1)
            select(never[:], ALU.is_gt, NEVER, 0, [[T, B], [0, SH], [1, T]], -1)

        CONSTS = 10

        @block.scalar
        def _(act):
            nc.scalar.preload_act_table_set("natural_log_exp_and_others")
            for a in range(2):
                lo, hi = a * SD, (a + 1) * SD
                act.dma_start(qT[lo:hi], d["s_qT"].rearrange("(g a) r t -> a r g t", a=2)[a, 0:SD, :, 0:N_SAMPLE]
                              ).then_inc(loaded, 16)
                act.dma_start(kT_new[lo:hi], d["s_kT"].rearrange("(g a) r t -> a r g t", a=2)[a, 0:SD, :, 0:P]
                              ).then_inc(loaded, 16)
            act.dma_start(v_new[:].rearrange("p (h e) -> p h e", h=SH), d["s_v"].rearrange("h t e -> t h e")[0:P]
                          ).then_inc(loaded, 16)
            act.dma_start(bias[:], d["sb_logit_bias"][0].partition_broadcast(P)).then_inc(loaded, 16)
            with act.Fori(0, B) as b:
                for n in range(PAGES // 2):
                    act.wait_ge(kT_done, b * PAGES + (2 * n + 2))
                    act.wait_ge(k_used, b * PAGES + (2 * n + 2 - 4 + PAGES))
                    nc.scalar.copy(kT[:, (2 * n + 1) % 4, :], ps_kT[1][:]).then_inc(kT_act, 1)
                act.wait_ge(m_ready, b + 1)
                nc.scalar.activation(L[:], L[:], ACT.Exp).then_inc(e_step, 1)
                act.wait_ge(e_step, b + 1)
                nc.scalar.activation(L[:], L[:], ACT.Ln, bias=1.0).then_inc(l_ready, 1)
                act.wait_ge(arg_ready, 3 * b + 3)
                nc.scalar.activation(zb[:], zb[:], ACT.Exp).then_inc(a_ready, 1)
            act.wait_ge(t_done, 1)
            nc.scalar.copy(o[:], ps_o[0:N_SAMPLE, :]).then_inc(t_ready, 1)

        @block.vector
        def _(dve):
            nc.vector.memset(q2[:], 0.0).then_inc(q_step, 1)
            dve.wait_ge(loaded, 96)
            dve.wait_ge(q_step, 1)
            for a in range(2):
                for g in range(G):
                    nc.vector.tensor_copy(q2[a * SD:(a + 1) * SD, :, g, a, :],
                                          qT[a * SD:(a + 1) * SD, g, :].rearrange("p (b t) -> p b t", b=B)
                                          ).then_inc(ready, 1)
            nc.vector.tensor_copy(bias_hq[:], bias[:].unsqueeze(2).to_broadcast([P, SH, T])).then_inc(ready, 1)
            dve.wait_ge(ready, 2 * G + 1)
            dve.wait_ge(consts, CONSTS)
            by_hq = bias_hq[:].rearrange("p h t -> p (h t)")

            with dve.Fori(0, B) as b:
                for n in range(PAGES // 2):
                    dve.wait_ge(kT_done, b * PAGES + (2 * n + 1))
                    dve.wait_ge(k_used, b * PAGES + (2 * n + 1 - 4 + PAGES))
                    nc.vector.tensor_copy(kT[:, 2 * n % 4, :], ps_kT[0][:]).then_inc(kT_dve, 1)
                dve.wait_ge(z_done, b + 1)
                dve.wait_ge(v_used, b * PAGES + PAGES)
                for n, (r0, k) in enumerate(((1 + HALF, HALF), (1, HALF), (0, 1))):
                    nc.vector.tensor_tensor(zb[:, :, r0:r0 + k],
                                            ps_z[n][:, 0:k * HQ].rearrange("p (r x) -> p x r", r=k),
                                            by_hq.unsqueeze(2).to_broadcast([P, HQ, k]), ALU.add).then_inc(zb_ready, 1)
                dve.wait_ge(zb_ready, 3 * b + 3)
                nc.vector.tensor_scalar(L[:], zb[:], CLAMP, None, ALU.min).then_inc(m_ready, 1)
                dve.wait_ge(l_ready, b + 1)
                nc.vector.tensor_tensor(L[:], zb[:], L[:], ALU.max).then_inc(L_ready, 1)
                dve.wait_ge(L_ready, b + 1)
                flat = lambda t: t[:].rearrange("p x r -> p (x r)")
                nc.vector.tensor_tensor_scan(flat(run), flat(restart), flat(L), 0.0, ALU.mult, ALU.add
                                             ).then_inc(run_ready, 1)
                for n in range(3):
                    dve.wait_ge(d_done, 3 * b + n + 1)
                    z = flat(zb)[:, n * W3:(n + 1) * W3]
                    nc.vector.tensor_tensor(z, ps_z[n][:, 0:W3], z, ALU.add).then_inc(arg_ready, 1)
                dve.wait_ge(o_done, b + 1)
                for a in range(2):
                    nc.vector.tensor_scalar(oT[a * SD:(a + 1) * SD, :, bass.ds(b, 1), :].rearrange("p g b t -> p g (b t)"),
                                            ps_o[a * SD:(a + 1) * SD, 0:HQ].rearrange("p (g a t) -> p g a t", g=G, a=2)[:, :, a],
                                            1.0, None, ALU.mult).then_inc(o_ready, 1)

        @block.tensor
        def _(pe):
            pe.sem_inc(k_used, PAGES)
            pe.sem_inc(v_used, PAGES)
            pe.wait_ge(consts, CONSTS)
            pe.wait_ge(loaded, 96)
            pe.wait_ge(ready, 2 * G + 1)

            def z_of(b, kt, out, start=True):
                for g in range(G):
                    ins = nc.tensor.matmul(out[:, g * 2 * T:(g + 1) * 2 * T], kt[:, g * P:(g + 1) * P],
                                           q2[:, bass.ds(b, 1), g].rearrange("p b a t -> p (b a t)"),
                                           start=start, stop=True, skip_group_check=not start)
                return ins

            with pe.Fori(0, B) as b:
                pe.wait_ge(arg_ready, 3 * b)
                for p in range(PAGES + 2):
                    if p < PAGES:
                        pe.wait_ge(k_loaded[p], b * 16 + 16)
                        evac, half = (kT_dve, kT_act)[p % 2], p // 2
                        pe.wait_ge(evac, b * HALF + half)
                        for g in range(G):
                            last = nc.tensor.transpose(ps_kT[p % 2][:, g * P:(g + 1) * P],
                                                       kp[:, p, g * P:(g + 1) * P], ident[:])
                        last.then_inc(kT_done, 1)
                    if p >= 2:
                        m = p - 2
                        pe.wait_ge((kT_dve, kT_act)[m % 2], b * HALF + (m // 2 + 1))
                        at = (HALF - 1 - m % HALF) * HQ
                        z_of(b, kT[:, m % 4, :], ps_z[m // HALF][:, at:at + HQ]).then_inc(k_used, 1)
                nc.tensor.matmul(ps_z[2][:, 0:HQ], ident[:], never[:, bass.ds(b, 1)].rearrange("p b h t -> p (b h t)"),
                                 start=True, stop=True)
                z_of(b, kT_new[:].rearrange("p g t -> p (g t)"), ps_z[2][:, 0:HQ], start=False).then_inc(z_done, 1)
                pe.wait_ge(run_ready, b + 1)
                for n in range(3):
                    cols = slice(n * W3, (n + 1) * W3)
                    nc.tensor.matmul(ps_z[n][:, 0:W3], neg_ones[:], run[:].rearrange("p x r -> p (x r)")[:, cols],
                                     start=True, stop=False)
                    nc.tensor.matmul(ps_z[n][:, 0:W3], below[:], L[:].rearrange("p x r -> p (x r)")[:, cols],
                                     start=False, stop=True).then_inc(d_done, 1)
                pe.wait_ge(a_ready, b + 1)
                pe.wait_ge(o_ready, 2 * b)
                for r in range(NS):
                    p = PAGES - r
                    if r:
                        pe.wait_ge(v_loaded[p], b * 16 + 16)
                    vt = vp[:, p, :] if r else v_new[:]
                    for g in range(G):
                        last = nc.tensor.matmul(ps_o[:, g * 2 * T:(g + 1) * 2 * T], vt[:, g * P:(g + 1) * P],
                                                zb[:, g * 2 * T:(g + 1) * 2 * T, r], start=r == 0 and g == 0,
                                                stop=r == NS - 1, skip_group_check=True)
                    if r:
                        last.then_inc(v_used, 1)
                pe.wait_ge(v_used, b * PAGES + 2 * PAGES)
                pe.sem_inc(o_done, 1)
            pe.wait_ge(o_ready, 2 * B)
            for g in range(G):
                last = nc.tensor.transpose(ps_o[0:N_SAMPLE, g * P:(g + 1) * P],
                                           oT[:, g].rearrange("p b t -> p (b t)"), ident[:])
            last.then_inc(t_done, 1)


def phase_out_route(nc, d):
    LAST = TILES - 1
    NR = N_GROUPS + N_EXP
    CONSTS, ROUTE, PLACE_STEPS = 14, 15, 25
    with Scope(nc, "or") as s:
        ident = s.sb("ident", [P, P])
        w_out = s.sb("w_out", [P, KD, D_MODEL])
        w_r = s.sb("w_r", [P, KD, NR])
        b_r = s.sb("b_r", [P, NR])
        g_gain = s.sb("g_gain", [P, GDV])
        s_gain = s.sb("s_gain", [P, SD])
        f_gain = s.sb("f_gain", [P, D_MODEL])
        eps = s.sb("eps", [P, 1])
        og, os_, gr = s.sb("og", [P, V_W]), s.sb("os", [P, SB_W]), s.sb("gr", [P, V_W])
        x = s.sb("x", [P, D_MODEL])
        sq = s.sb("sq", [P, 2, 512])
        ss, ln, rs = (s.sb(n, [P, GH + SH]) for n in ("ss", "ln", "rs"))
        sil = s.sb("sil", [P, V_W])
        sil2 = s.sb("sil2", [P, V_W])
        cat = s.sb("cat", [P, D_MODEL])
        catT = s.sb("catT", [P, KD, P])
        h = s.sb("h", [P, D_MODEL])
        hsq = s.sb("hsq", [P, D_MODEL])
        hs = s.sb("hs", [P, 4])
        hn = s.sb("hn", [P, D_MODEL])
        hnT = s.sb("hnT", [P, KD, P])
        before = s.sb("before", [P, P])
        ones = s.sb("ones", [P, P])
        iota_e = s.sb("iota_e", [P, N_EXP])
        iota_ei = s.sb("iota_ei", [P, N_EXP], I32)
        valid = s.sb("valid", [P, TILES])
        g8 = s.sb("g8", [P, 8])
        le = s.sb("le", [P, N_GROUPS, PER_GROUP])
        gm8, m8 = s.sb("gm8", [P, 8]), s.sb("m8", [P, 8])
        gi8, i8 = s.sb("gi8", [P, 8], U32), s.sb("i8", [P, 8], U32)
        gf = s.sb("gf", [P, 2])
        own = s.sb("own", [P, N_GROUPS])
        tmp8 = s.sb("tmp8", [P, PER_GROUP, N_GROUPS])
        l8 = s.sb("l8", [P, PER_GROUP])
        ef = s.sb("ef", [P, 2])
        e2 = s.sb("e2", [P, 2])
        E = s.sb("E", [P, 2, N_EXP])
        total = s.sb("total", [P, N_EXP])
        all_E = s.sb("all_E", [P, 2, TILES, N_EXP])
        all_pos = s.sb("all_pos", [P, TILES, N_EXP])
        all_g = s.sb("all_g", [P, TILES, N_GROUPS])
        all_m = s.sb("all_m", [P, TILES, 2])

        ps_t = [s.ps("t0", [P, 512]), s.ps("t1", [P, 512])]
        ps_h = [s.ps("h0", [P, 512]), s.ps("h1", [P, 512])]
        ps_n = [s.ps("n0", [P, 512]), s.ps("n1", [P, 512])]
        ps_r = s.ps("r", [P, 512])
        ps_p = s.ps("p", [P, 512])
        (consts, w_loaded, small, og_loaded, os_loaded, gr_loaded, x_loaded, x0_zero, sq_ready, ss_ready, ln_step,
         rs_ready, min_ready, ex_ready, sil_step, cat_step, cat_ready, cT_done, cT_act, cT_dve, o_done, h_ready,
         hss_step, hrs_ready, hn_step, hn_ready, st_h, st_n, nT_done, nT_act, nT_dve, r_done, dve_step, E_ready,
         p_done, route_done) = (s.sem(n) for n in (
             "consts", "w_loaded", "small", "og_loaded", "os_loaded", "gr_loaded", "x_loaded", "x0_zero", "sq_ready",
             "ss_ready", "ln_step", "rs_ready", "min_ready", "ex_ready", "sil_step", "cat_step", "cat_ready",
             "cT_done", "cT_act", "cT_dve", "o_done", "h_ready", "hss_step", "hrs_ready", "hn_step", "hn_ready",
             "st_h", "st_n", "nT_done", "nT_act", "nT_dve", "r_done", "dve_step", "E_ready", "p_done", "route_done"))
        cnt_i = s.sb("cnt_i", [P, N_EXP], I32)
        blk_i = s.sb("blk_i", [P, N_EXP], I32)
        blk = s.sb("blk", [P, N_EXP])
        ends = s.sb("ends", [P, N_EXP])
        start = s.sb("start", [P, N_EXP])
        one_row = s.sb("one_row", [P, N_EXP])
        picked = s.sb("picked", [P, TILES, N_EXP])
        dest = s.sb("dest", [P, 2, TILES])
        dest_u = s.sb("dest_u", [P, 2, TILES], I32)
        skip = s.sb("skip", [P, TILES])
        to = s.sb("to", [P, 2, TILES])
        to_u = s.sb("to_u", [P, 2, TILES], I32)
        token = s.sb("token", [P, TILES], I32)
        zero_i = s.sb("zero_i", [BLOCKS, P], I32)
        number = s.sb("number", [1, BLOCKS, N_EXP])
        le_b = s.sb("le_b", [1, BLOCKS, N_EXP])
        block_e = s.sb("block_e", [1, BLOCKS])
        block_i = s.sb("block_i", [1, BLOCKS], I32)
        eg = s.sb("eg", [P, TILES, N_GROUPS])
        gsum = s.sb("gsum", [P, TILES])
        em = s.sb("em", [P, TILES, 2])
        msum = s.sb("msum", [P, TILES])
        prod = s.sb("prod", [P, TILES])
        gate = s.sb("gate", [P, TILES])
        gates = s.sb("gates", [P, 2, TILES])
        (pos_ready, total_step, place_step, c_done, to_ready, soft_ready, stored, rows_zero, scattered) = (s.sem(n) for n in (
            "pos_ready", "total_step", "place_step", "c_done", "to_ready", "soft_ready", "stored", "rows_zero", "scattered"))
        block = s.block()

        @block.sync
        def _(sp):
            def load(t, rows, x_rows):
                sp.wait_ge(cat_ready, 3 * t)
                sp.dma_start(og[:], d["s_og"][rows, :]).then_inc(og_loaded, 16)
                sp.dma_start(os_[:].rearrange("p (h e) -> p h e", h=SH), d["s_os"].rearrange("h t e -> t h e")[rows]
                             ).then_inc(os_loaded, 16)
                sp.dma_start(gr[:], d["s_gr"][rows, :]).then_inc(gr_loaded, 16)
                sp.wait_ge(h_ready, 2 * t)
                if x_rows is not None:
                    sp.dma_start(x[:], d["x_prompt"][0, x_rows, :]).then_inc(x_loaded, 16)
                else:
                    sp.wait_ge(x0_zero, 1)
                    sp.dma_start(x[0:N_SAMPLE, :], d["x_sample"].rearrange("b t m -> (b t) m")).then_inc(x_loaded, 16)
                    sp.dma_start(x[PAD:P, :], d["meta_tokens"]).then_inc(x_loaded, 16)

            load(0, slice(0, P), None)
            w_rows = d["w_out"][0].rearrange("(k p) n -> p k n", p=P)
            for k in range(KD):
                sp.dma_start(w_out[:, k, :], w_rows[:, k, :]).then_inc(w_loaded, 16)
            with sp.Fori(1, TILES) as t:
                rows, x_rows = bass.ds(sp.snap(t * P), P), bass.ds(sp.snap(t * P - P), P)
                load(t, rows, x_rows)

        @block.gpsimd
        def _(pool):
            n = 0

            def step(ins):
                nonlocal n
                n += 1
                ins.then_inc(consts, 1)
                pool.wait_ge(consts, n)

            step(nc.gpsimd.memset(ident[:], 0.0))
            step(nc.gpsimd.affine_select(out=ident[:], in_=ident[:], compare_op=ALU.not_equal, fill=1.0, base=0,
                                         pattern=[[-1, P]], channel_multiplier=1))
            step(nc.gpsimd.memset(ones[:], 1.0))
            step(nc.gpsimd.memset(one_row[:], 1.0))
            step(nc.gpsimd.memset(before[:], 1.0))
            step(nc.gpsimd.affine_select(out=before[:], in_=before[:], compare_op=ALU.is_gt, fill=0.0, base=0,
                                         pattern=[[1, P]], channel_multiplier=-1))
            step(nc.gpsimd.iota(iota_ei[:], pattern=[[1, N_EXP]], base=0, channel_multiplier=0))
            step(nc.gpsimd.tensor_copy(iota_e[:], iota_ei[:]))
            step(nc.gpsimd.memset(valid[:], 1.0))
            step(nc.gpsimd.affine_select(out=valid[:, 0:1], in_=valid[:, 0:1], compare_op=ALU.is_ge, fill=0.0,
                                         base=-PAD, pattern=[[0, 1]], channel_multiplier=1))
            step(nc.gpsimd.memset(valid[0:N_SAMPLE, 0:1], 1.0))
            step(nc.gpsimd.iota(token[:], pattern=[[P, TILES]], base=0, channel_multiplier=1))
            step(nc.gpsimd.memset(zero_i[:], 0))
            step(nc.gpsimd.iota(number[:], pattern=[[1, BLOCKS], [0, N_EXP]], base=0, channel_multiplier=0,
                                allow_small_or_imprecise_dtypes=True))
            assert n == CONSTS
            pool.dma_start(d["s_rowtok"].rearrange("(b p) o -> b (p o)", p=P), zero_i[:]).then_inc(rows_zero, 16)
            pool.wait_ge(rows_zero, 16)
            pool.wait_ge(to_ready, 1)
            for k in range(2):
                for t in range(TILES):
                    pool.indirect_dma_start(
                        out=d["s_rowtok"], out_offset=bass.IndirectOffsetOnAxis(ap=to_u[:, k, t:t + 1], axis=0),
                        in_=token[:, t:t + 1], in_offset=None, bounds_check=BLOCKS * P - 1,
                        oob_is_err=False).then_inc(scattered, 16)
            pool.wait_ge(scattered, 16 * 2 * TILES)

        @block.scalar
        def _(act):
            nc.scalar.preload_act_table_set("natural_log_exp_and_others")
            act.dma_start(w_r[:, :, 0:N_GROUPS], d["router_group"][0].rearrange("(k p) n -> p k n", p=P)).then_inc(small, 16)
            for g in range(N_GROUPS):
                lo = N_GROUPS + g * PER_GROUP
                act.dma_start(w_r[:, :, lo:lo + PER_GROUP], d["router_expert"][0, g].rearrange("(k p) n -> p k n", p=P)
                              ).then_inc(small, 16)
            act.dma_start(b_r[:, 0:N_GROUPS], d["router_group_b"][0].partition_broadcast(P)).then_inc(small, 16)
            act.dma_start(b_r[:, N_GROUPS:], d["router_expert_b"][0].rearrange("g e -> (g e)").partition_broadcast(P)
                          ).then_inc(small, 16)
            act.dma_start(g_gain[:], d["gla_out_gain"][0].partition_broadcast(P)).then_inc(small, 16)
            act.dma_start(s_gain[:], d["sb_out_gain"][0].partition_broadcast(P)).then_inc(small, 16)
            act.dma_start(f_gain[:], d["norm_ffn_gain"][0].partition_broadcast(P)).then_inc(small, 16)
            act.wait_ge(consts, CONSTS)
            act.wait_ge(x0_zero, 2)

            def heads(t):
                act.wait_ge(og_loaded, 16 * t + 16)
                act.wait_ge(ss_ready, 2 * t)
                nc.scalar.activation(sq[:, 0], og[:], ACT.Square).then_inc(sq_ready, 1)
                act.wait_ge(os_loaded, 16 * t + 16)
                nc.scalar.activation(sq[:, 1], os_[:], ACT.Square).then_inc(sq_ready, 1)
                act.wait_ge(min_ready, t + 1)
                nc.scalar.activation(sil[:], sil[:], ACT.Exp).then_inc(ex_ready, 1)
                act.wait_ge(ss_ready, 2 * t + 2)
                act.wait_ge(cat_ready, 3 * t)
                nc.scalar.activation(ln[:, 0:GH], ss[:, 0:GH], ACT.Ln, bias=eps[:], scale=1.0 / GDV).then_inc(ln_step, 1)
                nc.scalar.activation(ln[:, GH:], ss[:, GH:], ACT.Ln, bias=eps[:], scale=1.0 / SD).then_inc(ln_step, 1)
                act.wait_ge(ln_step, 2 * t + 2)
                nc.scalar.activation(rs[:], ln[:], ACT.Exp, scale=-0.5).then_inc(rs_ready, 1)

            def cat_out(t):
                act.wait_ge(cT_done, t + 1)
                nc.scalar.copy(catT[:, 0:4, :], ps_t[0][:].rearrange("p (k t) -> p k t", k=4)).then_inc(cT_act, 1)

            def norm(t):
                act.wait_ge(h_ready, 2 * t + 2)
                nc.scalar.activation(hsq[:], h[:], ACT.Square, accum_out=hs[:, 0:1]).then_inc(hss_step, 1)
                act.wait_ge(hss_step, 2 * t + 1)
                nc.scalar.activation(hs[:, 1:2], hs[:, 0:1], ACT.Ln, bias=eps[:], scale=1.0 / D_MODEL).then_inc(hss_step, 1)
                act.wait_ge(hss_step, 2 * t + 2)
                act.wait_ge(hn_ready, t)
                nc.scalar.activation(hs[:, 2:3], hs[:, 1:2], ACT.Exp, scale=-0.5).then_inc(hrs_ready, 1)

            def norm_out(t):
                act.wait_ge(nT_done, t + 1)
                nc.scalar.copy(hnT[:, 0:4, :], ps_n[0][:].rearrange("p (k t) -> p k t", k=4)).then_inc(nT_act, 1)

            def rows_out(t, rows):
                act.wait_ge(h_ready, 2 * t + 2)
                act.dma_start(d["s_h"][rows, :], h[:]).then_inc(st_h, 16)
                act.wait_ge(hn_ready, t + 1)
                act.dma_start(d["s_xn"][rows, :], hn[:]).then_inc(st_n, 16)

            heads(0)
            cat_out(0)
            heads(1)
            norm(0)
            rows_out(0, slice(0, P))
            cat_out(1)
            with act.Fori(1, LAST) as t:
                rows = bass.ds(act.snap(t * P), P)
                norm_out(t - 1)
                heads(t + 1)
                norm(t)
                rows_out(t, rows)
                cat_out(t + 1)
            norm_out(LAST - 1)
            norm(LAST)
            rows_out(LAST, slice(LAST * P, ROWS))
            norm_out(LAST)
            act.wait_ge(route_done, TILES)
            nc.scalar.activation(eg[:], all_g[:], ACT.Exp).then_inc(soft_ready, 1)
            nc.scalar.activation(em[:], all_m[:], ACT.Exp).then_inc(soft_ready, 1)
            act.wait_ge(place_step, PLACE_STEPS)
            act.dma_start(d["s_dest"], dest_u[:].rearrange("p k t -> p (k t)")).then_inc(stored, 16)
            act.dma_start(d["s_gate"], gates[:].rearrange("p k t -> p (k t)")).then_inc(stored, 16)
            act.dma_start(d["s_block_e"], block_i[:]).then_inc(stored, 16)
            act.wait_ge(stored, 48)
            act.wait_ge(st_h, 16 * TILES)
            act.wait_ge(st_n, 16 * TILES)

        @block.vector
        def _(dve):
            nc.vector.memset(x[:], 0.0).then_inc(x0_zero, 1)
            nc.vector.memset(eps[:], EPS).then_inc(x0_zero, 1)
            nc.vector.memset(g8[:], -3e38).then_inc(x0_zero, 1)
            nc.vector.memset(total[:], 0.0).then_inc(x0_zero, 1)
            dve.wait_ge(x0_zero, 4)
            dve.wait_ge(small, 160)
            dve.wait_ge(consts, CONSTS)

            def heads(t):
                dve.wait_ge(gr_loaded, 16 * t + 16)
                nc.vector.tensor_scalar(sil[:], gr[:], -1.0, 80.0, ALU.mult, ALU.min).then_inc(min_ready, 1)
                dve.wait_ge(rs_ready, t)
                dve.wait_ge(sq_ready, 2 * t + 1)
                nc.vector.tensor_reduce(ss[:, 0:GH], sq[:, 0].rearrange("p (h e) -> p h e", h=GH), AX.X, ALU.add
                                        ).then_inc(ss_ready, 1)
                dve.wait_ge(sq_ready, 2 * t + 2)
                nc.vector.tensor_reduce(ss[:, GH:], sq[:, 1].rearrange("p (h e) -> p h e", h=SH), AX.X, ALU.add
                                        ).then_inc(ss_ready, 1)
                c = Chain(dve, sil_step, 3, t)
                dve.wait_ge(ex_ready, t + 1)
                c(nc.vector.tensor_scalar(sil2[:], sil[:], 1.0, None, ALU.add))
                c(nc.vector.reciprocal(sil2[:], sil2[:]))
                c(nc.vector.tensor_tensor(sil2[:], sil2[:], gr[:], ALU.mult))
                c.done()
                c = Chain(dve, cat_step, 3, t)
                dve.wait_ge(rs_ready, t + 1)
                dve.wait_ge(cT_done, t)
                a = cat[:, 0:V_W].rearrange("p (h e) -> p h e", h=GH)
                b = cat[:, V_W:].rearrange("p (h e) -> p h e", h=SH)
                c(nc.vector.tensor_tensor(a, og[:].rearrange("p (h e) -> p h e", h=GH),
                                          rs[:, 0:GH].unsqueeze(2).to_broadcast([P, GH, GDV]), ALU.mult), wait=False)
                c(nc.vector.tensor_tensor(b, os_[:].rearrange("p (h e) -> p h e", h=SH),
                                          rs[:, GH:].unsqueeze(2).to_broadcast([P, SH, SD]), ALU.mult))
                c(nc.vector.tensor_tensor(a, a, g_gain[:].unsqueeze(1).to_broadcast([P, GH, GDV]), ALU.mult))
                c.done()
                nc.vector.tensor_tensor(b, b, s_gain[:].unsqueeze(1).to_broadcast([P, SH, SD]), ALU.mult
                                        ).then_inc(cat_ready, 1)
                nc.vector.tensor_tensor(cat[:, 0:V_W], cat[:, 0:V_W], sil2[:], ALU.mult).then_inc(cat_ready, 2)

            def cat_out(t):
                dve.wait_ge(cT_done, t + 1)
                nc.vector.tensor_copy(catT[:, 4:8, :], ps_t[1][:].rearrange("p (k t) -> p k t", k=4)).then_inc(cT_dve, 1)

            def residual(t):
                dve.wait_ge(x_loaded, 16 * t + 32)
                dve.wait_ge(o_done, t + 1)
                dve.wait_ge(st_h, 16 * t)
                dve.wait_ge(hn_ready, t)
                for n in range(2):
                    cols = slice(n * 512, (n + 1) * 512)
                    nc.vector.tensor_tensor(h[:, cols], ps_h[n][:], x[:, cols], ALU.add).then_inc(h_ready, 1)

            def norm(t):
                dve.wait_ge(hrs_ready, t + 1)
                dve.wait_ge(nT_done, t)
                dve.wait_ge(st_n, 16 * t)
                nc.vector.tensor_scalar(hn[:], h[:], hs[:, 2:3], None, ALU.mult).then_inc(hn_step, 1)
                dve.wait_ge(hn_step, t + 1)
                nc.vector.tensor_tensor(hn[:], hn[:], f_gain[:], ALU.mult).then_inc(hn_ready, 1)

            def norm_out(t):
                dve.wait_ge(nT_done, t + 1)
                nc.vector.tensor_copy(hnT[:, 4:8, :], ps_n[1][:].rearrange("p (k t) -> p k t", k=4)).then_inc(nT_dve, 1)

            def route(t, at):
                c = Chain(dve, dve_step, ROUTE, t)
                dve.wait_ge(r_done, t + 1)
                c(nc.vector.tensor_tensor(g8[:, 0:N_GROUPS], ps_r[:, 0:N_GROUPS], b_r[:, 0:N_GROUPS], ALU.add))
                c(nc.vector.tensor_tensor(le[:].rearrange("p g e -> p (g e)"), ps_r[:, N_GROUPS:NR], b_r[:, N_GROUPS:],
                                          ALU.add), wait=False)
                c(nc.vector.max(gm8[:], g8[:]))
                c(nc.vector.tensor_scalar(all_g[:, at, :].rearrange("p a g -> p (a g)"), g8[:, 0:N_GROUPS], gm8[:, 0:1],
                                          None, ALU.subtract), wait=False)
                c(nc.vector.max_index(gi8[:], gm8[:], g8[:]))
                c(nc.vector.tensor_scalar(gf[:], gi8[:, 0:1].to_broadcast([P, 2]), 1.0, None, ALU.mult))
                c(nc.vector.tensor_scalar(own[:], iota_e[:, 0:N_GROUPS], gf[:, 0:1], None, ALU.is_equal))
                c(nc.vector.tensor_tensor(tmp8[:], le[:].rearrange("p g e -> p e g"),
                                          own[:].unsqueeze(1).to_broadcast([P, PER_GROUP, N_GROUPS]), ALU.mult))
                c(nc.vector.tensor_reduce(l8[:], tmp8[:], AX.X, ALU.add))
                c(nc.vector.tensor_scalar(gf[:], gf[:], float(PER_GROUP), None, ALU.mult), wait=False)
                c(nc.vector.max(m8[:], l8[:]))
                c(nc.vector.tensor_scalar(all_m[:, at, :].rearrange("p a k -> p (a k)"), m8[:, 0:2], m8[:, 0:1], None,
                                          ALU.subtract), wait=False)
                c(nc.vector.max_index(i8[:], m8[:], l8[:]))
                c(nc.vector.tensor_copy(ef[:], i8[:, 0:2]))
                c(nc.vector.tensor_tensor(e2[:], gf[:], ef[:], ALU.add))
                c.done()
                dve.wait_ge(p_done, t)
                for k in range(2):
                    nc.vector.tensor_scalar(E[:, k, :], iota_e[:], e2[:, k:k + 1], valid[:, at], ALU.is_equal, ALU.mult
                                            ).then_inc(E_ready, 1)
                dve.wait_ge(E_ready, 4 * t + 2)
                for k in range(2):
                    nc.vector.tensor_scalar(all_E[:, k, at, :].rearrange("p a e -> p (a e)"), E[:, k, :], 1.0, None,
                                            ALU.mult).then_inc(E_ready, 1)
                dve.wait_ge(p_done, t + 1)
                nc.vector.tensor_scalar(all_pos[:, at, :].rearrange("p a e -> p (a e)"), ps_p[:, 0:N_EXP], 1.0, None,
                                        ALU.mult).then_inc(pos_ready, 1)
                nc.vector.tensor_tensor(total[:], total[:], E[:, 0, :], ALU.add).then_inc(total_step, 1)
                dve.wait_ge(total_step, t + 1)
                nc.vector.tensor_tensor(total[:], total[:], E[:, 1, :], ALU.add).then_inc(route_done, 1)
                dve.wait_ge(route_done, t + 1)

            heads(0)
            cat_out(0)
            heads(1)
            residual(0)
            norm(0)
            cat_out(1)
            with dve.Fori(1, LAST) as t:
                norm_out(t - 1)
                heads(t + 1)
                route(t - 1, bass.ds(dve.snap(t - 1), 1))
                residual(t)
                norm(t)
                cat_out(t + 1)
            norm_out(LAST - 1)
            route(LAST - 1, slice(LAST - 1, LAST))
            residual(LAST)
            norm(LAST)
            norm_out(LAST)
            route(LAST, slice(LAST, TILES))

            c = Chain(dve, place_step)
            dve.wait_ge(pos_ready, TILES)
            dve.wait_ge(E_ready, 4 * TILES)
            dve.wait_ge(soft_ready, 2)
            c(nc.vector.tensor_reduce(gsum[:], eg[:], AX.X, ALU.add), wait=False)
            c(nc.vector.tensor_reduce(msum[:], em[:], AX.X, ALU.add))
            c(nc.vector.tensor_tensor(prod[:], gsum[:], msum[:], ALU.mult))
            c(nc.vector.reciprocal(gate[:], prod[:]))
            for k in range(2):
                c(nc.vector.tensor_tensor(gates[:, k, :], em[:, :, k], gate[:], ALU.mult), wait=False)
            dve.wait_ge(c_done, 1)
            c(nc.vector.tensor_scalar(cnt_i[:], ps_r[:, 0:N_EXP], float(P - 1), None, ALU.add))
            c(nc.vector.tensor_scalar(blk_i[:], cnt_i[:], 7, None, ALU.logical_shift_right))
            c(nc.vector.tensor_copy(blk[:], blk_i[:]))
            c(nc.vector.tensor_tensor_scan(ends[:], one_row[:], blk[:], 0.0, ALU.mult, ALU.add))
            c(nc.vector.tensor_tensor(start[:], ends[:], blk[:], ALU.subtract))
            c(nc.vector.tensor_scalar(start[:], start[:], float(P), None, ALU.mult))
            c(nc.vector.tensor_tensor(all_pos[:], all_pos[:], start[:].unsqueeze(1).to_broadcast([P, TILES, N_EXP]),
                                      ALU.add))
            for k in range(2):
                c(nc.vector.tensor_tensor(picked[:], all_pos[:], all_E[:, k], ALU.mult))
                c(nc.vector.tensor_reduce(dest[:, k], picked[:], AX.X, ALU.add))
            c(nc.vector.tensor_copy(dest_u[:], dest[:]))
            c(nc.vector.tensor_scalar(skip[:], valid[:], -1e6, 1e6, ALU.mult, ALU.add))
            for k in range(2):
                c(nc.vector.tensor_tensor(to[:, k], dest[:, k], skip[:], ALU.add))
            nc.vector.tensor_copy(to_u[:], to[:]).then_inc(to_ready, 1)
            c(nc.vector.tensor_tensor(le_b[:], number[:], ends[0:1, :].unsqueeze(1).to_broadcast([1, BLOCKS, N_EXP]),
                                      ALU.is_ge))
            c(nc.vector.tensor_reduce(block_e[:], le_b[:], AX.X, ALU.add))
            c(nc.vector.tensor_scalar(block_e[:], block_e[:], float(N_EXP - 1), None, ALU.min))
            c(nc.vector.tensor_copy(block_i[:], block_e[:]))
            assert c.n == PLACE_STEPS, c.n

        @block.tensor
        def _(pe):
            def cat_T(t):
                pe.wait_ge(cat_ready, 3 * t + 3)
                for k in range(KD):
                    last = nc.tensor.transpose(ps_t[k // 4][:, k % 4 * P:(k % 4 + 1) * P], cat[:, k * P:(k + 1) * P],
                                               ident[:])
                last.then_inc(cT_done, 1)

            def project(t):
                pe.wait_ge(cT_act, t + 1)
                pe.wait_ge(cT_dve, t + 1)
                pe.wait_ge(h_ready, 2 * t)
                for n in range(2):
                    for k in range(KD):
                        last = nc.tensor.matmul(ps_h[n][:], catT[:, k, :], w_out[:, k, n * 512:(n + 1) * 512],
                                                start=k == 0, stop=k == KD - 1)
                last.then_inc(o_done, 1)

            def norm_T(t):
                pe.wait_ge(hn_ready, t + 1)
                for k in range(KD):
                    last = nc.tensor.transpose(ps_n[k // 4][:, k % 4 * P:(k % 4 + 1) * P], hn[:, k * P:(k + 1) * P],
                                               ident[:])
                last.then_inc(nT_done, 1)

            def router(t):
                pe.wait_ge(nT_act, t + 1)
                pe.wait_ge(nT_dve, t + 1)
                for k in range(KD):
                    last = nc.tensor.matmul(ps_r[:, 0:NR], hnT[:, k, :], w_r[:, k, :], start=k == 0, stop=k == KD - 1)
                last.then_inc(r_done, 1)

            def count(t):
                pe.wait_ge(E_ready, 4 * t + 2)
                pe.wait_ge(route_done, t)
                for k in range(2):
                    nc.tensor.matmul(ps_p[:, 0:N_EXP], before[:], E[:, k, :], start=k == 0, stop=False)
                nc.tensor.matmul(ps_p[:, 0:N_EXP], ones[:], total[:], start=False, stop=True).then_inc(p_done, 1)

            pe.wait_ge(consts, CONSTS)
            pe.wait_ge(small, 160)
            cat_T(0)
            pe.wait_ge(w_loaded, 16 * KD)
            project(0)
            cat_T(1)
            with pe.Fori(1, LAST) as t:
                norm_T(t - 1)
                project(t)
                router(t - 1)
                cat_T(t + 1)
                count(t - 1)
            norm_T(LAST - 1)
            router(LAST - 1)
            count(LAST - 1)
            project(LAST)
            norm_T(LAST)
            router(LAST)
            count(LAST)
            pe.wait_ge(route_done, TILES)
            nc.tensor.matmul(ps_r[:, 0:N_EXP], ones[:], total[:], start=True, stop=True).then_inc(c_done, 1)


def phase_experts(nc, d):
    TURNS = BLOCKS // 2
    KE = D_EXP // P
    with Scope(nc, "ex") as s:
        ident = s.sb("ident", [P, P])
        expert = s.sb("expert", [1, BLOCKS], I32)
        w_gate = [s.sb(f"w_gate{u}", [P, KD, D_EXP]) for u in range(2)]
        w_up = [s.sb(f"w_up{u}", [P, KD, D_EXP]) for u in range(2)]
        w_down = [s.sb(f"w_down{u}", [P, KE, D_MODEL]) for u in range(2)]
        row_of = s.sb("row_of", [P, BLOCKS], I32)
        x = [s.sb(f"x{u}", [P, D_MODEL]) for u in range(2)]
        xT = s.sb("xT", [P, KD, P])
        sil = s.sb("sil", [P, D_EXP])
        hid = s.sb("hid", [P, D_EXP])
        hidT = s.sb("hidT", [P, KE, P])
        y = [s.sb(f"y{u}", [P, D_MODEL]) for u in range(2)]
        ps_x = [s.ps("ps_x0", [P, 512]), s.ps("ps_x1", [P, 512])]
        ps_g, ps_u, ps_h = s.ps("g", [P, 512]), s.ps("u", [P, 512]), s.ps("h", [P, 512])
        ps_y = [s.ps("ps_y0", [P, 512]), s.ps("ps_y1", [P, 512])]
        (ident_done, expert_loaded, xT_done, xT_act, xT_dve, g_done, u_done, sil_ready, hid_ready, hT_done, hT_ready,
         y_done, y_act, y_dve) = (s.sem(n) for n in (
             "ident_done", "expert_loaded", "xT_done", "xT_act", "xT_dve", "g_done", "u_done", "sil_ready",
             "hid_ready", "hT_done", "hT_ready", "y_done", "y_act", "y_dve"))
        rows_known = s.sem("rows_known")
        gate_loaded, up_loaded, down_loaded, x_loaded, st_y = (
            [s.sem(f"{n}{u}") for u in range(2)] for n in ("gate_loaded", "up_loaded", "down_loaded", "x_loaded", "st_y"))
        block = s.block()

        @block.sync
        def _(sp):
            sp.dma_start(expert[:], d["s_block_e"]).then_inc(expert_loaded, 16)
            sp.wait_ge(expert_loaded, 16)

            def load(i, u, first):
                b = 2 * i + u
                where = expert[0:1, u:u + 1] if first else expert[0:1, bass.ds(sp.snap(b), 1)]
                e = nc.values_load_multi_w_load_instructions(where, engines=[mybir.EngineType.SP], min_val=0,
                                                             max_val=N_EXP - 1)[1][0]
                if not first:
                    sp.wait_ge(u_done, b - 1)
                sp.dma_start(w_gate[u][:], d["w_gate"][0, bass.ds(e, 1)].rearrange("o (p k) n -> p (o k) n", k=KD)
                             ).then_inc(gate_loaded[u], 16)
                sp.dma_start(w_up[u][:], d["w_up"][0, bass.ds(e, 1)].rearrange("o (p k) n -> p (o k) n", k=KD)
                             ).then_inc(up_loaded[u], 16)
                if not first:
                    sp.wait_ge(y_done, b - 1)
                sp.dma_start(w_down[u][:], d["w_down"][0, bass.ds(e, 1)].rearrange("o (p k) n -> p (o k) n", k=KE)
                             ).then_inc(down_loaded[u], 16)

            load(0, 0, True)
            load(0, 1, True)
            with sp.Fori(1, TURNS) as i:
                load(i, 0, False)
                load(i, 1, False)

        @block.gpsimd
        def _(pool):
            make_identity(nc, pool, ident, ident_done)

            pool.dma_start(row_of[:], d["s_rowtok"].rearrange("(b p) o -> p (b o)", p=P),
                           allow_slow_non_contiguous=True).then_inc(rows_known, 16)
            pool.wait_ge(rows_known, 16)
            for b in range(BLOCKS):
                if b >= 2:
                    pool.wait_ge(xT_done, b - 1)
                pool.indirect_dma_start(out=x[b % 2][:], out_offset=None, in_=d["s_xn"],
                                        in_offset=bass.IndirectOffsetOnAxis(ap=row_of[:, b:b + 1], axis=0)
                                        ).then_inc(x_loaded[b % 2], 16)

        @block.scalar
        def _(act):
            def x_out(b):
                act.wait_ge(xT_done, b + 1)
                act.wait_ge(u_done, b)
                nc.scalar.copy(xT[:, 0:4, :], ps_x[0][:].rearrange("p (k t) -> p k t", k=4)).then_inc(xT_act, 1)

            def run(i, u, rows, last):
                b = 2 * i + u
                act.wait_ge(g_done, b + 1)
                act.wait_ge(hid_ready, b)
                nc.scalar.activation(sil[:], ps_g[:], ACT.Silu).then_inc(sil_ready, 1)
                if not last:
                    x_out(b + 1)
                act.wait_ge(y_done, b + 1)
                act.wait_ge(st_y[u], 16 * i)
                nc.scalar.copy(y[u][:, 0:512], ps_y[0][:]).then_inc(y_act, 1)
                act.wait_ge(y_act, b + 1)
                act.wait_ge(y_dve, b + 1)
                act.dma_start(d["s_y"][rows, :], y[u][:]).then_inc(st_y[u], 16)

            x_out(0)
            with act.Fori(0, TURNS - 1) as i:
                for u in range(2):
                    run(i, u, bass.ds(act.snap(i * (2 * P) + u * P), P), False)
            for u in range(2):
                run(TURNS - 1, u, slice((BLOCKS - 2 + u) * P, (BLOCKS - 1 + u) * P), u == 1)
            for u in range(2):
                act.wait_ge(st_y[u], 16 * TURNS)

        @block.vector
        def _(dve):
            def x_out(b):
                dve.wait_ge(xT_done, b + 1)
                dve.wait_ge(u_done, b)
                nc.vector.tensor_copy(xT[:, 4:8, :], ps_x[1][:].rearrange("p (k t) -> p k t", k=4)).then_inc(xT_dve, 1)

            def run(i, u, last):
                b = 2 * i + u
                dve.wait_ge(u_done, b + 1)
                dve.wait_ge(sil_ready, b + 1)
                dve.wait_ge(hT_done, b)
                nc.vector.tensor_tensor(hid[:], ps_u[:], sil[:], ALU.mult).then_inc(hid_ready, 1)
                if not last:
                    x_out(b + 1)
                dve.wait_ge(hT_done, b + 1)
                dve.wait_ge(y_done, b)
                nc.vector.tensor_copy(hidT[:], ps_h[:].rearrange("p (k t) -> p k t", k=KE)).then_inc(hT_ready, 1)
                dve.wait_ge(y_done, b + 1)
                dve.wait_ge(st_y[u], 16 * i)
                nc.vector.tensor_copy(y[u][:, 512:], ps_y[1][:]).then_inc(y_dve, 1)

            x_out(0)
            with dve.Fori(0, TURNS - 1) as i:
                for u in range(2):
                    run(i, u, False)
            for u in range(2):
                run(TURNS - 1, u, u == 1)

        @block.tensor
        def _(pe):
            def x_T(i, u):
                b = 2 * i + u
                pe.wait_ge(x_loaded[u], 16 * i + 16)
                pe.wait_ge(xT_act, b)
                pe.wait_ge(xT_dve, b)
                for k in range(KD):
                    last = nc.tensor.transpose(ps_x[k // 4][:, k % 4 * P:(k % 4 + 1) * P],
                                               x[u][:].rearrange("p (c k) -> p k c", k=KD)[:, k, :], ident[:])
                last.then_inc(xT_done, 1)

            def run(i, u, last_block):
                b = 2 * i + u
                pe.wait_ge(xT_act, b + 1)
                pe.wait_ge(xT_dve, b + 1)
                pe.wait_ge(gate_loaded[u], 16 * i + 16)
                pe.wait_ge(hid_ready, b)
                for k in range(KD):
                    last = nc.tensor.matmul(ps_g[:], xT[:, k, :], w_gate[u][:, k, :], start=k == 0, stop=k == KD - 1)
                last.then_inc(g_done, 1)
                pe.wait_ge(up_loaded[u], 16 * i + 16)
                for k in range(KD):
                    last = nc.tensor.matmul(ps_u[:], xT[:, k, :], w_up[u][:, k, :], start=k == 0, stop=k == KD - 1)
                last.then_inc(u_done, 1)
                if not last_block:
                    x_T(i + u, 1 - u)
                pe.wait_ge(hid_ready, b + 1)
                pe.wait_ge(hT_ready, b)
                for k in range(KE):
                    last = nc.tensor.transpose(ps_h[:, k * P:(k + 1) * P],
                                               hid[:].rearrange("p (c k) -> p k c", k=KE)[:, k, :], ident[:])
                last.then_inc(hT_done, 1)
                pe.wait_ge(hT_ready, b + 1)
                pe.wait_ge(down_loaded[u], 16 * i + 16)
                pe.wait_ge(y_act, b)
                pe.wait_ge(y_dve, b)
                for n in range(2):
                    for k in range(KE):
                        last = nc.tensor.matmul(ps_y[n][:], hidT[:, k, :], w_down[u][:, k, n * 512:(n + 1) * 512],
                                                start=k == 0, stop=k == KE - 1)
                last.then_inc(y_done, 1)

            pe.wait_ge(ident_done, 2)
            x_T(0, 0)
            with pe.Fori(0, TURNS - 1) as i:
                for u in range(2):
                    run(i, u, False)
            for u in range(2):
                run(TURNS - 1, u, u == 1)


def phase_combine(nc, d):
    R = 3
    with Scope(nc, "co") as s:
        place = s.sb("place", [P, 2, TILES], I32)
        gate = s.sb("gate", [P, 2, TILES])
        h = [s.sb(f"h{r}", [P, D_MODEL]) for r in range(R)]
        e = [[s.sb(f"e{k}{r}", [P, D_MODEL]) for r in range(R)] for k in range(2)]
        tables, add_step = s.sem("tables"), s.sem("add_step")
        h_loaded, e0_loaded, e1_loaded, stored = ([s.sem(f"{n}{r}") for r in range(R)] for n in (
            "h_loaded", "e0_loaded", "e1_loaded", "stored"))
        e_loaded = [e0_loaded, e1_loaded]
        block = s.block()

        @block.sync
        def _(sp):
            sp.dma_start(place[:].rearrange("p k t -> p (k t)"), d["s_dest"]).then_inc(tables, 16)
            sp.dma_start(gate[:].rearrange("p k t -> p (k t)"), d["s_gate"]).then_inc(tables, 16)
            for t in range(TILES):
                if t >= R:
                    sp.wait_ge(stored[t % R], 16 * (t // R))
                sp.dma_start(h[t % R][:], d["s_h"][t * P:(t + 1) * P, :]).then_inc(h_loaded[t % R], 16)

        @block.gpsimd
        def _(pool):
            pool.wait_ge(tables, 32)
            for t in range(TILES):
                if t >= R:
                    pool.wait_ge(add_step, 2 * (t - R) + 2)
                for k in range(2):
                    pool.indirect_dma_start(
                        out=e[k][t % R][:], out_offset=None, in_=d["s_y"],
                        in_offset=bass.IndirectOffsetOnAxis(ap=place[:, k, t:t + 1], axis=0)
                    ).then_inc(e_loaded[k][t % R], 16)

        @block.vector
        def _(dve):
            dve.wait_ge(tables, 32)
            for t in range(TILES):
                dve.wait_ge(h_loaded[t % R], 16 * (t // R + 1))
                for k in range(2):
                    dve.wait_ge(e_loaded[k][t % R], 16 * (t // R + 1))
                    nc.vector.scalar_tensor_tensor(h[t % R][:], e[k][t % R][:], gate[:, k, t:t + 1], h[t % R][:],
                                                   ALU.mult, ALU.add).then_inc(add_step, 1)
                    dve.wait_ge(add_step, 2 * t + k + 1)

        @block.scalar
        def _(act):
            for t in range(TILES):
                act.wait_ge(add_step, 2 * t + 2)
                if t:
                    act.dma_start(d["y_prompt"][0, (t - 1) * P:t * P, :], h[t % R][:]).then_inc(stored[t % R], 16)
                else:
                    act.dma_start(d["y_sample"].rearrange("b t m -> (b t) m"), h[0][0:N_SAMPLE, :]
                                  ).then_inc(stored[0], 16)
            for r in range(R):
                act.wait_ge(stored[r], 16 * ((TILES - r + R - 1) // R))


def phase_cache_rows(nc, d):
    with Scope(nc, "cr") as s:
        stored = s.sem("stored")
        block = s.block()

        @block.sync
        def _(sp):
            heads = d["s_v"].rearrange("h t e -> t h e")
            sp.dma_start(d["new_k_sample"][0].rearrange("b t h e -> (b t) (h e)"), d["s_k"][0:N_SAMPLE, :]
                         ).then_inc(stored, 16)
            sp.dma_start(d["new_v_sample"][0].rearrange("b t h e -> (b t) h e"), heads[0:N_SAMPLE]).then_inc(stored, 16)
            sp.dma_start(d["new_k_prompt"][0, 0].rearrange("t h e -> t (h e)"), d["s_k"][PAD:ROWS, :]
                         ).then_inc(stored, 16)
            sp.dma_start(d["new_v_prompt"][0, 0], heads[PAD:ROWS]).then_inc(stored, 16)
            sp.wait_ge(stored, 64)


SCRATCH = {
    "s_gqk": ((ROWS, 2 * QK_W), F32),
    "s_gv": ((ROWS, V_W), F32),
    "s_gr": ((ROWS, V_W), F32),
    "s_la": ((ROWS, QK_W), F32),
    "s_k": ((ROWS, SB_W), F32),
    "s_v": ((SH, ROWS, SD), F32),
    "s_qT": ((SH, SD + 2, ROWS), F32),
    "s_kT": ((SH, SD + 2, ROWS), F32),
    "s_og": ((ROWS, V_W), F32),
    "s_os": ((SH, ROWS, SD), F32),
    "s_h": ((ROWS, D_MODEL), F32),
    "s_xn": ((ROWS, D_MODEL), F32),
    "s_rowtok": ((BLOCKS * P, 1), I32),
    "s_dest": ((P, 2 * TILES), I32),
    "s_gate": ((P, 2 * TILES), F32),
    "s_block_e": ((1, BLOCKS), I32),
    "s_y": ((BLOCKS * P, D_MODEL), F32),
}

INPUTS = ["x_prompt", "x_sample", "cache_sb_k", "cache_sb_v", "state_gla", "page_table", "meta_tokens", "norm_mix_gain",
          "w_in", "gla_w_alpha", "gla_b_alpha", "gla_out_gain", "sb_q_gain", "sb_k_gain", "sb_logit_bias",
          "sb_out_gain", "w_out", "norm_ffn_gain", "router_group", "router_group_b", "router_expert",
          "router_expert_b", "w_gate", "w_up", "w_down"]
OUTPUTS = [("y_prompt", (1, SEQ, D_MODEL)), ("y_sample", (DEC_B, DEC_S, D_MODEL)),
           ("new_k_prompt", (1, 1, SEQ + N_META, SH, SD)), ("new_v_prompt", (1, 1, SEQ + N_META, SH, SD)),
           ("new_gla_prompt", (1, 1, GH, GDK, GDV)), ("new_k_sample", (1, DEC_B, DEC_S, SH, SD)),
           ("new_v_sample", (1, DEC_B, DEC_S, SH, SD)), ("new_gla_sample", (1, DEC_B, GH, GDK, GDV))]


def build(nc, d):
    phase_project(nc, d)
    phase_gla_prompt(nc, d)
    phase_gla_sample(nc, d)
    phase_attend(nc, d)
    phase_attend_sample(nc, d)
    phase_out_route(nc, d)
    phase_cache_rows(nc, d)
    phase_experts(nc, d)
    phase_combine(nc, d)


def kernel(**inputs):
    import numpy as _np
    import concourse.bacc as _bacc
    from concourse import mybir as _mybir
    from concourse.bass_utils import run_bass_kernel_spmd as _run

    nc = _bacc.Bacc("TRN2", target_bir_lowering=False, num_devices=1)
    arrays, d = {}, {}
    for name in INPUTS:
        a = _np.ascontiguousarray(inputs[name])
        arrays[f"in_{name}"] = a
        d[name] = nc.dram_tensor(f"in_{name}", a.shape, _mybir.dt.from_np(a.dtype), kind="ExternalInput").ap()
    for name, shape in OUTPUTS:
        d[name] = nc.dram_tensor(f"out_{name}", shape, F32, kind="ExternalOutput").ap()
    for name, (shape, dt) in SCRATCH.items():
        d[name] = nc.dram_tensor(name, shape, dt, kind="Internal").ap()
    build(nc, d)
    r = _run(nc, [arrays], core_ids=[0])
    return tuple(r.results[0][f"out_{name}"] for name, _ in OUTPUTS)
```

```python
import concourse.bass as bass
from concourse import mybir
from concourse.alu_op_type import AluOpType as ALU
from contextlib import ExitStack

ACT = mybir.ActivationFunctionType
AX = mybir.AxisListType
F32 = mybir.dt.float32
F32R = mybir.dt.float32r
I32 = mybir.dt.int32
U32 = mybir.dt.uint32

P = 128
D_MODEL = 1024
KD = D_MODEL // P
SEQ, N_META = 2048, 16
DEC_B, DEC_S = 8, 4
N_SAMPLE = DEC_B * DEC_S
PAD = P - N_META
TILES = 1 + SEQ // P
ROWS = TILES * P
GH, GDK, GDV = 4, 64, 128
SH, SD = 8, 64
QK_W, V_W, RANK, SB_W = GH * GDK, GH * GDV, 16, SH * SD
D_IN = 2 * QK_W + 2 * V_W + RANK + 3 * SB_W
OFF_GQK, OFF_GV, OFF_GR = 0, 2 * QK_W, 2 * QK_W + V_W
OFF_GA = OFF_GR + V_W
OFF_SQ, OFF_SK, OFF_SV = OFF_GA + RANK, OFF_GA + RANK + SB_W, OFF_GA + RANK + 2 * SB_W
CHUNK = 64
GLA_TAU = 16.0
EPS = 1e-6
CLAMP = 30.0
NEVER = -30000.0
PAST, PAGE = 4096, 128
PAGES = PAST // PAGE
N_GROUPS, PER_GROUP = 4, 8
N_EXP = N_GROUPS * PER_GROUP
D_EXP = 512
N_TOK = SEQ + N_META + N_SAMPLE
BLOCKS = (2 * N_TOK + N_EXP * (P - 1)) // P


class Chain:

    def __init__(self, eng, sem, per_round=0, i=0):
        self.eng, self.sem, self.per, self.i, self.n = eng, sem, per_round, i, 0

    def value(self):
        return self.i * self.per + self.n

    def __call__(self, ins, wait=True):
        self.n += 1
        ins.then_inc(self.sem, 1)
        if wait:
            self.eng.wait_ge(self.sem, self.value())

    def sync(self):
        self.eng.wait_ge(self.sem, self.value())

    def done(self):
        assert self.n == self.per, self.n


class Scope:

    def __init__(self, nc, tag):
        self.nc, self.tag, self.ctx, self.sems = nc, tag, ExitStack(), []

    def __enter__(self):
        self.ctx.__enter__()
        return self

    def __exit__(self, *a):
        self.running.__exit__(*a)
        self.nc.clear_and_free_semaphores(self.sems)
        self.nc.all_engine_barrier()
        return self.ctx.__exit__(*a)

    def sb(self, name, shape, dt=F32):
        return self.ctx.enter_context(self.nc.sbuf_tensor(f"{self.tag}_{name}", shape, dt))

    def ps(self, name, shape):
        return self.ctx.enter_context(self.nc.psum_tensor(f"{self.tag}_{name}", shape, F32))

    def sem(self, name):
        self.sems.append(self.nc.alloc_semaphore(f"{self.tag}_{name}"))
        return self.sems[-1]

    def block(self):
        self.running = self.nc.Block()
        return self.running.__enter__()


def make_identity(nc, pool, ident, done):
    nc.gpsimd.memset(ident[:], 0.0).then_inc(done, 1)
    pool.wait_ge(done, 1)
    nc.gpsimd.affine_select(out=ident[:], in_=ident[:], compare_op=ALU.not_equal, fill=1.0, base=0,
                            pattern=[[-1, P]], channel_multiplier=1).then_inc(done, 1)


def phase_project(nc, d):
    with Scope(nc, "pr") as s:
        w = s.sb("w_in", [P, KD, D_IN])
        w_alpha = s.sb("w_alpha", [RANK, QK_W])
        gain = s.sb("gain", [P, KD])
        q_gain = s.sb("q_gain", [P, SD])
        k_gain = s.sb("k_gain", [P, SD])
        b_alpha = s.sb("b_alpha", [P, QK_W])
        ident = s.sb("ident", [P, P])
        x = s.sb("x", [P, D_MODEL])
        xn = s.sb("xn", [P, D_MODEL])
        sq = s.sb("sq", [P, D_MODEL])
        ssum = s.sb("ssum", [P, 4])
        eps = s.sb("eps", [P, 1])
        xT = s.sb("xT", [P, KD, P])
        gaT = s.sb("gaT", [RANK, P])
        headsq = s.sb("headsq", [P, 2, SB_W])
        headss = s.sb("headss", [P, 2, SH])
        headln = s.sb("headln", [P, 2, SH])
        headrs = s.sb("headrs", [P, 2, SH])
        qk = s.sb("qk", [P, 2, SB_W])
        qkT = s.sb("qkT", [P, 2, 4 * P])
        gqk = s.sb("gqk", [P, 2 * QK_W])
        gv = s.sb("gv", [P, V_W])
        gr = s.sb("gr", [P, V_W])
        sv = s.sb("sv", [P, SB_W])
        t_a = s.sb("t_a", [P, QK_W])
        m_a = s.sb("m_a", [P, QK_W])
        e_a = s.sb("e_a", [P, QK_W])
        l_a = s.sb("l_a", [P, QK_W])
        l2_a = s.sb("l2_a", [P, QK_W])
        la = s.sb("la", [P, QK_W])

        extra = s.sb("extra", [SH, 4, ROWS])
        logit_bias = s.sb("logit_bias", [SH, 1])
        extra_step, bias_loaded, st_extra = s.sem("extra_step"), s.sem("bias_loaded"), s.sem("st_extra")

        ps_x = [s.ps("xT0", [P, 512]), s.ps("xT1", [P, 512])]
        ps_qkT = [s.ps("qT", [P, 512]), s.ps("kT", [P, 512])]
        bank = [s.ps(f"c{n}", [P, 512]) for n in range(4)]

        w_loaded, small_loaded, x_loaded, x0_loaded, x0_zero = (
            s.sem("w_loaded"), s.sem("small_loaded"), s.sem("x_loaded"), s.sem("x0_loaded"), s.sem("x0_zero"))
        ident_ready, eps_ready = s.sem("ident_ready"), s.sem("eps_ready")
        ss_ready, rstd_ready, xn_ready = s.sem("ss_ready"), s.sem("rstd_ready"), s.sem("xn_ready")
        act_step, dve_step = s.sem("act_step"), s.sem("dve_step")
        xT_done, xT_act, xT_dve = s.sem("xT_done"), s.sem("xT_act"), s.sem("xT_dve")
        proj_done = s.sem("proj_done")
        q_used, k_used, gqk_out, gv_out, gr_out, sv_out = (
            s.sem("q_used"), s.sem("k_used"), s.sem("gqk_out"), s.sem("gv_out"), s.sem("gr_out"), s.sem("sv_out"))
        ga_out, hl_step, ea_step = s.sem("ga_out"), s.sem("hl_step"), s.sem("ea_step")
        hs_ready, hsum_ready, hr_ready = s.sem("hs_ready"), s.sem("hsum_ready"), s.sem("hr_ready")
        qk_ready, qkT_done, qT_out, kT_out = s.sem("qk_ready"), s.sem("qkT_done"), s.sem("qT_out"), s.sem("kT_out")
        m_ready, l_ready, la_ready = s.sem("m_ready"), s.sem("l_ready"), s.sem("la_ready")
        st_qkT, st_k, st_gqk, st_gv, st_gr, st_sv, st_la = (s.sem(f"st_{n}") for n in
                                                            ("qkT", "k", "gqk", "gv", "gr", "sv", "la"))
        block = s.block()
        LAST = TILES - 1

        @block.sync
        def _(sp):
            sp.wait_ge(x0_zero, 1)
            sp.dma_start(x[0:N_SAMPLE, :], d["x_sample"].rearrange("b t m -> (b t) m")).then_inc(x0_loaded, 16)
            sp.dma_start(x[PAD:P, :], d["meta_tokens"]).then_inc(x0_loaded, 16)
            w_rows = d["w_in"][0].rearrange("(k p) n -> p k n", p=P)
            for k in range(KD):
                sp.dma_start(w[:, k, :], w_rows[:, k, :]).then_inc(w_loaded, 16)

            def store(i, rows):
                sp.wait_ge(gqk_out, i + 1)
                sp.dma_start(d["s_gqk"][rows, :], gqk[:]).then_inc(st_gqk, 16)
                sp.wait_ge(gv_out, i + 1)
                sp.dma_start(d["s_gv"][rows, :], gv[:]).then_inc(st_gv, 16)
                sp.wait_ge(gr_out, i + 1)
                sp.dma_start(d["s_gr"][rows, :], gr[:]).then_inc(st_gr, 16)
                sp.wait_ge(sv_out, i + 1)
                sp.dma_start(d["s_v"].rearrange("h t e -> t h e")[rows], sv[:].rearrange("p (h e) -> p h e", h=SH)
                             ).then_inc(st_sv, 16)
                sp.wait_ge(qk_ready, 2 * i + 2)
                sp.dma_start(d["s_k"][rows, :], qk[:, 1, :]).then_inc(st_k, 16)
                sp.wait_ge(la_ready, i + 1)
                sp.dma_start(d["s_la"][rows, :], la[:]).then_inc(st_la, 16)

            with sp.Fori(0, LAST) as i:
                rows = bass.ds(sp.snap(i * P), P)
                sp.wait_ge(xn_ready, i + 1)
                sp.dma_start(x[:], d["x_prompt"][0, rows, :]).then_inc(x_loaded, 16)
                store(i, rows)
            store(LAST, slice(LAST * P, ROWS))
            for st, n in ((st_gqk, 1), (st_gv, 1), (st_gr, 1), (st_sv, 1), (st_k, 1), (st_la, 1)):
                sp.wait_ge(st, 16 * n * TILES)

        @block.gpsimd
        def _(pool):
            make_identity(nc, pool, ident, ident_ready)
            nc.gpsimd.memset(extra[:, 0, :], 0.0)
            nc.gpsimd.memset(extra[:, 1:3, :], 1.0)
            nc.gpsimd.memset(extra[:, 3, 0:PAD], NEVER)
            nc.gpsimd.memset(extra[:, 3, PAD:], 0.0).then_inc(extra_step, 1)
            pool.dma_start(logit_bias[:], d["sb_logit_bias"][0].rearrange("(h o) -> h o", o=1)).then_inc(bias_loaded, 16)
            pool.wait_ge(bias_loaded, 16)
            pool.wait_ge(extra_step, 1)
            nc.gpsimd.tensor_scalar(extra[:, 0, :], extra[:, 0, :], logit_bias[:], None, ALU.add).then_inc(extra_step, 1)
            pool.wait_ge(extra_step, 2)
            for n, name in enumerate(("s_qT", "s_kT")):
                pool.dma_start(d[name][:, SD:, :], extra[:, 2 * n:2 * n + 2, :]).then_inc(st_extra, 16)
            pool.wait_ge(st_extra, 32)

        @block.scalar
        def _(act):
            nc.scalar.preload_act_table_set("natural_log_exp_and_others")
            act.dma_start(gain[:], d["norm_mix_gain"][0].rearrange("(k p) -> p k", p=P),
                          allow_slow_non_contiguous=True).then_inc(small_loaded, 16)
            act.dma_start(w_alpha[:], d["gla_w_alpha"][0]).then_inc(small_loaded, 16)
            act.dma_start(b_alpha[:], d["gla_b_alpha"][0].partition_broadcast(P)).then_inc(small_loaded, 16)
            act.dma_start(q_gain[:], d["sb_q_gain"][0].partition_broadcast(P)).then_inc(small_loaded, 16)
            act.dma_start(k_gain[:], d["sb_k_gain"][0].partition_broadcast(P)).then_inc(small_loaded, 16)
            act.wait_ge(eps_ready, 1)

            def norm(t, c):
                c(nc.scalar.activation(sq[:], x[:], ACT.Square, accum_out=ssum[:, 0:1]))
                c(nc.scalar.activation(ssum[:, 1:2], ssum[:, 0:1], ACT.Ln, bias=eps[:], scale=1.0 / D_MODEL))
                nc.scalar.activation(ssum[:, 2:3], ssum[:, 1:2], ACT.Exp, scale=-0.5).then_inc(rstd_ready, 1)

            def transposed(t):
                act.wait_ge(xT_done, t + 1)
                for k in range(0, KD // 2):
                    nc.scalar.activation(xT[:, k, :], ps_x[0][:, k * P:(k + 1) * P], ACT.Copy,
                                         scale=gain[:, k:k + 1]).then_inc(xT_act, 1)

            PER = 2
            act.wait_ge(x0_loaded, 32)
            norm(0, Chain(act, act_step))
            act.wait_ge(small_loaded, 80)
            transposed(0)

            def work(i, last, rows):
                if not last:
                    act.wait_ge(x_loaded, 16 * i + 16)
                    act.wait_ge(xn_ready, i + 1)
                    c = Chain(act, act_step, PER, i)
                    c.n = PER
                    norm(i + 1, c)
                for n in range(2):
                    act.wait_ge(proj_done, 8 * i + n + 1)
                    act.wait_ge(hsum_ready, 2 * i + n)
                    nc.scalar.activation(headsq[:, n, :], bank[n][:], ACT.Square).then_inc(hs_ready, 1)
                for n in range(2):
                    act.wait_ge(hsum_ready, 2 * i + n + 1)
                    nc.scalar.activation(headln[:, n, :], headss[:, n, :], ACT.Ln, bias=eps[:],
                                         scale=1.0 / SD).then_inc(hl_step, 1)
                    act.wait_ge(hl_step, 2 * i + n + 1)
                    nc.scalar.activation(headrs[:, n, :], headln[:, n, :], ACT.Exp, scale=-0.5).then_inc(hr_ready, 1)
                act.wait_ge(proj_done, 8 * i + 4)
                act.wait_ge(st_gv, 16 * i)
                nc.scalar.copy(gv[:], bank[3][:]).then_inc(gv_out, 1)
                act.wait_ge(proj_done, 8 * i + 5)
                nc.scalar.copy(gaT[:], ps_x[0][0:RANK, 0:P]).then_inc(ga_out, 1)
                act.wait_ge(m_ready, i + 1)
                nc.scalar.activation(e_a[:], m_a[:], ACT.Exp).then_inc(ea_step, 1)
                act.wait_ge(ea_step, i + 1)
                nc.scalar.activation(l_a[:], e_a[:], ACT.Ln, bias=1.0).then_inc(l_ready, 1)
                act.wait_ge(proj_done, 8 * i + 6)
                act.wait_ge(st_gr, 16 * i)
                nc.scalar.copy(gr[:], bank[0][:]).then_inc(gr_out, 1)
                act.wait_ge(qkT_done, 2 * i + 1)
                act.wait_ge(st_qkT, 64 * i)
                nc.scalar.copy(qkT[:, 0, :], ps_qkT[0][:]).then_inc(qT_out, 1)
                if not last:
                    transposed(i + 1)
                act.wait_ge(qT_out, i + 1)
                act.wait_ge(kT_out, i + 1)
                for n, name in enumerate(("s_qT", "s_kT")):
                    for a in range(2):
                        act.dma_start(d[name].rearrange("(g a) r t -> a r g t", a=2)[a, 0:SD, :, rows],
                                      qkT[a * SD:(a + 1) * SD, n, :].rearrange("p (g t) -> p g t", g=4)
                                      ).then_inc(st_qkT, 16)

            with act.Fori(0, LAST) as i:
                work(i, False, bass.ds(i * P, P))
            work(LAST, True, slice(LAST * P, ROWS))
            act.wait_ge(st_qkT, 64 * TILES)

        @block.vector
        def _(dve):
            nc.vector.memset(eps[:], EPS).then_inc(eps_ready, 1)
            nc.vector.memset(x[:], 0.0).then_inc(x0_zero, 1)

            def norm(t):
                dve.wait_ge(rstd_ready, t + 1)
                dve.wait_ge(xT_done, t)
                nc.vector.tensor_scalar(xn[:], x[:], ssum[:, 2:3], None, ALU.mult).then_inc(xn_ready, 1)

            def transposed(t):
                dve.wait_ge(xT_done, t + 1)
                for k in range(KD // 2, KD):
                    nc.vector.tensor_scalar(xT[:, k, :], ps_x[1][:, (k - 4) * P:(k - 3) * P],
                                            gain[:, k:k + 1], None, ALU.mult).then_inc(xT_dve, 1)

            dve.wait_ge(x0_loaded, 32)
            norm(0)
            dve.wait_ge(small_loaded, 80)
            transposed(0)
            nc.vector.tensor_scalar(q_gain[:], q_gain[:], float(SD) ** -0.5, None, ALU.mult).then_inc(eps_ready, 1)
            dve.wait_ge(eps_ready, 2)
            PER = 2

            def work(i, last):
                if not last:
                    norm(i + 1)
                c = Chain(dve, dve_step, PER, i)
                for n in range(2):
                    dve.wait_ge(hs_ready, 2 * i + n + 1)
                    dve.wait_ge(hr_ready, 2 * i + n)
                    nc.vector.tensor_reduce(headss[:, n, :], headsq[:, n, :].rearrange("p (h e) -> p h e", h=SH),
                                            AX.X, ALU.add).then_inc(hsum_ready, 1)
                for n, (g, used) in enumerate(((q_gain, q_used), (k_gain, k_used))):
                    dve.wait_ge(hr_ready, 2 * i + n + 1)
                    dve.wait_ge(qkT_done, 2 * i)
                    if n == 1:
                        dve.wait_ge(st_k, 16 * i)
                    out = qk[:, n, :].rearrange("p (h e) -> p h e", h=SH)
                    nc.vector.tensor_tensor(out, bank[n][:].rearrange("p (h e) -> p h e", h=SH),
                                            headrs[:, n, :].unsqueeze(2).to_broadcast([P, SH, SD]),
                                            ALU.mult).then_inc(used, 1)
                    dve.wait_ge(used, i + 1)
                    nc.vector.tensor_tensor(out, out, g[:].unsqueeze(1).to_broadcast([P, SH, SD]),
                                            ALU.mult).then_inc(qk_ready, 1)
                dve.wait_ge(proj_done, 8 * i + 3)
                dve.wait_ge(st_gqk, 16 * i)
                nc.vector.tensor_copy(gqk[:], bank[2][:]).then_inc(gqk_out, 1)
                dve.wait_ge(proj_done, 8 * i + 7)
                dve.wait_ge(la_ready, i)
                c(nc.vector.tensor_tensor(t_a[:], bank[1][:, 0:QK_W], b_alpha[:], ALU.add))
                dve.wait_ge(l_ready, i)
                nc.vector.tensor_scalar(m_a[:], t_a[:], -1.0, CLAMP, ALU.mult, ALU.min).then_inc(m_ready, 1)
                dve.wait_ge(l_ready, i + 1)
                c(nc.vector.scalar_tensor_tensor(l2_a[:], t_a[:], -1.0, l_a[:], ALU.mult, ALU.max))
                dve.wait_ge(st_la, 16 * i)
                nc.vector.tensor_scalar(la[:], l2_a[:], -1.0 / GLA_TAU, None, ALU.mult).then_inc(la_ready, 1)
                dve.wait_ge(proj_done, 8 * i + 8)
                dve.wait_ge(st_sv, 16 * i)
                nc.vector.tensor_copy(sv[:], bank[2][:]).then_inc(sv_out, 1)
                dve.wait_ge(qkT_done, 2 * i + 2)
                dve.wait_ge(st_qkT, 64 * i)
                nc.vector.tensor_copy(qkT[:, 1, :], ps_qkT[1][:]).then_inc(kT_out, 1)
                if not last:
                    transposed(i + 1)
                c.done()

            with dve.Fori(0, LAST) as i:
                work(i, False)
            work(LAST, True)

        @block.tensor
        def _(pe):
            def transpose_x(t):
                pe.wait_ge(xn_ready, t + 1)
                for k in range(KD):
                    last = nc.tensor.transpose(ps_x[k // 4][:, (k % 4) * P:(k % 4 + 1) * P],
                                               xn[:, k * P:(k + 1) * P], ident[:])
                last.then_inc(xT_done, 1)

            def project(out, off, n):
                for k in range(KD):
                    last = nc.tensor.matmul(out, xT[:, k, :], w[:, k, off:off + n], start=k == 0, stop=k == KD - 1)
                last.then_inc(proj_done, 1)

            pe.wait_ge(ident_ready, 2)
            transpose_x(0)
            pe.wait_ge(w_loaded, 16 * KD)
            pe.wait_ge(small_loaded, 80)

            def work(i, last_tile):
                pe.wait_ge(xT_act, 4 * i + 4)
                pe.wait_ge(xT_dve, 4 * i + 4)
                pe.wait_ge(gr_out, i)
                project(bank[0][:], OFF_SQ, SB_W)
                pe.wait_ge(m_ready, i)
                project(bank[1][:], OFF_SK, SB_W)
                pe.wait_ge(sv_out, i)
                project(bank[2][:], OFF_GQK, 2 * QK_W)
                pe.wait_ge(gv_out, i)
                project(bank[3][:], OFF_GV, V_W)
                for k in range(KD):
                    last = nc.tensor.matmul(ps_x[0][0:RANK, 0:P], w[:, k, OFF_GA:OFF_GA + RANK], xT[:, k, :],
                                            start=k == 0, stop=k == KD - 1)
                last.then_inc(proj_done, 1)
                pe.wait_ge(q_used, i + 1)
                project(bank[0][:], OFF_GR, V_W)
                pe.wait_ge(k_used, i + 1)
                pe.wait_ge(ga_out, i + 1)
                nc.tensor.matmul(bank[1][:, 0:QK_W], gaT[:], w_alpha[:], start=True, stop=True).then_inc(proj_done, 1)
                pe.wait_ge(gqk_out, i + 1)
                project(bank[2][:], OFF_SV, SB_W)
                for n, out in enumerate((qT_out, kT_out)):
                    pe.wait_ge(qk_ready, 2 * i + n + 1)
                    pe.wait_ge(out, i)
                    for g in range(4):
                        last = nc.tensor.transpose(ps_qkT[n][:, g * P:(g + 1) * P],
                                                   qk[:, n, g * P:(g + 1) * P], ident[:])
                    last.then_inc(qkT_done, 1)
                if not last_tile:
                    transpose_x(i + 1)

            with pe.Fori(0, LAST) as i:
                work(i, False)
            work(LAST, True)


def phase_gla_prompt(nc, d):
    H2 = P // 2
    with Scope(nc, "gp") as s:
        ident = s.sb("ident", [P, P])
        sums = s.sb("sums", [P, 4, P])
        causal = s.sb("causal", [P, P])
        ones = s.sb("ones", [P, 1])
        la, gqk, gv = s.sb("la", [P, QK_W]), s.sb("gqk", [P, 2 * QK_W]), s.sb("gv", [P, V_W])
        ex = s.sb("ex", [P, 4, QK_W])
        exn = s.sb("exn", [P, QK_W])
        scaled = s.sb("scaled", [P, 4, QK_W])
        ke = s.sb("ke", [P, QK_W])
        tT = s.sb("tT", [P, 4, 2, P])
        sc = s.sb("sc", [P, 2, 2, P])
        decay = s.sb("decay", [P, 2])
        state = s.sb("state", [P, 2, GDV])
        o = s.sb("o", [P, V_W])
        ps_b = [s.ps("b0", [P, 512]), s.ps("b1", [P, 512])]
        ps_t = [s.ps("t0", [P, 512]), s.ps("t1", [P, 512])]
        ps_s = [s.ps("s0", [P, 512]), s.ps("s1", [P, 512])]
        ps_kv = s.ps("kv", [P, 512])
        ps_d = s.ps("d", [P, 512])
        (consts, zeroed, la_loaded, qk_loaded, v_loaded, b_done, ex_ready, qk_ready, t_done, t_act, t_dve, s_done,
         sc_ready, o_done, kv_done, state_ready, o_ready, stored, state_stored) = (s.sem(n) for n in (
             "consts", "zeroed", "la_loaded", "qk_loaded", "v_loaded", "b_done", "ex_ready", "qk_ready", "t_done",
             "t_act", "t_dve", "s_done", "sc_ready", "o_done", "kv_done", "state_ready", "o_ready", "stored",
             "state_stored"))
        block = s.block()
        head = lambda h: (h % 2 * GDK, h % 2 * GDK + GDK, h // 2)

        @block.sync
        def _(sp):
            def load(c, to, rows):
                sp.wait_ge(b_done, c)
                sp.dma_start(la[to, :], d["s_la"][rows, :]).then_inc(la_loaded, 16)
                sp.wait_ge(qk_ready, c * 6)
                sp.dma_start(gqk[to, :], d["s_gqk"][rows, :]).then_inc(qk_loaded, 16)
                sp.wait_ge(kv_done, c)
                sp.dma_start(gv[to, :], d["s_gv"][rows, :]).then_inc(v_loaded, 16)

            sp.wait_ge(zeroed, 3)
            load(0, slice(PAD, P), slice(PAD, P))
            with sp.Fori(1, TILES) as c:
                rows = bass.ds(sp.snap(c * P), P)
                load(c, slice(0, P), rows)
            sp.wait_ge(state_ready, 1 + GH * TILES)
            sp.dma_start(d["new_gla_prompt"][0, 0].rearrange("(g a) k v -> a k g v", a=2)[0],
                         state[0:GDK]).then_inc(state_stored, 16)
            sp.dma_start(d["new_gla_prompt"][0, 0].rearrange("(g a) k v -> a k g v", a=2)[1],
                         state[GDK:]).then_inc(state_stored, 16)
            sp.wait_ge(state_stored, 32)

        def consts_on_pool(pool):
            n = 0

            def step(ins):
                nonlocal n
                n += 1
                ins.then_inc(consts, 1)
                pool.wait_ge(consts, n)

            def select(t, op, base, step_t, mult):
                step(nc.gpsimd.affine_select(out=t, in_=t, compare_op=op, fill=0.0, base=base,
                                             pattern=[[step_t, t.shape[1]]], channel_multiplier=mult))

            step(nc.gpsimd.memset(ident[:], 0.0))
            step(nc.gpsimd.affine_select(out=ident[:], in_=ident[:], compare_op=ALU.not_equal, fill=1.0, base=0,
                                         pattern=[[-1, P]], channel_multiplier=1))
            step(nc.gpsimd.memset(ones[:], 1.0))
            step(nc.gpsimd.memset(sums[:], 1.0))
            step(nc.gpsimd.memset(causal[:], 1.0))
            for t in (sums[:, 0, :], sums[:, 1, :], causal[:]):
                select(t, ALU.is_ge, 0, 1, -1)
            step(nc.gpsimd.tensor_scalar(sums[0:32, 1, :], sums[0:32, 1, :], 1.0, None, ALU.subtract))
            for lo in (32, 64):
                step(nc.gpsimd.tensor_scalar(sums[lo:lo + 32, 1, H2:], sums[lo:lo + 32, 1, H2:], 1.0, None,
                                             ALU.subtract))
            select(sums[:, 2, :], ALU.is_gt, 0, -1, 1)
            select(sums[:, 3, 0:H2], ALU.is_gt, 0, -1, 1)
            select(sums[:, 3, 0:H2], ALU.is_gt, H2, 0, -1)
            select(sums[:, 3, H2:], ALU.is_ge, H2, 1, -1)
            select(sums[:, 3, H2:], ALU.is_ge, -H2, 0, 1)
            return n

        CONSTS = 16

        @block.gpsimd
        def _(pool):
            for n, t in enumerate((la, gqk, gv)):
                nc.gpsimd.memset(t[:], 0.0).then_inc(zeroed, 1)
            assert consts_on_pool(pool) == CONSTS

        @block.scalar
        def _(act):
            nc.scalar.preload_act_table_set("natural_log_exp_and_others")
            def work(c, rows, of):
                act.wait_ge(b_done, c + 1)
                act.wait_ge(qk_ready, c * 6)
                for n in range(2):
                    nc.scalar.activation(ex[:, 2 * n:2 * n + 2, :], ps_b[n][:].rearrange("p (a n) -> p a n", a=2),
                                         ACT.Exp).then_inc(ex_ready, 1)
                nc.scalar.activation(exn[:], ps_b[0][:, QK_W:], ACT.Exp, scale=-1.0).then_inc(ex_ready, 1)
                act.wait_ge(state_ready, c * GH + 1)
                nc.scalar.activation(decay[:], ps_d[:, 0:2], ACT.Exp).then_inc(ex_ready, 1)
                act.wait_ge(t_done, 2 * c + 1)
                act.wait_ge(s_done, c)
                nc.scalar.copy(tT[:, 0:2], ps_t[0][:].rearrange("p (a g t) -> p a g t", a=2, g=2)
                               ).then_inc(t_act, 1)
                act.wait_ge(o_done, c + 1)
                act.wait_ge(stored, c * 16)
                for a in range(2):
                    nc.scalar.copy(o[:].rearrange("p (g a v) -> p a g v", g=2, a=2)[:, a],
                                   ps_s[a][:, 256:].rearrange("p (g v) -> p g v", g=2)).then_inc(o_ready, 1)
                act.wait_ge(o_ready, 2 * c + 2)
                act.dma_start(d["s_og"][rows, :], o[of, :]).then_inc(stored, 16)

            work(0, slice(PAD, P), slice(PAD, P))
            with act.Fori(1, TILES) as c:
                work(c, bass.ds(act.snap(c * P), P), slice(0, P))
            act.wait_ge(stored, 16 * TILES)

        @block.vector
        def _(dve):
            nc.vector.memset(state[:], 0.0).then_inc(state_ready, 1)
            dve.wait_ge(consts, CONSTS)

            def work(c):
                dve.wait_ge(qk_loaded, c * 16 + 16)
                dve.wait_ge(ex_ready, c * 4 + 3)
                dve.wait_ge(t_done, 2 * c)
                dve.wait_ge(kv_done, c)
                q, k = gqk[:, 0:QK_W], gqk[:, QK_W:]
                for out, src, by, rows in ((scaled[:, 0], q, ex[:, 1], slice(0, P)), (scaled[:, 1], k, exn, slice(0, P)),
                                           (scaled[:, 2], q, ex[:, 0], slice(0, P)),
                                           (scaled[:, 3], k, ex[:, 3], slice(0, H2)),
                                           (scaled[:, 3], q, ex[:, 3], slice(H2, P)),
                                           (ke, k, ex[:, 2], slice(0, P))):
                    nc.vector.scalar_tensor_tensor(out[rows, :], src[rows, :], GDK ** -0.5 if src is q else 1.0,
                                                   by[rows, :], ALU.mult, ALU.mult).then_inc(qk_ready, 1)
                dve.wait_ge(t_done, 2 * c + 2)
                dve.wait_ge(o_done, c)
                nc.vector.tensor_copy(tT[:, 2:4], ps_t[1][:].rearrange("p (a g t) -> p a g t", a=2, g=2)
                                      ).then_inc(t_dve, 1)
                dve.wait_ge(s_done, c + 1)
                for a in range(2):
                    nc.vector.scalar_tensor_tensor(sc[:, a], ps_s[a][:, 0:256].rearrange("p (g t) -> p g t", g=2),
                                                   1e37, causal[:].unsqueeze(1).to_broadcast([P, 2, P]), ALU.min,
                                                   ALU.mult).then_inc(sc_ready, 1)
                dve.wait_ge(kv_done, c + 1)
                dve.wait_ge(ex_ready, c * 4 + 4)
                dve.wait_ge(state_ready, c * GH + 1)
                for h in range(GH):
                    lo, hi, g = head(h)
                    nc.vector.scalar_tensor_tensor(state[lo:hi, g, :], state[lo:hi, g, :], decay[lo:hi, g:g + 1],
                                                   ps_kv[lo:hi, h * GDV:(h + 1) * GDV], ALU.mult,
                                                   ALU.add).then_inc(state_ready, 1)

            work(0)
            with dve.Fori(1, TILES) as c:
                work(c)

        @block.tensor
        def _(pe):
            pe.wait_ge(consts, CONSTS)

            def work(c):
                pe.wait_ge(la_loaded, c * 16 + 16)
                pe.wait_ge(ex_ready, c * 4)
                for n in range(4):
                    nc.tensor.matmul(ps_b[n // 2][:, n % 2 * QK_W:(n % 2 + 1) * QK_W], sums[:, n, :], la[:],
                                     start=True, stop=True)
                for g in range(2):
                    last = nc.tensor.matmul(ps_d[:, g:g + 1], la[:, g * P:(g + 1) * P], ones[:], start=True,
                                            stop=True)
                last.then_inc(b_done, 1)
                for n in range(4):
                    pe.wait_ge(qk_ready, c * 6 + (n + 1 if n < 3 else 5))
                    if n % 2 == 0:
                        pe.wait_ge(t_dve if n else t_act, c)
                    for g in range(2):
                        last = nc.tensor.transpose(ps_t[n // 2][:, (n % 2 * 2 + g) * P:(n % 2 * 2 + g + 1) * P],
                                                   scaled[:, n, g * P:(g + 1) * P], ident[:])
                    if n % 2:
                        last.then_inc(t_done, 1)
                pe.wait_ge(v_loaded, c * 16 + 16)
                pe.wait_ge(qk_ready, c * 6 + 6)
                pe.wait_ge(state_ready, c * GH + 1)
                for h in range(GH):
                    last_kv = nc.tensor.matmul(ps_kv[:, h * GDV:(h + 1) * GDV], ke[:, h // 2 * P:(h // 2 + 1) * P],
                                               gv[:, h * GDV:(h + 1) * GDV], start=True, stop=True)
                pe.wait_ge(t_act, c + 1)
                pe.wait_ge(t_dve, c + 1)
                pe.wait_ge(sc_ready, 2 * c)
                for h in range(GH):
                    lo, hi, g = head(h)
                    out = ps_s[h % 2]
                    nc.tensor.matmul(out[:, g * P:(g + 1) * P], tT[lo:hi, 1, g, :], tT[lo:hi, 0, g, :], start=True,
                                     stop=True)
                    last = nc.tensor.matmul(out[0:H2, g * P + H2:(g + 1) * P], tT[lo:hi, 3, g, 0:H2],
                                            tT[lo:hi, 3, g, H2:], start=True, stop=True)
                last.then_inc(s_done, 1)
                pe.wait_ge(sc_ready, 2 * c + 2)
                pe.wait_ge(o_ready, 2 * c)
                for h in range(GH):
                    lo, hi, g = head(h)
                    out = ps_s[h % 2][:, 256 + g * GDV:256 + (g + 1) * GDV]
                    nc.tensor.matmul(out, sc[:, h % 2, g, :], gv[:, h * GDV:(h + 1) * GDV], start=True, stop=False)
                    last = nc.tensor.matmul(out, tT[lo:hi, 2, g, :], state[lo:hi, g, :], start=False, stop=True)
                last.then_inc(o_done, 1)
                pe.wait_ge(o_done, c + 1)
                pe.sem_inc(kv_done, 1)

            work(0)
            with pe.Fori(1, TILES) as c:
                work(c)


def phase_gla_sample(nc, d):
    N, B, T = N_SAMPLE, DEC_B, DEC_S
    with Scope(nc, "gs") as s:
        ident = s.sb("ident", [P, P])
        upto = s.sb("upto", [N, N])
        after = s.sb("after", [N, N])
        member = s.sb("member", [N, B])
        la, gqk, gv = s.sb("la", [N, QK_W]), s.sb("gqk", [N, 2 * QK_W]), s.sb("gv", [N, V_W])
        state = s.sb("state", [GDK, B, GH, GDV])
        eb, en, ee = (s.sb(n, [N, QK_W]) for n in ("eb", "en", "ee"))
        qe, kd, ke = (s.sb(n, [N, QK_W]) for n in ("qe", "kd", "ke"))
        kem = s.sb("kem", [N, B, QK_W])
        tT = s.sb("tT", [GDK, 2, GH, N])
        qeTm = s.sb("qeTm", [GDK, B, GH, N])
        sc = s.sb("sc", [N, GH, N])
        decay = s.sb("decay", [GDK, GH, B])
        o = s.sb("o", [N, V_W])
        zero = s.sb("zero", [PAD - N, V_W])
        ps_b, ps_e, ps_d = s.ps("b", [N, 512]), s.ps("e", [N, 512]), s.ps("d", [GDK, 512])
        ps_t, ps_s, ps_o = s.ps("t", [GDK, 512]), s.ps("s", [N, 512]), s.ps("o_", [N, 512])
        ps_kv = [s.ps("kv0", [GDK, 512]), s.ps("kv1", [GDK, 512])]
        (consts, loaded, b_done, ex_ready, qk_ready, t_done, t_ready, s_done, sc_ready, o_done, kv_done,
         state_ready, o_ready, stored, dve_step, zeroed) = (s.sem(n) for n in (
             "consts", "loaded", "b_done", "ex_ready", "qk_ready", "t_done", "t_ready", "s_done", "sc_ready",
             "o_done", "kv_done", "state_ready", "o_ready", "stored", "dve_step", "zeroed"))
        block = s.block()
        rows = slice(0, N)

        @block.sync
        def _(sp):
            sp.dma_start(la[:], d["s_la"][rows, :]).then_inc(loaded, 16)
            sp.dma_start(gqk[:], d["s_gqk"][rows, :]).then_inc(loaded, 16)
            sp.dma_start(gv[:], d["s_gv"][rows, :]).then_inc(loaded, 16)
            sp.dma_start(state[:], d["state_gla"][0].rearrange("b h k v -> k b h v")).then_inc(loaded, 16)
            sp.wait_ge(zeroed, 1)
            sp.dma_start(d["s_og"][N:PAD, :], zero[:]).then_inc(stored, 16)
            sp.dma_start(d["s_os"].rearrange("h t e -> t h e")[N:PAD], zero[:].rearrange("p (h e) -> p h e", h=SH)).then_inc(stored, 16)
            sp.wait_ge(o_ready, 1)
            sp.dma_start(d["s_og"][rows, :], o[:]).then_inc(stored, 16)
            sp.wait_ge(state_ready, B * GH)
            sp.dma_start(d["new_gla_sample"][0].rearrange("b h k v -> k b h v"), state[:]).then_inc(stored, 16)
            sp.wait_ge(stored, 64)

        @block.gpsimd
        def _(pool):
            nc.gpsimd.memset(zero[:], 0.0).then_inc(zeroed, 1)
            make_identity(nc, pool, ident, consts)
            n = 2

            def step(ins):
                nonlocal n
                n += 1
                ins.then_inc(consts, 1)
                pool.wait_ge(consts, n)

            def select(t, op, base, pattern, mult):
                step(nc.gpsimd.affine_select(out=t, in_=t, compare_op=op, fill=0.0, base=base, pattern=pattern,
                                             channel_multiplier=mult))

            for t in (upto, after):
                step(nc.gpsimd.memset(t[:], 1.0))
                select(t[:], ALU.is_ge, 0, [[-T, B], [0, T]], 1)
                select(t[:], ALU.is_ge, T - 1, [[T, B], [0, T]], -1)
            select(upto[:], ALU.is_ge, 0, [[1, N]], -1)
            select(after[:], ALU.is_gt, 0, [[-1, N]], 1)
            step(nc.gpsimd.memset(member[:], 1.0))
            select(member[:], ALU.is_ge, 0, [[-T, B]], 1)
            select(member[:], ALU.is_ge, T - 1, [[T, B]], -1)

        CONSTS = 13

        @block.scalar
        def _(act):
            nc.scalar.preload_act_table_set("natural_log_exp_and_others")
            act.wait_ge(b_done, 1)
            nc.scalar.activation(eb[:], ps_b[:, 0:QK_W], ACT.Exp).then_inc(ex_ready, 1)
            nc.scalar.activation(en[:], ps_b[:, 0:QK_W], ACT.Exp, scale=-1.0).then_inc(ex_ready, 1)
            nc.scalar.activation(ee[:], ps_e[:, 0:QK_W], ACT.Exp).then_inc(ex_ready, 1)
            nc.scalar.activation(decay[:], ps_d[:, 0:GH * B].rearrange("p (h b) -> p h b", h=GH),
                                 ACT.Exp).then_inc(ex_ready, 1)
            act.wait_ge(o_done, 1)
            nc.scalar.copy(o[:], ps_o[:]).then_inc(o_ready, 1)

        @block.vector
        def _(dve):
            nc.vector.memset(qeTm[:], 0.0).then_inc(dve_step, 1)
            dve.wait_ge(loaded, 64)
            dve.wait_ge(ex_ready, 4)
            dve.wait_ge(consts, CONSTS)
            nc.vector.scalar_tensor_tensor(qe[:], gqk[:, 0:QK_W], GDK ** -0.5, eb[:], ALU.mult,
                                           ALU.mult).then_inc(qk_ready, 1)
            nc.vector.tensor_tensor(kd[:], gqk[:, QK_W:], en[:], ALU.mult).then_inc(qk_ready, 1)
            nc.vector.tensor_tensor(ke[:], gqk[:, QK_W:], ee[:], ALU.mult).then_inc(dve_step, 1)
            dve.wait_ge(dve_step, 2)
            for b in range(B):
                nc.vector.tensor_scalar(kem[:, b, :], ke[:], member[:, b:b + 1], None, ALU.mult).then_inc(qk_ready, 1)
            dve.wait_ge(t_done, 1)
            nc.vector.tensor_copy(tT[:], ps_t[:, 0:2 * GH * N].rearrange("p (a h t) -> p a h t", a=2, h=GH)
                                  ).then_inc(t_ready, 1)
            dve.wait_ge(t_ready, 1)
            for b in range(B):
                nc.vector.tensor_copy(qeTm[:, b, :, b * T:(b + 1) * T], tT[:, 0, :, b * T:(b + 1) * T]
                                      ).then_inc(t_ready, 1)
            dve.wait_ge(s_done, 1)
            nc.vector.tensor_tensor(sc[:], ps_s[:, 0:GH * N].rearrange("p (h t) -> p h t", h=GH),
                                    upto[:].unsqueeze(1).to_broadcast([N, GH, N]), ALU.mult).then_inc(sc_ready, 1)
            dve.wait_ge(o_done, 1)
            for b in range(B):
                dve.wait_ge(kv_done, b + 1)
                for h in range(GH):
                    nc.vector.scalar_tensor_tensor(state[:, b, h, :], state[:, b, h, :], decay[:, h, b:b + 1],
                                                   ps_kv[b % 2][:, h * GDV:(h + 1) * GDV], ALU.mult,
                                                   ALU.add).then_inc(state_ready, 1)

        @block.tensor
        def _(pe):
            pe.wait_ge(consts, CONSTS)
            pe.wait_ge(loaded, 64)
            nc.tensor.matmul(ps_b[:, 0:QK_W], upto[:], la[:], start=True, stop=True)
            nc.tensor.matmul(ps_e[:, 0:QK_W], after[:], la[:], start=True, stop=True)
            for h in range(GH):
                last = nc.tensor.matmul(ps_d[:, h * B:(h + 1) * B], la[:, h * GDK:(h + 1) * GDK], member[:],
                                        start=True, stop=True)
            last.then_inc(b_done, 1)
            pe.wait_ge(qk_ready, 2)
            for n, src in enumerate((qe, kd)):
                for h in range(GH):
                    at = (n * GH + h) * N
                    last = nc.tensor.transpose(ps_t[:, at:at + N], src[:, h * GDK:(h + 1) * GDK], ident[0:N, 0:N])
            last.then_inc(t_done, 1)
            pe.wait_ge(t_ready, 1)
            for h in range(GH):
                last = nc.tensor.matmul(ps_s[:, h * N:(h + 1) * N], tT[:, 1, h, :], tT[:, 0, h, :],
                                        start=True, stop=True)
            last.then_inc(s_done, 1)
            pe.wait_ge(sc_ready, 1)
            pe.wait_ge(t_ready, 1 + B)
            for h in range(GH):
                out = ps_o[:, h * GDV:(h + 1) * GDV]
                nc.tensor.matmul(out, sc[:, h, :], gv[:, h * GDV:(h + 1) * GDV], start=True, stop=False)
                for b in range(B):
                    last = nc.tensor.matmul(out, qeTm[:, b, h, :], state[:, b, h, :], start=False, stop=b == B - 1)
            last.then_inc(o_done, 1)
            pe.wait_ge(qk_ready, 2 + B)
            for b in range(B):
                if b >= 2:
                    pe.wait_ge(state_ready, (b - 1) * GH)
                for h in range(GH):
                    last = nc.tensor.matmul(ps_kv[b % 2][:, h * GDV:(h + 1) * GDV], kem[:, b, h * GDK:(h + 1) * GDK],
                                            gv[:, h * GDV:(h + 1) * GDV], start=True, stop=True)
                last.then_inc(kv_done, 1)


def attention_units():
    units = []
    for g in range((TILES - 1) // 4, -1, -1):
        q0, q1 = max(4 * g - 3, 0), 4 * g
        for j in range(q1, -1, -1):
            units.append((g, j, q0, q1, max(j - q0, 0) * P, j == q1))
    return units


def phase_attend(nc, d):
    units = attention_units()
    NU, NG = len(units), (TILES - 1) // 4 + 1
    R, RA = 5, 3
    assert NU % R == 0 and NU % RA == 0
    KA = SD + 2
    width = [(q1 - q0 + 1) * P for g, j, q0, q1, c0, first in units]
    with Scope(nc, "at") as s:
        neg_tri = s.sb("neg_tri", [P, P])
        neg_ones = s.sb("neg_ones", [P, P])
        ident = s.sb("ident", [P, P])
        never = s.sb("never", [P, P])
        zeros = s.sb("zeros", [P, P])
        kT = s.sb("kT", [KA, ROWS])
        qT = s.sb("qT", [KA, ROWS])
        v = s.sb("v", [P, TILES, SD])
        L = s.sb("L", [P, R, 512])
        acc = s.sb("acc", [P, 3, 512])
        a = s.sb("a", [P, RA, 512])
        o = s.sb("o", [P, 2, 4, SD])
        ps_d = [s.ps(f"d{n}", [P, 512]) for n in range(R)]
        ps_o = [s.ps(f"o{n}", [P, 512]) for n in range(2)]
        (consts, ones_ready, z_done, m_ready, e_step, l_ready, L_ready, acc_ready, d_done, a_ready,
         o_done, o_out, stored) = (s.sem(n) for n in (
             "consts", "ones_ready", "z_done", "m_ready", "e_step", "l_ready", "L_ready", "acc_ready",
             "d_done", "a_ready", "o_done", "o_out", "stored"))
        loaded = [s.sem(f"loaded{g}") for g in range(NG)]
        block = s.block()

        def done(h, n):
            return h * NU + (n + 1 + R)

        def summed(h, n):
            n_sums = NU - NG
            before = sum(units[m][1] > 0 for m in range(n % NU + 1))
            return (h + n // NU) * n_sums + (before + R) if n >= 0 else h * n_sums + (before - n_sums + R)

        ranges = [(max(4 * g - 3, 0), 4 * g) for g in range(NG - 1, -1, -1)]
        last_of = [max(n for n in range(NU) if units[n][0] == NG - 1 - k) for k in range(NG)]

        @block.sync
        def _(sp):
            def load(h, k, skip=0):
                q0, q1 = ranges[k]
                cols = slice(q0 * P, (q1 + 1) * P)
                for t, name, skipped in ((kT, "s_kT", skip), (qT, "s_qT", 0)):
                    use = slice(q0 * P + skipped, (q1 + 1) * P)
                    sp.dma_start(t[:, use], d[name][bass.ds(h, 1), :, use].rearrange("a r t -> (a r) t")
                                 ).then_inc(loaded[k], 16)
                sp.dma_start(v[:, q0:q1 + 1, :], d["s_v"][bass.ds(h, 1), cols].rearrange("a (t p) e -> p (a t) e", p=P)
                             ).then_inc(loaded[k], 16)

            def store(h, k):
                q0, q1 = ranges[k]
                sp.wait_ge(o_out, h * NG + (k + 1))
                if q0:
                    sp.dma_start(d["s_os"][bass.ds(h, 1), q0 * P:(q1 + 1) * P].rearrange("a (t p) e -> p (a t) e", p=P),
                                 o[:, k % 2]).then_inc(stored, 16)
                else:
                    sp.dma_start(d["s_os"][bass.ds(h, 1), PAD:P].rearrange("a p e -> (a p) e"),
                                 o[PAD:P, k % 2, 0, :]).then_inc(stored, 16)

            for k in range(NG):
                load(0, k)
            with sp.Fori(0, SH - 1) as h:
                for k in range(NG):
                    sp.wait_ge(o_done, done(h, last_of[k]))
                    load(h + 1, k, skip=0 if ranges[k][0] else 1)
                    store(h, k)
            for k in range(NG):
                store(SH - 1, k)
            sp.wait_ge(stored, SH * NG * 16)

        @block.gpsimd
        def _(pool):
            nc.gpsimd.memset(neg_ones[:], -1.0).then_inc(ones_ready, 1)
            nc.gpsimd.memset(neg_tri[:], -1.0).then_inc(consts, 1)
            pool.wait_ge(consts, 1)
            nc.gpsimd.affine_select(out=neg_tri[:], in_=neg_tri[:], compare_op=ALU.is_ge, fill=0.0, base=0,
                                    pattern=[[-1, P]], channel_multiplier=1).then_inc(ones_ready, 1)
            nc.gpsimd.memset(never[:], NEVER).then_inc(consts, 1)
            pool.wait_ge(consts, 2)
            nc.gpsimd.affine_select(out=never[:], in_=never[:], compare_op=ALU.is_ge, fill=0.0, base=0,
                                    pattern=[[-1, P]], channel_multiplier=1).then_inc(ones_ready, 1)
            nc.gpsimd.memset(zeros[:], 0.0).then_inc(consts, 1)
            nc.gpsimd.memset(ident[:], 0.0).then_inc(consts, 1)
            pool.wait_ge(consts, 4)
            nc.gpsimd.affine_select(out=ident[:], in_=ident[:], compare_op=ALU.not_equal, fill=1.0, base=0,
                                    pattern=[[-1, P]], channel_multiplier=1).then_inc(ones_ready, 1)
            pool.sem_inc(acc_ready, R)

            def sum_up(h, n):
                g, j, q0, q1, c0, first = units[n]
                W, l, new, old = width[n], L[:, n % R, :], acc[:, n % 3, :], acc[:, (n - 1) % 3, :]
                if j == 0:
                    return
                pool.wait_ge(d_done, done(h, n - 2))
                pool.wait_ge(acc_ready, summed(h, n - 1))
                pool.wait_ge(L_ready, done(h, n) - R)
                lo = c0
                if j >= q0:
                    lo = c0 + P
                    ins = nc.gpsimd.tensor_tensor(new[:, c0:lo], l[:, c0:lo], zeros[:], ALU.add)
                if lo < W:
                    ins = nc.gpsimd.tensor_tensor(new[:, lo:W], l[:, lo:W], old[:, lo:W], ALU.add)
                ins.then_inc(acc_ready, 1)

            with pool.Fori(0, SH) as h:
                for n in range(NU):
                    sum_up(h, n)

        @block.scalar
        def _(act):
            nc.scalar.preload_act_table_set("natural_log_exp_and_others")
            act.sem_inc(a_ready, R)
            act.sem_inc(e_step, R)

            def weight(h, n):
                g, j, q0, q1, c0, first = units[n]
                act.wait_ge(d_done, done(h, n))
                act.wait_ge(o_done, done(h, n - RA))
                nc.scalar.activation(a[:, n % RA, c0:width[n]], ps_d[n % R][:, c0:width[n]],
                                     ACT.Exp).then_inc(a_ready, 1)

            with act.Fori(0, SH) as h:
                for n in range(NU + 2):
                    if n < NU:
                        g, j, q0, q1, c0, first = units[n]
                        l = L[:, n % R, c0:width[n]]
                        act.wait_ge(m_ready, done(h, n) - R)
                        nc.scalar.activation(l, l, ACT.Exp).then_inc(e_step, 1)
                    if n >= 2:
                        weight(h, n - 2)
                    if n < NU:
                        act.wait_ge(e_step, done(h, n))
                        nc.scalar.activation(l, l, ACT.Ln, bias=1.0).then_inc(l_ready, 1)

        @block.vector
        def _(dve):
            def clamp(h, n):
                g, j, q0, q1, c0, first = units[n]
                dve.wait_ge(z_done, done(h, n) - R)
                dve.wait_ge(d_done, done(h, n - R))
                dve.wait_ge(acc_ready, summed(h, n - R))
                nc.vector.tensor_scalar(L[:, n % R, c0:width[n]], ps_d[n % R][:, c0:width[n]], CLAMP, None,
                                        ALU.min).then_inc(m_ready, 1)

            def softplus(h, n):
                g, j, q0, q1, c0, first = units[n]
                dve.wait_ge(l_ready, done(h, n) - R)
                l = L[:, n % R, c0:width[n]]
                nc.vector.tensor_tensor(l, ps_d[n % R][:, c0:width[n]], l, ALU.max).then_inc(L_ready, 1)

            def out(h, k):
                T = ranges[k][1] - ranges[k][0] + 1
                dve.wait_ge(o_done, done(h, last_of[k]))
                dve.wait_ge(stored, (h * NG + k) * 16)
                nc.vector.tensor_copy(o[:, k % 2, 0:T, :], ps_o[k % 2][:, 0:T * SD].rearrange(
                    "p (t e) -> p t e", t=T)).then_inc(o_out, 1)

            with dve.Fori(0, SH) as h:
                clamp(h, 0)
                for n in range(NU):
                    if n + 1 < NU:
                        clamp(h, n + 1)
                    softplus(h, n)
                    for k in range(NG):
                        if last_of[k] + 5 == n:
                            out(h, k)
                for k in range(NG):
                    if last_of[k] + 5 >= NU:
                        out(h, k)

        @block.tensor
        def _(pe):
            pe.sem_inc(d_done, R)
            pe.sem_inc(o_done, R)
            pe.wait_ge(ones_ready, 4)

            def logits(h, n):
                g, j, q0, q1, c0, first = units[n]
                if first:
                    pe.wait_ge(loaded[NG - 1 - g], h * 48 + 48)
                elif j < q0 and j % 4 == 0:
                    pe.wait_ge(loaded[NG - 1 - j // 4], h * 48 + 48)
                pe.wait_ge(a_ready, done(h, n - R))
                last = nc.tensor.matmul(ps_d[n % R][:, c0:width[n]], kT[:, j * P:(j + 1) * P],
                                        qT[:, q0 * P + c0:(q1 + 1) * P], start=True, stop=True)
                if j >= q0:
                    last = nc.tensor.matmul(ps_d[n % R][:, c0:c0 + P], ident[:], never[:], start=False, stop=True,
                                            skip_group_check=True)
                last.then_inc(z_done, 1)

            def exponent(h, n):
                g, j, q0, q1, c0, first = units[n]
                pe.wait_ge(L_ready, done(h, n) - R)
                last = nc.tensor.matmul(ps_d[n % R][:, c0:width[n]], neg_tri[:], L[:, n % R, c0:width[n]],
                                        start=False, stop=True, skip_group_check=True)
                if not first:
                    lo = c0 + P if j >= q0 else c0
                    pe.wait_ge(acc_ready, summed(h, n - 1))
                    last = nc.tensor.matmul(ps_d[n % R][:, lo:width[n]], neg_ones[:], acc[:, (n - 1) % 3, lo:width[n]],
                                            start=False, stop=True, skip_group_check=True)
                last.then_inc(d_done, 1)

            def values(h, n):
                g, j, q0, q1, c0, first = units[n]
                k = NG - 1 - g
                if first:
                    pe.wait_ge(o_out, h * NG + max(k - 1, 0))
                pe.wait_ge(a_ready, done(h, n))
                for t in range(c0 // P, q1 - q0 + 1):
                    last = nc.tensor.matmul(ps_o[k % 2][:, t * SD:(t + 1) * SD], a[:, n % RA, t * P:(t + 1) * P],
                                            v[:, j, :], start=first, stop=j == 0, skip_group_check=True)
                last.then_inc(o_done, 1)

            with pe.Fori(0, SH) as h:
                for n in range(NU + 4):
                    if n < NU:
                        logits(h, n)
                    if 2 <= n < NU + 2:
                        exponent(h, n - 2)
                    if n >= 4:
                        values(h, n - 4)


def phase_attend_sample(nc, d):
    HALVES, J = 2, 4
    T = DEC_S
    HQ = SH * T
    G = SH // 2
    C = PAGES // 4
    PER = 4 * J
    X = C + 1
    with Scope(nc, "as") as s:
        ident = s.sb("ident", [P, P])
        row_i = s.sb("row_i", [P, 4], I32)
        row_f = s.sb("row_f", [P, 4])
        ends = s.sb("ends", [P, 2 * HALVES])
        key_f = s.sb("key_f", [P, P])
        never = s.sb("never", [P, HALVES, P])
        own = s.sb("own", [P, SH])
        sel = s.sb("sel", [P, HALVES, N_SAMPLE])
        bias = s.sb("bias", [P, 1])
        table = s.sb("table", [1, DEC_B * PAGES], I32)
        qT = s.sb("qT", [P, G, N_SAMPLE])
        kT_new = s.sb("kT_new", [P, G, P])
        v_new = s.sb("v_new", [P, SB_W])
        QJ, AJ = G * P + HQ, P + HQ
        q_hi, q_lo = (s.sb(f"q_{n}", [P, HALVES, J * QJ], F32R) for n in ("hi", "lo"))
        kn_hi, kn_lo = (s.sb(f"kn_{n}", [P, G, P], F32R) for n in ("hi", "lo"))
        vn_hi, vn_lo = (s.sb(f"vn_{n}", [P, SB_W], F32R) for n in ("hi", "lo"))
        k_raw = s.sb("k_raw", [P, J, 4, SB_W])
        v_raw = s.sb("v_raw", [P, J, 4, SB_W])
        k_hi, k_lo = (s.sb(f"k_{n}", [P, 2, G, 4, P], F32R) for n in ("hi", "lo"))
        v_hi, v_lo = (s.sb(f"v_{n}", [P, 2, 4, SB_W], F32R) for n in ("hi", "lo"))
        ones = s.sb("ones", [P, 4 * P])
        z_new = s.sb("z_new", [P, P])
        L = s.sb("L", [P, 4 * P])
        run = s.sb("run", [P, 4 * P])
        carry = s.sb("carry", [P, 1])
        a = s.sb("a", [P, 4 * P])
        a_hi, a_lo = (s.sb(f"a_{n}", [P, 4, J * AJ], F32R) for n in ("hi", "lo"))
        o = kT_new[0:N_SAMPLE].rearrange("p g t -> p (g t)")
        ps_kT = [s.ps(f"kT{n}", [P, 512]) for n in range(4)]
        ps_z, ps_a, ps_o, ps_f = (s.ps(n, [P, 512]) for n in ("ps_z", "ps_a", "ps_o", "ps_f"))
        (consts, ones_ready, loaded, table_loaded, step, ready, kT_done, kT_hi, kT_lo, z_used, z_done, zn_ready, m_ready, e_step,
         l_ready, L_ready, run_ready, carry_ready, arg_ready, a_ready, aT_done, aT_hi, aT_lo, vs_hi, vs_lo, v_used,
         o_done, own_ready, f_done, f_ready, stored) = (s.sem(n) for n in (
             "consts", "ones_ready", "loaded", "table_loaded", "step", "ready", "kT_done", "kT_hi", "kT_lo", "z_used", "z_done",
             "zn_ready", "m_ready", "e_step", "l_ready", "L_ready", "run_ready", "carry_ready", "arg_ready",
             "a_ready", "aT_done", "aT_hi", "aT_lo", "vs_hi", "vs_lo", "v_used", "o_done", "own_ready", "f_done",
             "f_ready", "stored"))
        k_loaded = [s.sem(f"k{j}") for j in range(J)]
        v_loaded = [s.sem(f"v{j}") for j in range(J)]
        CONSTS, N_LOADS = 5, 9
        block = s.block()

        def pages_before(H, c):
            return PER * c + PER * C * H

        def own_rows(t, W):
            return t[:, 0:W // P].rearrange("p r (j y) -> p r j y", y=AJ)[:, :, :, 0:HQ]

        def q_cols(t, h2, g):
            at = g * P + (2 * g + h2) * T
            return t[h2 * SD:(h2 + 1) * SD].rearrange("p H (j y) -> p H j y", y=QJ)[:, :, :, at:at + T]

        @block.sync
        def _(sp):
            sp.dma_start(table[:], d["page_table"].rearrange("(o b) n -> o (b n)", o=1)).then_inc(table_loaded, 16)
            sp.wait_ge(table_loaded, 16)
            pages = d["cache_sb_k"].shape[1]
            k_rows = d["cache_sb_k"][0].rearrange("n t h e -> n t (h e)")
            v_rows = d["cache_sb_v"][0].rearrange("n t h e -> n t (h e)")

            def load(H, c, j, rows, buf, slot, sems, free, count):
                first = (J * H + j + 1) * PAGES - 4 - 4 * c
                at = slice(first, first + 4) if isinstance(first, int) else bass.ds(sp.snap(first), 4)
                _, ids = nc.values_load_multi_w_load_instructions(
                    table[0:1, at], engines=[mybir.EngineType.SP], min_val=0, max_val=pages - 1)
                if count is not None:
                    sp.wait_ge(free, count)
                for r in range(4):
                    sp.dma_start(buf[:, slot, r, :], rows[bass.ds(ids[r], 1)].rearrange("a t n -> (a t) n")
                                 ).then_inc(sems[j], 16)

            def keys(H, c, j, wait=True):
                load(H, c, j, k_rows, k_raw, j, k_loaded, kT_done,
                     pages_before(H, c) + (4 * j + 4 - PER) if wait else None)

            def values(H, c, j, wait=True):
                load(H, c, j, v_rows, v_raw, j, v_loaded, vs_lo,
                     J * c + (J * C * H + j + 1 - J) if wait else None)

            for H in range(HALVES):
                for j in range(2):
                    keys(H, 0, j, wait=H > 0)
                if H:
                    for j in range(J):
                        values(H - 1, C - 1, j)
                for j in range(2, J):
                    keys(H, 0, j, wait=H > 0)
                for j in range(J):
                    keys(H, 1, j)
                    values(H, 0, j, wait=H > 0)
                with sp.Fori(2, C) as c:
                    for j in range(J):
                        keys(H, c, j)
                        values(H, c - 1, j)
            for j in range(J):
                values(HALVES - 1, C - 1, j)
            sp.wait_ge(f_ready, 1)
            sp.dma_start(d["s_os"].rearrange("h t e -> t h e")[0:N_SAMPLE], o.rearrange("p (h e) -> p h e", h=SH)
                         ).then_inc(stored, 16)
            sp.wait_ge(stored, 16)

        @block.gpsimd
        def _(pool):
            make_identity(nc, pool, ident, consts)
            nc.gpsimd.iota(row_i[:], pattern=[[0, 4]], base=0, channel_multiplier=1).then_inc(consts, 1)
            nc.gpsimd.iota(key_f[:], pattern=[[1, P]], base=0, channel_multiplier=0,
                           allow_small_or_imprecise_dtypes=True).then_inc(consts, 1)
            nc.gpsimd.memset(ones[:], 1.0).then_inc(consts, 1)

            def lo_part(H, c, j):
                pool.wait_ge(vs_hi, J * c + (J * C * H + j + 1))
                u = j % 2
                nc.gpsimd.tensor_tensor(v_lo[:, u], v_raw[:, j], v_hi[:, u].bitcast(F32), ALU.subtract
                                        ).then_inc(vs_lo, 1)

            for H in range(HALVES):
                with pool.Fori(0, C) as c:
                    for j in range(J):
                        lo_part(H, c, j)

        @block.scalar
        def _(act):
            nc.scalar.preload_act_table_set("natural_log_exp_and_others")
            for h2 in range(2):
                lo, hi = h2 * SD, (h2 + 1) * SD
                act.dma_start(qT[lo:hi], d["s_qT"].rearrange("(g a) r t -> a r g t", a=2)[h2, 0:SD, :, 0:N_SAMPLE]
                              ).then_inc(loaded, 16)
                act.dma_start(kT_new[lo:hi], d["s_kT"].rearrange("(g a) r t -> a r g t", a=2)[h2, 0:SD, :, 0:P]
                              ).then_inc(loaded, 16)
            act.dma_start(v_new[:].rearrange("p (h e) -> p h e", h=SH), d["s_v"].rearrange("h t e -> t h e")[0:P]
                          ).then_inc(loaded, 16)
            for j in range(J):
                act.dma_start(bias[j * HQ:(j + 1) * HQ, :], d["sb_logit_bias"][0].unsqueeze(1).to_broadcast([SH, T])
                              ).then_inc(loaded, 16)

            def evac(H, c, j, r):
                g = 4 * j + r
                if r % 2 == 0:
                    act.wait_ge(kT_done, pages_before(H, c) + (g + 2))
                if r == 0:
                    act.wait_ge(z_used, J * c + (J * C * H + j + 1))
                nc.scalar.copy(k_hi[:, j % 2, :, r, :], ps_kT[r][:].rearrange("p (g t) -> p g t", g=G)
                               ).then_inc(kT_hi, 1)

            def v_part(H, c, j):
                act.wait_ge(v_loaded[j], 64 * c + (64 * C * H + 64))
                act.wait_ge(v_used, J * c + (J * C * H + j + 1))
                nc.scalar.copy(v_hi[:, j % 2], v_raw[:, j]).then_inc(vs_hi, 1)

            def chunk(H, c, more=True):
                new = isinstance(c, int) and c == 0
                W = P if new else 4 * P
                x1 = c + (X * H + 1)
                if not new:
                    v_part(H, c - 1, 0)
                if more:
                    for r in range(4):
                        evac(H, c, 0, r)
                act.wait_ge(m_ready, x1)
                nc.scalar.activation(L[:, 0:W], L[:, 0:W], ACT.Exp).then_inc(e_step, 1)
                act.wait_ge(e_step, x1)
                nc.scalar.activation(L[:, 0:W], L[:, 0:W], ACT.Ln, bias=1.0).then_inc(l_ready, 1)
                if more:
                    evac(H, c, 1, 0)
                    evac(H, c, 1, 1)
                act.wait_ge(arg_ready, x1)
                nc.scalar.activation(a[:, 0:W], a[:, 0:W], ACT.Exp).then_inc(a_ready, 1)
                if more:
                    evac(H, c, 1, 2)
                    evac(H, c, 1, 3)
                if not new:
                    v_part(H, c - 1, 1)
                act.wait_ge(aT_done, x1)
                nc.scalar.copy(own_rows(a_hi, W), ps_a[:, 0:W].rearrange("p (r j x) -> p r j x", j=J, x=HQ)
                               ).then_inc(aT_hi, 1)
                if more:
                    for r in range(4):
                        evac(H, c, 2, r)
                if not new:
                    v_part(H, c - 1, 2)
                    v_part(H, c - 1, 3)
                if more:
                    for r in range(4):
                        evac(H, c, 3, r)

            for H in range(HALVES):
                chunk(H, 0)
                with act.Fori(1, C) as c:
                    chunk(H, c)
                chunk(H, C, more=False)
            act.wait_ge(f_done, 1)
            nc.scalar.copy(o, ps_f[0:N_SAMPLE, :]).then_inc(f_ready, 1)

        @block.vector
        def _(dve):
            c = Chain(dve, step)
            for z in (q_hi, q_lo, a_hi, a_lo):
                c(nc.vector.memset(z[:].bitcast(F32), 0.0), wait=False)
            dve.wait_ge(loaded, 16 * N_LOADS)
            dve.wait_ge(consts, CONSTS)
            c.sync()
            whole = [(kn_hi[:], kn_lo[:], kT_new[:]), (vn_hi[:], vn_lo[:], v_new[:])]
            whole += [(q_cols(q_hi, h2, g), q_cols(q_lo, h2, g),
                       qT[h2 * SD:(h2 + 1) * SD, g, :].rearrange("p (H j t) -> p H j t", H=HALVES, j=J))
                      for h2 in range(2) for g in range(G)]
            for hi, lo, x in whole:
                c(nc.vector.tensor_copy(hi, x), wait=False)
            c.sync()
            for hi, lo, x in whole:
                c(nc.vector.tensor_tensor(lo, x, hi.bitcast(F32), ALU.subtract), wait=False)
            c(nc.vector.tensor_scalar(row_i[:, 0:1], row_i[:, 0:1], 5, None, ALU.logical_shift_right), wait=False)
            c(nc.vector.tensor_scalar(row_i[:, 1:2], row_i[:, 1:2], T - 1, None, ALU.bitwise_and), wait=False)
            c(nc.vector.tensor_scalar(row_i[:, 2:3], row_i[:, 2:3], 2, SH - 1, ALU.logical_shift_right, ALU.bitwise_and))
            c(nc.vector.tensor_copy(row_f[:], row_i[:]))
            for H in range(HALVES):
                first, tok = ends[:, 2 * H:2 * H + 1], ends[:, 2 * H + 1:2 * H + 2]
                c(nc.vector.tensor_scalar(first, row_f[:, 0:1], float(T), float(J * T * H), ALU.mult, ALU.add))
                c(nc.vector.tensor_tensor(tok, first, row_f[:, 1:2], ALU.add))
                c(nc.vector.tensor_scalar(never[:, H], key_f[:], first, None, ALU.is_ge))
                c(nc.vector.scalar_tensor_tensor(never[:, H], key_f[:], tok, never[:, H], ALU.is_lt, ALU.mult))
                c(nc.vector.tensor_scalar(never[:, H], never[:, H], -NEVER, NEVER, ALU.mult, ALU.add))
                c(nc.vector.tensor_scalar(sel[:, H], key_f[:, 0:N_SAMPLE], tok, None, ALU.is_equal))
            c(nc.vector.tensor_scalar(own[:], key_f[:, 0:SH], row_f[:, 2:3], None, ALU.is_equal))
            dve.sem_inc(ready, 1)

            def evac(H, c, j, r):
                dve.wait_ge(kT_hi, pages_before(H, c) + (4 * j + r + 1))
                nc.vector.tensor_tensor(k_lo[:, j % 2, :, r, :], ps_kT[r][:].rearrange("p (g t) -> p g t", g=G),
                                        k_hi[:, j % 2, :, r, :].bitcast(F32), ALU.subtract).then_inc(kT_lo, 1)

            def chunk(H, c, more=True):
                new = isinstance(c, int) and c == 0
                W = P if new else 4 * P
                x1 = c + (X * H + 1)
                src = z_new[:] if new else ps_z[:]
                if more:
                    for r in range(4):
                        evac(H, c, 0, r)
                dve.wait_ge(z_done, x1)
                if new:
                    nc.vector.tensor_tensor(z_new[:], ps_z[:, 0:P], never[:, H], ALU.add).then_inc(zn_ready, 1)
                    dve.wait_ge(zn_ready, H + 1)
                nc.vector.tensor_scalar(L[:, 0:W], src, bias[:], CLAMP, ALU.add, ALU.min).then_inc(m_ready, 1)
                dve.wait_ge(l_ready, x1)
                nc.vector.scalar_tensor_tensor(L[:, 0:W], src, bias[:], L[:, 0:W], ALU.add, ALU.max
                                               ).then_inc(L_ready, 1)
                dve.wait_ge(L_ready, x1)
                if not new:
                    dve.wait_ge(carry_ready, x1 - 1)
                nc.vector.tensor_tensor_scan(run[:, 0:W][:, ::-1], ones[:, 0:W], L[:, 0:W][:, ::-1],
                                             0.0 if new else carry[:], ALU.mult, ALU.add).then_inc(run_ready, 1)
                dve.wait_ge(run_ready, x1)
                nc.vector.tensor_copy(carry[:], run[:, 0:1]).then_inc(carry_ready, 1)
                if not (new and H == 0):
                    dve.wait_ge(aT_done, x1 - 1)
                nc.vector.scalar_tensor_tensor(a[:, 0:W], src, bias[:], run[:, 0:W], ALU.add, ALU.subtract
                                               ).then_inc(arg_ready, 1)
                if more:
                    for r in range(4):
                        evac(H, c, 1, r)
                dve.wait_ge(aT_hi, x1)
                nc.vector.tensor_tensor(own_rows(a_lo, W), ps_a[:, 0:W].rearrange("p (r j x) -> p r j x", j=J, x=HQ),
                                        own_rows(a_hi, W).bitcast(F32), ALU.subtract).then_inc(aT_lo, 1)
                if more:
                    for j in (2, 3):
                        for r in range(4):
                            evac(H, c, j, r)

            for H in range(HALVES):
                chunk(H, 0)
                with dve.Fori(1, C) as c:
                    chunk(H, c)
                chunk(H, C, more=False)
                dve.wait_ge(o_done, H + 1)
                nc.vector.tensor_tensor(v_new[:].rearrange("p (h e) -> p h e", h=SH),
                                        ps_o[:].rearrange("p (h e) -> p h e", h=SH),
                                        own[:].unsqueeze(2).to_broadcast([P, SH, SD]), ALU.mult).then_inc(own_ready, 1)

        @block.tensor
        def _(pe):
            pe.sem_inc(z_used, 2)
            pe.sem_inc(v_used, 2)
            pe.wait_ge(consts, CONSTS)
            pe.wait_ge(ready, 1)

            def keys_T(H, c, j):
                pe.wait_ge(k_loaded[j], 64 * c + (64 * C * H + 64))
                for r in range(4):
                    if r % 2 == 0 and not (isinstance(c, int) and c == 0 and H == 0 and j == 0):
                        pe.wait_ge(kT_lo, pages_before(H, c) + (4 * j + r + 2 - 4))
                    for g in range(G):
                        last = nc.tensor.transpose(ps_kT[r][:, g * P:(g + 1) * P],
                                                   k_raw[:, j, r, g * P:(g + 1) * P], ident[:])
                    last.then_inc(kT_done, 1)

            def q_of(t, H, j, g):
                return t[:, H, j * G * P + g * P:j * G * P + (g + 1) * P]

            def a_of(t, r, j):
                return t[:, r, j * P:(j + 1) * P]

            def product(out, l_hi, l_lo, r_hi, r_lo, start, stop):
                nc.tensor.matmul(out, l_hi, r_hi, start=start, stop=False, skip_group_check=True)
                nc.tensor.matmul(out, l_hi, r_lo, start=False, stop=False, skip_group_check=True)
                return nc.tensor.matmul(out, l_lo, r_hi, start=False, stop=stop, skip_group_check=True)

            def logits(H, c, j):
                pe.wait_ge(kT_lo, pages_before(H, c) + (4 * j + 4))
                if j == 0:
                    pe.wait_ge(arg_ready, c + (X * H + 1))
                u = j % 2
                for g in range(G):
                    last = product(ps_z[:], q_of(q_hi, H, j, g), q_of(q_lo, H, j, g),
                                   k_hi[:, u, g].rearrange("p r t -> p (r t)"),
                                   k_lo[:, u, g].rearrange("p r t -> p (r t)"), g == j == 0, g == j == 3)
                last.then_inc(z_used, 1)

            def last_logits(H, c):
                logits(H, c, J - 1)
                pe.wait_ge(z_used, J * c + (J * C * H + J + 2))
                pe.sem_inc(z_done, 1)

            def new_logits(H):
                if H:
                    pe.wait_ge(arg_ready, X * H)
                for j in range(J):
                    for g in range(G):
                        last = product(ps_z[:, 0:P], q_of(q_hi, H, j, g), q_of(q_lo, H, j, g), kn_hi[:, g],
                                       kn_lo[:, g], g == j == 0, g == j == 3)
                last.then_inc(z_done, 1)

            def weights_T(H, c, n):
                x1 = c + (X * H + 1)
                pe.wait_ge(a_ready, x1)
                if not (isinstance(c, int) and c == 0 and H == 0):
                    pe.wait_ge(aT_lo, x1 - 1)
                for r in range(n):
                    last = nc.tensor.transpose(ps_a[:, r * P:(r + 1) * P], a[:, r * P:(r + 1) * P], ident[:])
                last.then_inc(aT_done, 1)

            def values(H, c, j):
                if j == 0:
                    pe.wait_ge(aT_lo, c + (X * H + 1))
                if isinstance(c, int) and c == 0:
                    product(ps_o[:], a_of(a_hi, 0, j), a_of(a_lo, 0, j), vn_hi[:], vn_lo[:], j == 0, False)
                    return
                pe.wait_ge(vs_lo, J * c + (J * C * H + j + 1 - J))
                for r in range(4):
                    last = product(ps_o[:], a_of(a_hi, r, j), a_of(a_lo, r, j), v_hi[:, j % 2, r],
                                   v_lo[:, j % 2, r], False, j == r == 3)
                last.then_inc(v_used, 1)

            def chunk(H, c):
                new = isinstance(c, int) and c == 0
                keys_T(H, c, 0)
                if new:
                    new_logits(H)
                else:
                    last_logits(H, c - 1)
                keys_T(H, c, 1)
                logits(H, c, 0)
                weights_T(H, c, 1 if new else 4)
                keys_T(H, c, 2)
                logits(H, c, 1)
                values(H, c, 0)
                values(H, c, 1)
                keys_T(H, c, 3)
                logits(H, c, 2)
                values(H, c, 2)
                values(H, c, 3)

            for H in range(HALVES):
                if H:
                    pe.wait_ge(own_ready, H)
                    pe.wait_ge(a_ready, X * H)
                chunk(H, 0)
                with pe.Fori(1, C) as c:
                    chunk(H, c)
                last_logits(H, C - 1)
                weights_T(H, C, 4)
                for j in range(J):
                    values(H, C, j)
                pe.wait_ge(v_used, J * C * (H + 1) + 2)
                pe.sem_inc(o_done, 1)
                pe.wait_ge(own_ready, H + 1)
                last = nc.tensor.matmul(ps_f[0:N_SAMPLE, :], sel[:, H], v_new[:], start=H == 0, stop=H == HALVES - 1)
            last.then_inc(f_done, 1)


def phase_out_route(nc, d):
    LAST = TILES - 1
    NR = N_GROUPS + N_EXP
    SMALL = 16 * 11
    CONSTS, ROUTE, PLACE_STEPS = 14, 15, 30
    with Scope(nc, "or") as s:
        ident = s.sb("ident", [P, P])
        w_out = s.sb("w_out", [P, KD, D_MODEL])
        w_r = s.sb("w_r", [P, KD, NR])
        b_r = s.sb("b_r", [P, NR])
        gains = s.sb("gains", [P, 2])
        f_gain = s.sb("f_gain", [P, D_MODEL])
        eps = s.sb("eps", [P, 1])
        og, os_, gr = s.sb("og", [P, V_W]), s.sb("os", [P, SB_W]), s.sb("gr", [P, V_W])
        x = s.sb("x", [P, D_MODEL])
        sq = s.sb("sq", [P, 2, 512])
        ss, ln, rs = (s.sb(n, [P, GH + SH]) for n in ("ss", "ln", "rs"))
        sil = s.sb("sil", [P, V_W])
        cat = s.sb("cat", [P, D_MODEL])
        catT = s.sb("catT", [P, KD, P])
        h = s.sb("h", [P, D_MODEL])
        hsq = s.sb("hsq", [P, D_MODEL])
        hs = s.sb("hs", [P, 4])
        hn = s.sb("hn", [P, D_MODEL])
        hnT = s.sb("hnT", [P, KD, P])
        before = s.sb("before", [P, P])
        ones = s.sb("ones", [P, P])
        iota_e = s.sb("iota_e", [P, N_EXP])
        iota_ei = s.sb("iota_ei", [P, N_EXP], I32)
        valid = s.sb("valid", [P, TILES])
        g8 = s.sb("g8", [P, 8])
        le = s.sb("le", [P, N_GROUPS, PER_GROUP])
        gm8, m8 = s.sb("gm8", [P, 8]), s.sb("m8", [P, 8])
        gi8, i8 = s.sb("gi8", [P, 8], U32), s.sb("i8", [P, 8], U32)
        gf = s.sb("gf", [P, 2])
        own = s.sb("own", [P, N_GROUPS])
        tmp8 = s.sb("tmp8", [P, PER_GROUP, N_GROUPS])
        l8 = s.sb("l8", [P, PER_GROUP])
        ef = s.sb("ef", [P, 2])
        e2 = s.sb("e2", [P, 2])
        E = s.sb("E", [P, 2, N_EXP])
        total = s.sb("total", [P, N_EXP])
        all_E = s.sb("all_E", [P, 2, TILES, N_EXP])
        all_pos = s.sb("all_pos", [P, TILES, N_EXP])
        all_g = s.sb("all_g", [P, TILES, N_GROUPS])
        all_m = s.sb("all_m", [P, TILES, 2])

        ps_t = [s.ps("t0", [P, 512]), s.ps("t1", [P, 512])]
        ps_h = [s.ps("h0", [P, 512]), s.ps("h1", [P, 512])]
        ps_n = [s.ps("n0", [P, 512]), s.ps("n1", [P, 512])]
        ps_r = s.ps("r", [P, 512])
        ps_p = s.ps("p", [P, 512])
        (consts, small, og_loaded, os_loaded, gr_loaded, x_loaded, x0_zero, sq_ready, ss_ready, ln_step,
         rs_ready, min_ready, ex_ready, sil_step, sil_ready, cat_step, cat_ready, cT_done, cT_act, cT_dve, o_done, h_ready,
         hss_step, hrs_ready, w_scaled, hn_ready, st_h, st_n, nT_done, nT_act, nT_dve, r_done, dve_step, E_ready,
         p_done, route_done) = (s.sem(n) for n in (
             "consts", "small", "og_loaded", "os_loaded", "gr_loaded", "x_loaded", "x0_zero", "sq_ready",
             "ss_ready", "ln_step", "rs_ready", "min_ready", "ex_ready", "sil_step", "sil_ready", "cat_step", "cat_ready",
             "cT_done", "cT_act", "cT_dve", "o_done", "h_ready", "hss_step", "hrs_ready", "w_scaled", "hn_ready",
             "st_h", "st_n", "nT_done", "nT_act", "nT_dve", "r_done", "dve_step", "E_ready", "p_done", "route_done"))
        w_loaded = [s.sem(f"w{k}") for k in range(KD)]
        cnt_i = s.sb("cnt_i", [P, N_EXP], I32)
        blk_i = s.sb("blk_i", [P, N_EXP], I32)
        blk = s.sb("blk", [P, N_EXP])
        ends = s.sb("ends", [P, N_EXP])
        start = s.sb("start", [P, N_EXP])
        one_row = s.sb("one_row", [P, N_EXP])
        picked = s.sb("picked", [P, TILES, N_EXP])
        dest = s.sb("dest", [P, 2, TILES])
        dest_u = s.sb("dest_u", [P, 2, TILES], I32)
        skip = s.sb("skip", [P, TILES])
        to = s.sb("to", [P, 2, TILES])
        to_u = s.sb("to_u", [P, 2, TILES], I32)
        token = s.sb("token", [P, TILES], I32)
        zero_i = s.sb("zero_i", [P, BLOCKS + 1], I32)
        lane = s.sb("lane", [P, 2, TILES], I32)
        blk_of = s.sb("blk_of", [P, 2, TILES], I32)
        number = s.sb("number", [1, BLOCKS, N_EXP])
        le_b = s.sb("le_b", [1, BLOCKS, N_EXP])
        block_e = s.sb("block_e", [1, BLOCKS])
        turns_i = s.sb("turns_i", [1, 1], I32)
        block_i = s.sb("block_i", [1, BLOCKS + 1], I32)
        eg = s.sb("eg", [P, TILES, N_GROUPS])
        gsum = s.sb("gsum", [P, TILES])
        em = s.sb("em", [P, TILES, 2])
        msum = s.sb("msum", [P, TILES])
        prod = s.sb("prod", [P, TILES])
        gate = s.sb("gate", [P, TILES])
        gates = s.sb("gates", [P, 2, TILES])
        (pos_ready, total_step, place_step, c_done, to_ready, soft_ready, stored, rows_zero, scattered) = (s.sem(n) for n in (
            "pos_ready", "total_step", "place_step", "c_done", "to_ready", "soft_ready", "stored", "rows_zero", "scattered"))
        block = s.block()

        @block.sync
        def _(sp):
            def load(t, rows, x_rows):
                sp.wait_ge(cat_ready, 3 * t)
                sp.dma_start(og[:], d["s_og"][rows, :]).then_inc(og_loaded, 16)
                sp.dma_start(os_[:].rearrange("p (h e) -> p h e", h=SH), d["s_os"].rearrange("h t e -> t h e")[rows]
                             ).then_inc(os_loaded, 16)
                sp.dma_start(gr[:], d["s_gr"][rows, :]).then_inc(gr_loaded, 16)
                sp.wait_ge(h_ready, 2 * t)
                if x_rows is not None:
                    sp.dma_start(x[:], d["x_prompt"][0, x_rows, :]).then_inc(x_loaded, 16)
                else:
                    sp.wait_ge(x0_zero, 1)
                    sp.dma_start(x[0:N_SAMPLE, :], d["x_sample"].rearrange("b t m -> (b t) m")).then_inc(x_loaded, 16)
                    sp.dma_start(x[PAD:P, :], d["meta_tokens"]).then_inc(x_loaded, 16)

            load(0, slice(0, P), None)
            w_rows = d["w_out"][0].rearrange("(k p) n -> p k n", p=P)
            for k in range(KD):
                sp.dma_start(w_out[:, k, :], w_rows[:, k, :]).then_inc(w_loaded[k], 16)
            with sp.Fori(1, TILES) as t:
                rows, x_rows = bass.ds(sp.snap(t * P), P), bass.ds(sp.snap(t * P - P), P)
                load(t, rows, x_rows)

        @block.gpsimd
        def _(pool):
            n = 0

            def step(ins):
                nonlocal n
                n += 1
                ins.then_inc(consts, 1)
                pool.wait_ge(consts, n)

            step(nc.gpsimd.memset(ident[:], 0.0))
            step(nc.gpsimd.affine_select(out=ident[:], in_=ident[:], compare_op=ALU.not_equal, fill=1.0, base=0,
                                         pattern=[[-1, P]], channel_multiplier=1))
            step(nc.gpsimd.memset(ones[:], 1.0))
            step(nc.gpsimd.memset(one_row[:], 1.0))
            step(nc.gpsimd.memset(before[:], 1.0))
            step(nc.gpsimd.affine_select(out=before[:], in_=before[:], compare_op=ALU.is_gt, fill=0.0, base=0,
                                         pattern=[[1, P]], channel_multiplier=-1))
            step(nc.gpsimd.iota(iota_ei[:], pattern=[[1, N_EXP]], base=0, channel_multiplier=0))
            step(nc.gpsimd.tensor_copy(iota_e[:], iota_ei[:]))
            step(nc.gpsimd.memset(valid[:], 1.0))
            step(nc.gpsimd.affine_select(out=valid[:, 0:1], in_=valid[:, 0:1], compare_op=ALU.is_ge, fill=0.0,
                                         base=-PAD, pattern=[[0, 1]], channel_multiplier=1))
            step(nc.gpsimd.memset(valid[0:N_SAMPLE, 0:1], 1.0))
            step(nc.gpsimd.iota(token[:], pattern=[[P, TILES]], base=0, channel_multiplier=1))
            step(nc.gpsimd.memset(zero_i[:], 0))
            step(nc.gpsimd.iota(number[:], pattern=[[1, BLOCKS], [0, N_EXP]], base=0, channel_multiplier=0,
                                allow_small_or_imprecise_dtypes=True))
            assert n == CONSTS
            pool.dma_start(d["s_rowtok"].rearrange("(p b) o -> p (b o)", p=P), zero_i[:]).then_inc(rows_zero, 16)
            pool.wait_ge(rows_zero, 16)
            pool.wait_ge(to_ready, 1)
            for k in range(2):
                for t in range(TILES):
                    pool.indirect_dma_start(
                        out=d["s_rowtok"], out_offset=bass.IndirectOffsetOnAxis(ap=to_u[:, k, t:t + 1], axis=0),
                        in_=token[:, t:t + 1], in_offset=None, bounds_check=(BLOCKS + 1) * P - 1,
                        oob_is_err=False).then_inc(scattered, 16)
            pool.wait_ge(scattered, 16 * 2 * TILES)

        @block.scalar
        def _(act):
            nc.scalar.preload_act_table_set("natural_log_exp_and_others")
            act.dma_start(w_r[:, :, 0:N_GROUPS], d["router_group"][0].rearrange("(k p) n -> p k n", p=P)).then_inc(small, 16)
            for g in range(N_GROUPS):
                lo = N_GROUPS + g * PER_GROUP
                act.dma_start(w_r[:, :, lo:lo + PER_GROUP], d["router_expert"][0, g].rearrange("(k p) n -> p k n", p=P)
                              ).then_inc(small, 16)
            act.dma_start(b_r[:, 0:N_GROUPS], d["router_group_b"][0].partition_broadcast(P)).then_inc(small, 16)
            act.dma_start(b_r[:, N_GROUPS:], d["router_expert_b"][0].rearrange("g e -> (g e)").partition_broadcast(P)
                          ).then_inc(small, 16)
            act.dma_start(gains[:, 0:1], d["gla_out_gain"].rearrange("o e -> e o")).then_inc(small, 16)
            for n in range(P // SD):
                act.dma_start(gains[n * SD:(n + 1) * SD, 1:2], d["sb_out_gain"].rearrange("o e -> e o")
                              ).then_inc(small, 16)
            act.dma_start(f_gain[:], d["norm_ffn_gain"][0].partition_broadcast(P)).then_inc(small, 16)
            act.wait_ge(consts, CONSTS)
            act.wait_ge(x0_zero, 2)

            def heads(t):
                act.wait_ge(og_loaded, 16 * t + 16)
                act.wait_ge(ss_ready, 2 * t)
                nc.scalar.activation(sq[:, 0], og[:], ACT.Square).then_inc(sq_ready, 1)
                act.wait_ge(os_loaded, 16 * t + 16)
                nc.scalar.activation(sq[:, 1], os_[:], ACT.Square).then_inc(sq_ready, 1)
                act.wait_ge(min_ready, t + 1)
                nc.scalar.activation(sil[:], sil[:], ACT.Exp).then_inc(sil_step, 1)
                act.wait_ge(sil_step, 2 * t + 1)
                nc.scalar.activation(sil[:], sil[:], ACT.Ln, bias=1.0).then_inc(sil_step, 1)
                act.wait_ge(sil_step, 2 * t + 2)
                nc.scalar.activation(sil[:], sil[:], ACT.Exp, scale=-1.0).then_inc(ex_ready, 1)
                act.wait_ge(ss_ready, 2 * t + 2)
                act.wait_ge(cat_ready, 3 * t)
                nc.scalar.activation(ln[:, 0:GH], ss[:, 0:GH], ACT.Ln, bias=eps[:], scale=1.0 / GDV).then_inc(ln_step, 1)
                nc.scalar.activation(ln[:, GH:], ss[:, GH:], ACT.Ln, bias=eps[:], scale=1.0 / SD).then_inc(ln_step, 1)
                act.wait_ge(ln_step, 2 * t + 2)
                nc.scalar.activation(rs[:], ln[:], ACT.Exp, scale=-0.5).then_inc(rs_ready, 1)

            def cat_out(t):
                act.wait_ge(cT_done, t + 1)
                nc.scalar.copy(catT[:, 0:4, :], ps_t[0][:].rearrange("p (k t) -> p k t", k=4)).then_inc(cT_act, 1)

            def norm(t):
                act.wait_ge(h_ready, 2 * t + 2)
                nc.scalar.activation(hsq[:], h[:], ACT.Square, accum_out=hs[:, 0:1]).then_inc(hss_step, 1)
                act.wait_ge(hss_step, 2 * t + 1)
                nc.scalar.activation(hs[:, 1:2], hs[:, 0:1], ACT.Ln, bias=eps[:], scale=1.0 / D_MODEL).then_inc(hss_step, 1)
                act.wait_ge(hss_step, 2 * t + 2)
                act.wait_ge(hn_ready, t)
                nc.scalar.activation(hs[:, 2:3], hs[:, 1:2], ACT.Exp, scale=-0.5).then_inc(hrs_ready, 1)

            def norm_out(t):
                act.wait_ge(nT_done, t + 1)
                nc.scalar.copy(hnT[:, 0:4, :], ps_n[0][:].rearrange("p (k t) -> p k t", k=4)).then_inc(nT_act, 1)

            def rows_out(t, rows):
                act.wait_ge(h_ready, 2 * t + 2)
                act.dma_start(d["s_h"][rows, :], h[:]).then_inc(st_h, 16)
                act.wait_ge(hn_ready, t + 1)
                act.dma_start(d["s_xn"][rows, :], hn[:]).then_inc(st_n, 16)

            heads(0)
            act.wait_ge(small, SMALL)
            for k in range(KD):
                act.wait_ge(w_loaded[k], 16)
                n = 0 if k < V_W // P else 1
                nc.scalar.activation(w_out[:, k, :], w_out[:, k, :], ACT.Copy, scale=gains[:, n:n + 1]
                                     ).then_inc(w_scaled, 1)
            cat_out(0)
            heads(1)
            norm(0)
            rows_out(0, slice(0, P))
            cat_out(1)
            with act.Fori(1, LAST) as t:
                rows = bass.ds(act.snap(t * P), P)
                norm_out(t - 1)
                heads(t + 1)
                norm(t)
                cat_out(t + 1)
                rows_out(t, rows)
            norm_out(LAST - 1)
            norm(LAST)
            rows_out(LAST, slice(LAST * P, ROWS))
            norm_out(LAST)
            act.wait_ge(route_done, TILES)
            nc.scalar.activation(eg[:], all_g[:], ACT.Exp).then_inc(soft_ready, 1)
            nc.scalar.activation(em[:], all_m[:], ACT.Exp).then_inc(soft_ready, 1)
            act.wait_ge(place_step, PLACE_STEPS)
            act.dma_start(d["s_dest"], dest_u[:].rearrange("p k t -> p (k t)")).then_inc(stored, 16)
            act.dma_start(d["s_gate"], gates[:].rearrange("p k t -> p (k t)")).then_inc(stored, 16)
            act.dma_start(d["s_block_e"], block_i[:]).then_inc(stored, 16)
            act.wait_ge(stored, 48)
            act.wait_ge(st_h, 16 * TILES)
            act.wait_ge(st_n, 16 * TILES)

        @block.vector
        def _(dve):
            nc.vector.memset(x[:], 0.0).then_inc(x0_zero, 1)
            nc.vector.memset(eps[:], EPS).then_inc(x0_zero, 1)
            nc.vector.memset(g8[:], -3e38).then_inc(x0_zero, 1)
            nc.vector.memset(total[:], 0.0).then_inc(x0_zero, 1)
            dve.wait_ge(x0_zero, 4)
            dve.wait_ge(small, SMALL)
            dve.wait_ge(consts, CONSTS)

            def heads(t):
                dve.wait_ge(gr_loaded, 16 * t + 16)
                dve.wait_ge(cat_ready, 3 * t)
                nc.vector.tensor_scalar(sil[:], gr[:], -1.0, 80.0, ALU.mult, ALU.min).then_inc(min_ready, 1)
                dve.wait_ge(rs_ready, t)
                dve.wait_ge(sq_ready, 2 * t + 1)
                nc.vector.tensor_reduce(ss[:, 0:GH], sq[:, 0].rearrange("p (h e) -> p h e", h=GH), AX.X, ALU.add
                                        ).then_inc(ss_ready, 1)
                dve.wait_ge(sq_ready, 2 * t + 2)
                nc.vector.tensor_reduce(ss[:, GH:], sq[:, 1].rearrange("p (h e) -> p h e", h=SH), AX.X, ALU.add
                                        ).then_inc(ss_ready, 1)
                c = Chain(dve, cat_step, 1, t)
                dve.wait_ge(rs_ready, t + 1)
                dve.wait_ge(cT_done, t)
                a = cat[:, 0:V_W].rearrange("p (h e) -> p h e", h=GH)
                b = cat[:, V_W:].rearrange("p (h e) -> p h e", h=SH)
                c(nc.vector.tensor_tensor(a, og[:].rearrange("p (h e) -> p h e", h=GH),
                                          rs[:, 0:GH].unsqueeze(2).to_broadcast([P, GH, GDV]), ALU.mult))
                c.done()
                nc.vector.tensor_tensor(b, os_[:].rearrange("p (h e) -> p h e", h=SH),
                                        rs[:, GH:].unsqueeze(2).to_broadcast([P, SH, SD]), ALU.mult
                                        ).then_inc(cat_ready, 1)
                dve.wait_ge(ex_ready, t + 1)
                nc.vector.tensor_tensor(sil[:], gr[:], sil[:], ALU.mult).then_inc(sil_ready, 1)
                dve.wait_ge(sil_ready, t + 1)
                nc.vector.tensor_tensor(cat[:, 0:V_W], cat[:, 0:V_W], sil[:], ALU.mult).then_inc(cat_ready, 2)

            def cat_out(t):
                dve.wait_ge(cT_done, t + 1)
                nc.vector.tensor_copy(catT[:, 4:8, :], ps_t[1][:].rearrange("p (k t) -> p k t", k=4)).then_inc(cT_dve, 1)

            def residual(t):
                dve.wait_ge(x_loaded, 16 * t + 32)
                dve.wait_ge(o_done, t + 1)
                dve.wait_ge(st_h, 16 * t)
                dve.wait_ge(hn_ready, t)
                for n in range(2):
                    cols = slice(n * 512, (n + 1) * 512)
                    nc.vector.tensor_tensor(h[:, cols], ps_h[n][:], x[:, cols], ALU.add).then_inc(h_ready, 1)

            def norm(t):
                dve.wait_ge(hrs_ready, t + 1)
                dve.wait_ge(nT_done, t)
                dve.wait_ge(st_n, 16 * t)
                nc.vector.scalar_tensor_tensor(hn[:], h[:], hs[:, 2:3], f_gain[:], ALU.mult, ALU.mult
                                               ).then_inc(hn_ready, 1)

            def norm_out(t):
                dve.wait_ge(nT_done, t + 1)
                nc.vector.tensor_copy(hnT[:, 4:8, :], ps_n[1][:].rearrange("p (k t) -> p k t", k=4)).then_inc(nT_dve, 1)

            def route(t, at):
                c = Chain(dve, dve_step, ROUTE, t)
                dve.wait_ge(r_done, t + 1)
                c(nc.vector.tensor_tensor(g8[:, 0:N_GROUPS], ps_r[:, 0:N_GROUPS], b_r[:, 0:N_GROUPS], ALU.add))
                c(nc.vector.tensor_tensor(le[:].rearrange("p g e -> p (g e)"), ps_r[:, N_GROUPS:NR], b_r[:, N_GROUPS:],
                                          ALU.add), wait=False)
                c(nc.vector.max(gm8[:], g8[:]))
                c(nc.vector.tensor_scalar(all_g[:, at, :].rearrange("p a g -> p (a g)"), g8[:, 0:N_GROUPS], gm8[:, 0:1],
                                          None, ALU.subtract), wait=False)
                c(nc.vector.max_index(gi8[:], gm8[:], g8[:]))
                c(nc.vector.tensor_scalar(gf[:], gi8[:, 0:1].to_broadcast([P, 2]), 1.0, None, ALU.mult))
                c(nc.vector.tensor_scalar(own[:], iota_e[:, 0:N_GROUPS], gf[:, 0:1], None, ALU.is_equal))
                c(nc.vector.tensor_tensor(tmp8[:], le[:].rearrange("p g e -> p e g"),
                                          own[:].unsqueeze(1).to_broadcast([P, PER_GROUP, N_GROUPS]), ALU.mult))
                c(nc.vector.tensor_reduce(l8[:], tmp8[:], AX.X, ALU.add))
                c(nc.vector.tensor_scalar(gf[:], gf[:], float(PER_GROUP), None, ALU.mult), wait=False)
                c(nc.vector.max(m8[:], l8[:]))
                c(nc.vector.tensor_scalar(all_m[:, at, :].rearrange("p a k -> p (a k)"), m8[:, 0:2], m8[:, 0:1], None,
                                          ALU.subtract), wait=False)
                c(nc.vector.max_index(i8[:], m8[:], l8[:]))
                c(nc.vector.tensor_copy(ef[:], i8[:, 0:2]))
                c(nc.vector.tensor_tensor(e2[:], gf[:], ef[:], ALU.add))
                c.done()
                dve.wait_ge(p_done, t)
                for k in range(2):
                    nc.vector.tensor_scalar(E[:, k, :], iota_e[:], e2[:, k:k + 1], valid[:, at], ALU.is_equal, ALU.mult
                                            ).then_inc(E_ready, 1)
                dve.wait_ge(E_ready, 4 * t + 2)
                for k in range(2):
                    nc.vector.tensor_scalar(all_E[:, k, at, :].rearrange("p a e -> p (a e)"), E[:, k, :], 1.0, None,
                                            ALU.mult).then_inc(E_ready, 1)

            def counted(t, at):
                dve.wait_ge(p_done, t + 1)
                nc.vector.tensor_scalar(all_pos[:, at, :].rearrange("p a e -> p (a e)"), ps_p[:, 0:N_EXP], 1.0, None,
                                        ALU.mult).then_inc(pos_ready, 1)
                nc.vector.tensor_tensor(total[:], total[:], E[:, 0, :], ALU.add).then_inc(total_step, 1)
                dve.wait_ge(total_step, t + 1)
                nc.vector.tensor_tensor(total[:], total[:], E[:, 1, :], ALU.add).then_inc(route_done, 1)
                dve.wait_ge(route_done, t + 1)

            heads(0)
            cat_out(0)
            heads(1)
            residual(0)
            norm(0)
            cat_out(1)

            def turn(t, at):
                norm_out(t - 1)
                if not (isinstance(t, int) and t == LAST):
                    heads(t + 1)
                residual(t)
                if not (isinstance(t, int) and t == LAST):
                    cat_out(t + 1)
                norm(t)
                if not (isinstance(t, int) and t == 1):
                    counted(t - 2, at(t - 2))
                route(t - 1, at(t - 1))

            fixed = lambda t: slice(t, t + 1)
            turn(1, fixed)
            with dve.Fori(2, LAST) as t:
                turn(t, lambda t: bass.ds(dve.snap(t), 1))
            turn(LAST, fixed)
            norm_out(LAST)
            counted(LAST - 1, fixed(LAST - 1))
            route(LAST, fixed(LAST))
            counted(LAST, fixed(LAST))

            c = Chain(dve, place_step)
            dve.wait_ge(pos_ready, TILES)
            dve.wait_ge(E_ready, 4 * TILES)
            dve.wait_ge(soft_ready, 2)
            c(nc.vector.tensor_reduce(gsum[:], eg[:], AX.X, ALU.add), wait=False)
            c(nc.vector.tensor_reduce(msum[:], em[:], AX.X, ALU.add))
            c(nc.vector.tensor_tensor(prod[:], gsum[:], msum[:], ALU.mult))
            c(nc.vector.reciprocal(gate[:], prod[:]))
            for k in range(2):
                c(nc.vector.tensor_tensor(gates[:, k, :], em[:, :, k], gate[:], ALU.mult), wait=False)
            dve.wait_ge(c_done, 1)
            c(nc.vector.tensor_scalar(cnt_i[:], ps_r[:, 0:N_EXP], float(P - 1), None, ALU.add))
            c(nc.vector.tensor_scalar(blk_i[:], cnt_i[:], 7, None, ALU.logical_shift_right))
            c(nc.vector.tensor_copy(blk[:], blk_i[:]))
            c(nc.vector.tensor_tensor_scan(ends[:], one_row[:], blk[:], 0.0, ALU.mult, ALU.add))
            c(nc.vector.tensor_tensor(start[:], ends[:], blk[:], ALU.subtract))
            c(nc.vector.tensor_scalar(start[:], start[:], float(P), None, ALU.mult))
            c(nc.vector.tensor_tensor(all_pos[:], all_pos[:], start[:].unsqueeze(1).to_broadcast([P, TILES, N_EXP]),
                                      ALU.add))
            for k in range(2):
                c(nc.vector.tensor_tensor(picked[:], all_pos[:], all_E[:, k], ALU.mult))
                c(nc.vector.tensor_reduce(dest[:, k], picked[:], AX.X, ALU.add))
            c(nc.vector.tensor_copy(dest_u[:], dest[:]))
            c(nc.vector.tensor_scalar(skip[:], valid[:], -1e6, 1e6, ALU.mult, ALU.add))
            c(nc.vector.tensor_scalar(lane[:], dest_u[:], P - 1, None, ALU.bitwise_and), wait=False)
            c(nc.vector.tensor_scalar(blk_of[:], dest_u[:], 7, None, ALU.logical_shift_right))
            c(nc.vector.scalar_tensor_tensor(to[:], lane[:], float(BLOCKS + 1), blk_of[:], ALU.mult, ALU.add))
            for k in range(2):
                c(nc.vector.tensor_tensor(to[:, k], to[:, k], skip[:], ALU.add))
            nc.vector.tensor_copy(to_u[:], to[:]).then_inc(to_ready, 1)
            c(nc.vector.tensor_tensor(le_b[:], number[:], ends[0:1, :].unsqueeze(1).to_broadcast([1, BLOCKS, N_EXP]),
                                      ALU.is_ge))
            c(nc.vector.tensor_reduce(block_e[:], le_b[:], AX.X, ALU.add))
            c(nc.vector.tensor_scalar(block_e[:], block_e[:], float(N_EXP - 1), None, ALU.min))
            c(nc.vector.tensor_copy(block_i[:, 0:BLOCKS], block_e[:]))
            c(nc.vector.tensor_scalar(turns_i[:], ends[0:1, N_EXP - 1:N_EXP], 1.0, None, ALU.add))
            c(nc.vector.tensor_scalar(block_i[:, BLOCKS:], turns_i[:], 1, None, ALU.logical_shift_right))
            assert c.n == PLACE_STEPS, c.n

        @block.tensor
        def _(pe):
            def cat_T(t):
                pe.wait_ge(cat_ready, 3 * t + 3)
                for k in range(KD):
                    last = nc.tensor.transpose(ps_t[k // 4][:, k % 4 * P:(k % 4 + 1) * P], cat[:, k * P:(k + 1) * P],
                                               ident[:])
                last.then_inc(cT_done, 1)

            def project(t):
                pe.wait_ge(cT_act, t + 1)
                pe.wait_ge(cT_dve, t + 1)
                pe.wait_ge(h_ready, 2 * t)
                for n in range(2):
                    for k in range(KD):
                        last = nc.tensor.matmul(ps_h[n][:], catT[:, k, :], w_out[:, k, n * 512:(n + 1) * 512],
                                                start=k == 0, stop=k == KD - 1)
                last.then_inc(o_done, 1)

            def norm_T(t):
                pe.wait_ge(hn_ready, t + 1)
                for k in range(KD):
                    last = nc.tensor.transpose(ps_n[k // 4][:, k % 4 * P:(k % 4 + 1) * P], hn[:, k * P:(k + 1) * P],
                                               ident[:])
                last.then_inc(nT_done, 1)

            def router(t):
                pe.wait_ge(nT_act, t + 1)
                pe.wait_ge(nT_dve, t + 1)
                for k in range(KD):
                    last = nc.tensor.matmul(ps_r[:, 0:NR], hnT[:, k, :], w_r[:, k, :], start=k == 0, stop=k == KD - 1)
                last.then_inc(r_done, 1)

            def count(t):
                pe.wait_ge(E_ready, 4 * t + 2)
                pe.wait_ge(route_done, t)
                for k in range(2):
                    nc.tensor.matmul(ps_p[:, 0:N_EXP], before[:], E[:, k, :], start=k == 0, stop=False)
                nc.tensor.matmul(ps_p[:, 0:N_EXP], ones[:], total[:], start=False, stop=True).then_inc(p_done, 1)

            pe.wait_ge(consts, CONSTS)
            pe.wait_ge(small, SMALL)
            cat_T(0)
            pe.wait_ge(w_scaled, KD)
            project(0)
            cat_T(1)
            norm_T(0)
            project(1)
            cat_T(2)
            router(0)
            with pe.Fori(2, LAST) as t:
                norm_T(t - 1)
                project(t)
                cat_T(t + 1)
                count(t - 2)
                router(t - 1)
            norm_T(LAST - 1)
            project(LAST)
            count(LAST - 2)
            router(LAST - 1)
            norm_T(LAST)
            count(LAST - 1)
            router(LAST)
            count(LAST)
            pe.wait_ge(route_done, TILES)
            nc.tensor.matmul(ps_r[:, 0:N_EXP], ones[:], total[:], start=True, stop=True).then_inc(c_done, 1)


def phase_experts(nc, d):
    TURNS = BLOCKS // 2
    KE = D_EXP // P
    with Scope(nc, "ex") as s:
        ident = s.sb("ident", [P, P])
        expert = s.sb("expert", [1, BLOCKS + 1], I32)
        w_gate = [s.sb(f"w_gate{u}", [P, KD, D_EXP]) for u in range(2)]
        w_up = [s.sb(f"w_up{u}", [P, KD, D_EXP]) for u in range(2)]
        w_down = [s.sb(f"w_down{u}", [P, KE, D_MODEL]) for u in range(2)]
        row_of = s.sb("row_of", [P, BLOCKS + 1], I32)
        x = [s.sb(f"x{u}", [P, D_MODEL]) for u in range(2)]
        xT = s.sb("xT", [P, KD, P])
        sil = s.sb("sil", [P, D_EXP])
        hid = s.sb("hid", [P, D_EXP])
        hidT = s.sb("hidT", [P, KE, P])
        y = [s.sb(f"y{u}", [P, D_MODEL]) for u in range(2)]
        ps_x = [s.ps("ps_x0", [P, 512]), s.ps("ps_x1", [P, 512])]
        ps_g, ps_u, ps_h = s.ps("g", [P, 512]), s.ps("u", [P, 512]), s.ps("h", [P, 512])
        ps_y = [s.ps("ps_y0", [P, 512]), s.ps("ps_y1", [P, 512])]
        (ident_done, expert_loaded, xT_done, xT_act, xT_dve, g_done, u_done, sil_ready, hid_ready, hT_done, hT_ready,
         y_done, y_act, y_dve) = (s.sem(n) for n in (
             "ident_done", "expert_loaded", "xT_done", "xT_act", "xT_dve", "g_done", "u_done", "sil_ready",
             "hid_ready", "hT_done", "hT_ready", "y_done", "y_act", "y_dve"))
        zeros = s.sb("zeros", [P, 2, D_MODEL])
        rows_known, zeros_ready, zeros_stored = (s.sem(n) for n in ("rows_known", "zeros_ready", "zeros_stored"))
        gate_loaded, up_loaded, down_loaded, x_loaded, st_y = (
            [s.sem(f"{n}{u}") for u in range(2)] for n in ("gate_loaded", "up_loaded", "down_loaded", "x_loaded", "st_y"))
        block = s.block()

        def turns(eng):
            eng.wait_ge(expert_loaded, 16)
            return eng.value_load(expert[0:1, BLOCKS:], min_val=1, max_val=TURNS)

        @block.sync
        def _(sp):
            sp.dma_start(expert[:], d["s_block_e"]).then_inc(expert_loaded, 16)
            used = turns(sp)

            def load(i, u, first):
                b = 2 * i + u
                where = expert[0:1, u:u + 1] if first else expert[0:1, bass.ds(sp.snap(b), 1)]
                e = nc.values_load_multi_w_load_instructions(where, engines=[mybir.EngineType.SP], min_val=0,
                                                             max_val=N_EXP - 1)[1][0]
                if not first:
                    sp.wait_ge(u_done, b - 1)
                sp.dma_start(w_gate[u][:], d["w_gate"][0, bass.ds(e, 1)].rearrange("o (p k) n -> p (o k) n", k=KD)
                             ).then_inc(gate_loaded[u], 16)
                sp.dma_start(w_up[u][:], d["w_up"][0, bass.ds(e, 1)].rearrange("o (p k) n -> p (o k) n", k=KD)
                             ).then_inc(up_loaded[u], 16)
                if not first:
                    sp.wait_ge(y_done, b - 1)
                sp.dma_start(w_down[u][:], d["w_down"][0, bass.ds(e, 1)].rearrange("o (p k) n -> p (o k) n", k=KE)
                             ).then_inc(down_loaded[u], 16)

            load(0, 0, True)
            load(0, 1, True)
            with sp.Fori(1, TURNS) as i:
                with sp.If(i < used):
                    load(i, 0, False)
                    load(i, 1, False)
            sp.wait_ge(zeros_ready, 1)
            with sp.Fori(1, TURNS) as i:
                with sp.If(i < used):
                    sp.sem_inc(zeros_stored, 16)
                with sp.If(used <= i):
                    sp.dma_start(d["s_y"][bass.ds(sp.snap(i * (2 * P)), 2 * P), :].rearrange("(a p) n -> p a n", p=P),
                                 zeros[:]).then_inc(zeros_stored, 16)
            sp.wait_ge(zeros_stored, 16 * (TURNS - 1))

        @block.gpsimd
        def _(pool):
            make_identity(nc, pool, ident, ident_done)

            pool.dma_start(row_of[:], d["s_rowtok"].rearrange("(p b) o -> p (b o)", p=P)).then_inc(rows_known, 16)
            pool.wait_ge(rows_known, 16)
            def gather(b):
                pool.indirect_dma_start(out=x[b % 2][:], out_offset=None, in_=d["s_xn"],
                                        in_offset=bass.IndirectOffsetOnAxis(ap=row_of[:, b:b + 1], axis=0)
                                        ).then_inc(x_loaded[b % 2], 16)

            used = turns(pool)
            gather(0)
            gather(1)
            pool.wait_ge(xT_done, 1)
            gather(2)
            for i in range(1, TURNS):
                with pool.If(used > i):
                    pool.wait_ge(xT_done, 2 * i)
                    gather(2 * i + 1)
                    pool.wait_ge(xT_done, 2 * i + 1)
                    gather(2 * i + 2)
            for u in range(2):
                pool.wait_ge(st_y[u], used * 16)

        @block.scalar
        def _(act):
            def x_out(b):
                act.wait_ge(xT_done, b + 1)
                act.wait_ge(u_done, b)
                nc.scalar.copy(xT[:, 0:4, :], ps_x[0][:].rearrange("p (k t) -> p k t", k=4)).then_inc(xT_act, 1)

            def run(i, u, rows):
                b = 2 * i + u
                act.wait_ge(g_done, b + 1)
                act.wait_ge(hid_ready, b)
                nc.scalar.activation(sil[:], ps_g[:], ACT.Silu).then_inc(sil_ready, 1)
                x_out(b + 1)
                act.wait_ge(y_done, b + 1)
                act.wait_ge(st_y[u], 16 * i)
                nc.scalar.copy(y[u][:, 0:512], ps_y[0][:]).then_inc(y_act, 1)
                act.wait_ge(y_act, b + 1)
                act.wait_ge(y_dve, b + 1)
                act.dma_start(d["s_y"][rows, :], y[u][:]).then_inc(st_y[u], 16)

            used = turns(act)
            x_out(0)
            with act.Fori(0, TURNS) as i:
                with act.If(i < used):
                    for u in range(2):
                        run(i, u, bass.ds(act.snap(i * (2 * P) + u * P), P))

        @block.vector
        def _(dve):
            def x_out(b):
                dve.wait_ge(xT_done, b + 1)
                dve.wait_ge(u_done, b)
                nc.vector.tensor_copy(xT[:, 4:8, :], ps_x[1][:].rearrange("p (k t) -> p k t", k=4)).then_inc(xT_dve, 1)

            def run(i, u):
                b = 2 * i + u
                dve.wait_ge(u_done, b + 1)
                dve.wait_ge(sil_ready, b + 1)
                dve.wait_ge(hT_done, b)
                nc.vector.tensor_tensor(hid[:], ps_u[:], sil[:], ALU.mult).then_inc(hid_ready, 1)
                x_out(b + 1)
                dve.wait_ge(hT_done, b + 1)
                dve.wait_ge(y_done, b)
                nc.vector.tensor_copy(hidT[:], ps_h[:].rearrange("p (k t) -> p k t", k=KE)).then_inc(hT_ready, 1)
                dve.wait_ge(y_done, b + 1)
                dve.wait_ge(st_y[u], 16 * i)
                nc.vector.tensor_copy(y[u][:, 512:], ps_y[1][:]).then_inc(y_dve, 1)

            nc.vector.memset(zeros[:], 0.0).then_inc(zeros_ready, 1)
            used = turns(dve)
            x_out(0)
            with dve.Fori(0, TURNS) as i:
                with dve.If(i < used):
                    for u in range(2):
                        run(i, u)

        @block.tensor
        def _(pe):
            def x_T(i, u):
                b = 2 * i + u
                pe.wait_ge(x_loaded[u], 16 * i + 16)
                pe.wait_ge(xT_act, b)
                pe.wait_ge(xT_dve, b)
                for k in range(KD):
                    last = nc.tensor.transpose(ps_x[k // 4][:, k % 4 * P:(k % 4 + 1) * P],
                                               x[u][:].rearrange("p (c k) -> p k c", k=KD)[:, k, :], ident[:])
                last.then_inc(xT_done, 1)

            def run(i, u):
                b = 2 * i + u
                pe.wait_ge(xT_act, b + 1)
                pe.wait_ge(xT_dve, b + 1)
                pe.wait_ge(gate_loaded[u], 16 * i + 16)
                pe.wait_ge(hid_ready, b)
                for k in range(KD):
                    last = nc.tensor.matmul(ps_g[:], xT[:, k, :], w_gate[u][:, k, :], start=k == 0, stop=k == KD - 1)
                last.then_inc(g_done, 1)
                pe.wait_ge(up_loaded[u], 16 * i + 16)
                for k in range(KD):
                    last = nc.tensor.matmul(ps_u[:], xT[:, k, :], w_up[u][:, k, :], start=k == 0, stop=k == KD - 1)
                last.then_inc(u_done, 1)
                x_T(i + u, 1 - u)
                pe.wait_ge(hid_ready, b + 1)
                pe.wait_ge(hT_ready, b)
                for k in range(KE):
                    last = nc.tensor.transpose(ps_h[:, k * P:(k + 1) * P],
                                               hid[:].rearrange("p (c k) -> p k c", k=KE)[:, k, :], ident[:])
                last.then_inc(hT_done, 1)
                pe.wait_ge(hT_ready, b + 1)
                pe.wait_ge(down_loaded[u], 16 * i + 16)
                pe.wait_ge(y_act, b)
                pe.wait_ge(y_dve, b)
                for n in range(2):
                    for k in range(KE):
                        last = nc.tensor.matmul(ps_y[n][:], hidT[:, k, :], w_down[u][:, k, n * 512:(n + 1) * 512],
                                                start=k == 0, stop=k == KE - 1)
                last.then_inc(y_done, 1)

            used = turns(pe)
            pe.wait_ge(ident_done, 2)
            x_T(0, 0)
            with pe.Fori(0, TURNS) as i:
                with pe.If(i < used):
                    for u in range(2):
                        run(i, u)


def phase_combine(nc, d):
    R = 3
    with Scope(nc, "co") as s:
        place = s.sb("place", [P, 2, TILES], I32)
        gate = s.sb("gate", [P, 2, TILES])
        h = [s.sb(f"h{r}", [P, D_MODEL]) for r in range(R)]
        e = [[s.sb(f"e{k}{r}", [P, D_MODEL]) for r in range(R)] for k in range(2)]
        tables, add_step = s.sem("tables"), s.sem("add_step")
        h_loaded, e0_loaded, e1_loaded, stored = ([s.sem(f"{n}{r}") for r in range(R)] for n in (
            "h_loaded", "e0_loaded", "e1_loaded", "stored"))
        e_loaded = [e0_loaded, e1_loaded]
        block = s.block()

        @block.sync
        def _(sp):
            sp.dma_start(place[:].rearrange("p k t -> p (k t)"), d["s_dest"]).then_inc(tables, 16)
            sp.dma_start(gate[:].rearrange("p k t -> p (k t)"), d["s_gate"]).then_inc(tables, 16)
            for t in range(TILES):
                if t >= R:
                    sp.wait_ge(stored[t % R], 16 * (t // R))
                sp.dma_start(h[t % R][:], d["s_h"][t * P:(t + 1) * P, :]).then_inc(h_loaded[t % R], 16)

        @block.gpsimd
        def _(pool):
            pool.wait_ge(tables, 32)
            for t in range(TILES):
                if t >= R:
                    pool.wait_ge(add_step, 2 * (t - R) + 2)
                for k in range(2):
                    pool.indirect_dma_start(
                        out=e[k][t % R][:], out_offset=None, in_=d["s_y"],
                        in_offset=bass.IndirectOffsetOnAxis(ap=place[:, k, t:t + 1], axis=0)
                    ).then_inc(e_loaded[k][t % R], 16)

        @block.vector
        def _(dve):
            dve.wait_ge(tables, 32)
            for t in range(TILES):
                dve.wait_ge(h_loaded[t % R], 16 * (t // R + 1))
                for k in range(2):
                    dve.wait_ge(e_loaded[k][t % R], 16 * (t // R + 1))
                    nc.vector.scalar_tensor_tensor(h[t % R][:], e[k][t % R][:], gate[:, k, t:t + 1], h[t % R][:],
                                                   ALU.mult, ALU.add).then_inc(add_step, 1)
                    dve.wait_ge(add_step, 2 * t + k + 1)

        @block.scalar
        def _(act):
            for t in range(TILES):
                act.wait_ge(add_step, 2 * t + 2)
                if t:
                    act.dma_start(d["y_prompt"][0, (t - 1) * P:t * P, :], h[t % R][:]).then_inc(stored[t % R], 16)
                else:
                    act.dma_start(d["y_sample"].rearrange("b t m -> (b t) m"), h[0][0:N_SAMPLE, :]
                                  ).then_inc(stored[0], 16)
            for r in range(R):
                act.wait_ge(stored[r], 16 * ((TILES - r + R - 1) // R))


def phase_cache_rows(nc, d):
    with Scope(nc, "cr") as s:
        stored = s.sem("stored")
        block = s.block()

        @block.sync
        def _(sp):
            heads = d["s_v"].rearrange("h t e -> t h e")
            sp.dma_start(d["new_k_sample"][0].rearrange("b t h e -> (b t) (h e)"), d["s_k"][0:N_SAMPLE, :]
                         ).then_inc(stored, 16)
            sp.dma_start(d["new_v_sample"][0].rearrange("b t h e -> (b t) h e"), heads[0:N_SAMPLE]).then_inc(stored, 16)
            sp.dma_start(d["new_k_prompt"][0, 0].rearrange("t h e -> t (h e)"), d["s_k"][PAD:ROWS, :]
                         ).then_inc(stored, 16)
            sp.dma_start(d["new_v_prompt"][0, 0], heads[PAD:ROWS]).then_inc(stored, 16)
            sp.wait_ge(stored, 64)


SCRATCH = {
    "s_gqk": ((ROWS, 2 * QK_W), F32),
    "s_gv": ((ROWS, V_W), F32),
    "s_gr": ((ROWS, V_W), F32),
    "s_la": ((ROWS, QK_W), F32),
    "s_k": ((ROWS, SB_W), F32),
    "s_v": ((SH, ROWS, SD), F32),
    "s_qT": ((SH, SD + 2, ROWS), F32),
    "s_kT": ((SH, SD + 2, ROWS), F32),
    "s_og": ((ROWS, V_W), F32),
    "s_os": ((SH, ROWS, SD), F32),
    "s_h": ((ROWS, D_MODEL), F32),
    "s_xn": ((ROWS, D_MODEL), F32),
    "s_rowtok": (((BLOCKS + 1) * P, 1), I32),
    "s_dest": ((P, 2 * TILES), I32),
    "s_gate": ((P, 2 * TILES), F32),
    "s_block_e": ((1, BLOCKS + 1), I32),
    "s_y": ((BLOCKS * P, D_MODEL), F32),
}

INPUTS = ["x_prompt", "x_sample", "cache_sb_k", "cache_sb_v", "state_gla", "page_table", "meta_tokens", "norm_mix_gain",
          "w_in", "gla_w_alpha", "gla_b_alpha", "gla_out_gain", "sb_q_gain", "sb_k_gain", "sb_logit_bias",
          "sb_out_gain", "w_out", "norm_ffn_gain", "router_group", "router_group_b", "router_expert",
          "router_expert_b", "w_gate", "w_up", "w_down"]
OUTPUTS = [("y_prompt", (1, SEQ, D_MODEL)), ("y_sample", (DEC_B, DEC_S, D_MODEL)),
           ("new_k_prompt", (1, 1, SEQ + N_META, SH, SD)), ("new_v_prompt", (1, 1, SEQ + N_META, SH, SD)),
           ("new_gla_prompt", (1, 1, GH, GDK, GDV)), ("new_k_sample", (1, DEC_B, DEC_S, SH, SD)),
           ("new_v_sample", (1, DEC_B, DEC_S, SH, SD)), ("new_gla_sample", (1, DEC_B, GH, GDK, GDV))]


def build(nc, d):
    phase_project(nc, d)
    phase_gla_prompt(nc, d)
    phase_gla_sample(nc, d)
    phase_attend(nc, d)
    phase_attend_sample(nc, d)
    phase_out_route(nc, d)
    phase_cache_rows(nc, d)
    phase_experts(nc, d)
    phase_combine(nc, d)


def kernel(**inputs):
    import numpy as _np
    import concourse.bacc as _bacc
    from concourse import mybir as _mybir
    from concourse.bass_utils import run_bass_kernel_spmd as _run

    nc = _bacc.Bacc("TRN2", target_bir_lowering=False, num_devices=1)
    arrays, d = {}, {}
    for name in INPUTS:
        a = _np.ascontiguousarray(inputs[name])
        arrays[f"in_{name}"] = a
        d[name] = nc.dram_tensor(f"in_{name}", a.shape, _mybir.dt.from_np(a.dtype), kind="ExternalInput").ap()
    for name, shape in OUTPUTS:
        d[name] = nc.dram_tensor(f"out_{name}", shape, F32, kind="ExternalOutput").ap()
    for name, (shape, dt) in SCRATCH.items():
        d[name] = nc.dram_tensor(name, shape, dt, kind="Internal").ap()
    build(nc, d)
    r = _run(nc, [arrays], core_ids=[0])
    return tuple(r.results[0][f"out_{name}"] for name, _ in OUTPUTS)
```
